# Optimizing a Trainium2 kernel written in Bass

```python
import math
import jax, jax.numpy as jnp
from jax import lax
import numpy as np

D_MODEL = 1024
BATCH = 1
SEQ = 512
DEPTH = 1

NSA_HEADS = 8
NSA_KV_HEADS = 2
NSA_GROUP = NSA_HEADS // NSA_KV_HEADS
HEAD_DIM = 64
CMP_BLOCK = 32
CMP_STRIDE = 16
CMP_HIDDEN = 256
SEL_BLOCK = 64
SEL_TOPK = 8
WINDOW = 256
WIN_QBLOCK = 128
FORCE_SCORE = 1.0e4
RET_HEADS = 4
RET_QK_DIM = 64
RET_V_DIM = 128
RET_CHUNK = 128
D_FF = 4 * D_MODEL
ROPE_THETA = 10000.0
EPS = 1e-6
NEG_INF = -1.0e30

NSA_Q_DIM = NSA_HEADS * HEAD_DIM
NSA_KV_DIM = NSA_KV_HEADS * HEAD_DIM
NSA_GATE_DIM = 3 * NSA_HEADS
RET_QK_WIDTH = RET_HEADS * RET_QK_DIM
RET_V_WIDTH = RET_HEADS * RET_V_DIM
MIX_WIDTH = NSA_Q_DIM + RET_V_WIDTH
IN_SIZES = [NSA_Q_DIM, NSA_KV_DIM, NSA_KV_DIM, NSA_KV_DIM, NSA_KV_DIM, NSA_KV_DIM, NSA_KV_DIM,
            NSA_GATE_DIM, RET_QK_WIDTH, RET_QK_WIDTH, RET_V_WIDTH, RET_V_WIDTH]
IN_WIDTH = sum(IN_SIZES)


def rms_norm(x, w):
    xf = x.astype(jnp.float32)
    y = xf * lax.rsqrt(jnp.mean(xf * xf, axis=-1, keepdims=True) + EPS)
    return (y * w.astype(jnp.float32)).astype(x.dtype)

def rope(x, pos):
    half = x.shape[-1] // 2
    inv = ROPE_THETA ** (-jnp.arange(half, dtype=jnp.float32) / half)
    ang = pos.astype(jnp.float32)[:, None] * inv[None, :]
    cos, sin = jnp.cos(ang), jnp.sin(ang)
    xf = x.astype(jnp.float32)
    x1, x2 = xf[..., :half], xf[..., half:]
    return jnp.concatenate([x1 * cos - x2 * sin, x2 * cos + x1 * sin], axis=-1).astype(x.dtype)

def masked_softmax(s, mask):
    s = jnp.where(mask, s.astype(jnp.float32), NEG_INF)
    p = jax.nn.softmax(s, axis=-1)
    return jnp.where(mask, p, 0.0)

def compress(blocks, w1, w2):
    b, g, n, l, d = blocks.shape
    return jax.nn.silu(blocks.reshape(b, g, n, l * d) @ w1) @ w2

def nsa_mixer(q, kc, vc, ks, vs, kw, vw, gates, q_norm_w, k_norm_w,
              cmp_pe_k, cmp_pe_v, cmp_wk1, cmp_wk2, cmp_wv1, cmp_wv2):
    B, S, _ = q.shape
    G, R, dh = NSA_KV_HEADS, NSA_GROUP, HEAD_DIM
    pos = jnp.arange(S)
    scale = dh ** -0.5
    q = q.reshape(B, S, G, R, dh).transpose(0, 2, 3, 1, 4)
    q = rope(rms_norm(q, q_norm_w), pos)

    def prep_k(k, w):
        k = k.reshape(B, S, G, dh).transpose(0, 2, 1, 3)
        return rope(rms_norm(k, w), pos)

    def prep_v(v):
        return v.reshape(B, S, G, dh).transpose(0, 2, 1, 3)

    kc, ks, kw = prep_k(kc, k_norm_w[0]), prep_k(ks, k_norm_w[1]), prep_k(kw, k_norm_w[2])
    vc, vs, vw = prep_v(vc), prep_v(vs), prep_v(vw)

    n_cmp = (S - CMP_BLOCK) // CMP_STRIDE + 1
    c_start = jnp.arange(n_cmp) * CMP_STRIDE
    cidx = c_start[:, None] + jnp.arange(CMP_BLOCK)[None, :]
    k_cmp = compress(kc[:, :, cidx] + cmp_pe_k, cmp_wk1, cmp_wk2)
    v_cmp = compress(vc[:, :, cidx] + cmp_pe_v, cmp_wv1, cmp_wv2)
    s_cmp = jnp.einsum('bgrqd,bgcd->bgrqc', q, k_cmp) * scale
    cmask = (c_start + CMP_BLOCK - 1)[None, :] <= pos[:, None]
    p_cmp = masked_softmax(s_cmp, cmask)
    o_cmp = jnp.einsum('bgrqc,bgcd->bgrqd', p_cmp.astype(v_cmp.dtype), v_cmp)

    n_blk = S // SEL_BLOCK
    jb = jnp.arange(n_blk)
    overlap = ((c_start[:, None] < (jb[None, :] + 1) * SEL_BLOCK)
               & (c_start[:, None] + CMP_BLOCK > jb[None, :] * SEL_BLOCK)).astype(jnp.float32)
    p_slc = jnp.einsum('bgrqc,cj->bgqj', p_cmp, overlap)
    cur = pos // SEL_BLOCK
    forced = (jb[None, :] == 0) | (jb[None, :] == cur[:, None]) | (jb[None, :] == cur[:, None] - 1)
    valid = jb[None, :] <= cur[:, None]
    score = jnp.where(forced, FORCE_SCORE, jnp.where(valid, p_slc, -1.0))
    n_sel = min(SEL_TOPK, n_blk)
    _, sel_idx = lax.top_k(score, n_sel)

    k_blocks = ks.reshape(B, G, n_blk, SEL_BLOCK, dh)
    v_blocks = vs.reshape(B, G, n_blk, SEL_BLOCK, dh)
    nq = S // SEL_BLOCK
    q_b = jnp.moveaxis(q.reshape(B, G, R, nq, SEL_BLOCK, dh), 3, 0)
    idx_b = jnp.moveaxis(sel_idx.reshape(B, G, nq, SEL_BLOCK, n_sel), 2, 0)
    t_b = pos.reshape(nq, SEL_BLOCK)
    bi = jnp.arange(B)[:, None, None, None]
    gi = jnp.arange(G)[None, :, None, None]
    n_keys = n_sel * SEL_BLOCK

    def sel_block(args):
        qc, ic, tc = args
        ksel = k_blocks[bi, gi, ic]
        vsel = v_blocks[bi, gi, ic]
        s = jnp.einsum('bgrqd,bgqnkd->bgrqnk', qc, ksel) * scale
        kpos = ic[..., None] * SEL_BLOCK + jnp.arange(SEL_BLOCK)
        mask = (kpos <= tc[None, None, :, None, None])[:, :, None]
        p = masked_softmax(s.reshape(B, G, R, SEL_BLOCK, n_keys),
                           mask.reshape(B, G, 1, SEL_BLOCK, n_keys))
        return jnp.einsum('bgrqk,bgqkd->bgrqd', p.astype(vsel.dtype),
                          vsel.reshape(B, G, SEL_BLOCK, n_keys, dh))

    o_sel = lax.map(sel_block, (q_b, idx_b, t_b))
    o_sel = jnp.moveaxis(o_sel, 0, 3).reshape(B, G, R, S, dh)

    nw = S // WIN_QBLOCK
    n_wk = WIN_QBLOCK + WINDOW
    widx = jnp.arange(nw)[:, None] * WIN_QBLOCK + jnp.arange(n_wk)[None, :]
    pad = ((0, 0), (0, 0), (WINDOW, 0), (0, 0))
    kwin = jnp.pad(kw, pad)[:, :, widx]
    vwin = jnp.pad(vw, pad)[:, :, widx]
    kpos = widx - WINDOW
    qw = q.reshape(B, G, R, nw, WIN_QBLOCK, dh)
    s_w = jnp.einsum('bgrcqd,bgckd->bgrcqk', qw, kwin) * scale
    tq = pos.reshape(nw, WIN_QBLOCK)
    diff = tq[:, :, None] - kpos[:, None, :]
    wmask = (diff >= 0) & (diff < WINDOW) & (kpos[:, None, :] >= 0)
    p_w = masked_softmax(s_w, wmask)
    o_win = jnp.einsum('bgrcqk,bgckd->bgrcqd', p_w.astype(vwin.dtype), vwin).reshape(B, G, R, S, dh)

    g = jax.nn.sigmoid(gates.astype(jnp.float32)).reshape(B, S, 3, G, R)
    g = g.transpose(2, 0, 3, 4, 1)[..., None].astype(q.dtype)
    o = g[0] * o_cmp + g[1] * o_sel + g[2] * o_win
    return o.transpose(0, 3, 1, 2, 4).reshape(B, S, NSA_Q_DIM)

def retention_mixer(q, k, v, gate, ret_norm_w):
    B, S, _ = q.shape
    H, dk, dv, C = RET_HEADS, RET_QK_DIM, RET_V_DIM, RET_CHUNK
    out_dtype = q.dtype
    pos = jnp.arange(S)
    q = rope(q.reshape(B, S, H, dk).transpose(0, 2, 1, 3), pos).astype(jnp.float32)
    k = (rope(k.reshape(B, S, H, dk).transpose(0, 2, 1, 3), pos).astype(jnp.float32)) * (dk ** -0.5)
    v = v.reshape(B, S, H, dv).transpose(0, 2, 1, 3).astype(jnp.float32)

    log_gamma = jnp.log(1.0 - 2.0 ** (-5.0 - jnp.arange(H, dtype=jnp.float32)))
    i = jnp.arange(C)
    d_int = i[:, None] - i[None, :]
    dmat = jnp.where(d_int >= 0,
                     jnp.exp(log_gamma[:, None, None] * jnp.maximum(d_int, 0).astype(jnp.float32)), 0.0)
    xi = jnp.exp(log_gamma[:, None] * (i + 1).astype(jnp.float32))[..., None]
    zeta = jnp.exp(log_gamma[:, None] * (C - 1 - i).astype(jnp.float32))[..., None]
    gamma_c = jnp.exp(log_gamma * C)[:, None, None]

    nc = S // C
    to_chunks = lambda t: jnp.moveaxis(t.reshape(B, H, nc, C, t.shape[-1]), 2, 0)

    def step(state, inp):
        qc, kc, vc = inp
        inner = jnp.einsum('bhqd,bhkd->bhqk', qc, kc) * dmat
        y = (jnp.einsum('bhqk,bhkv->bhqv', inner, vc)
             + jnp.einsum('bhqd,bhdv->bhqv', qc, state) * xi)
        state = gamma_c * state + jnp.einsum('bhkd,bhkv->bhdv', kc * zeta, vc)
        return state, y

    state0 = jnp.zeros((B, H, dk, dv), jnp.float32)
    _, y = lax.scan(step, state0, (to_chunks(q), to_chunks(k), to_chunks(v)))
    y = jnp.moveaxis(y, 0, 2).reshape(B, H, S, dv)
    mu = jnp.mean(y, axis=-1, keepdims=True)
    var = jnp.mean(jnp.square(y - mu), axis=-1, keepdims=True)
    y = (y - mu) * lax.rsqrt(var + EPS) * ret_norm_w.astype(jnp.float32)[None, :, None, :]
    y = y.transpose(0, 2, 1, 3).reshape(B, S, RET_V_WIDTH)
    return (jax.nn.silu(gate.astype(jnp.float32)) * y).astype(out_dtype)

def first_inputs(seed: int = 0) -> dict:
    key = jax.random.key(seed)
    ks = jax.random.split(key, 16)
    nrm = lambda k, shape, s: jax.random.normal(k, shape, jnp.float32) * s
    L = DEPTH
    return {
        "x": nrm(ks[0], (BATCH, SEQ, D_MODEL), 1.0),
        "ln1_w": 1.0 + nrm(ks[1], (L, D_MODEL), 0.02),
        "w_in": nrm(ks[2], (L, D_MODEL, IN_WIDTH), D_MODEL ** -0.5),
        "q_norm_w": 1.0 + nrm(ks[3], (L, HEAD_DIM), 0.02),
        "k_norm_w": 1.0 + nrm(ks[4], (L, 3, HEAD_DIM), 0.02),
        "cmp_pe_k": nrm(ks[5], (L, CMP_BLOCK, HEAD_DIM), 0.02),
        "cmp_pe_v": nrm(ks[6], (L, CMP_BLOCK, HEAD_DIM), 0.02),
        "cmp_wk1": nrm(ks[7], (L, CMP_BLOCK * HEAD_DIM, CMP_HIDDEN), (CMP_BLOCK * HEAD_DIM) ** -0.5),
        "cmp_wk2": nrm(ks[8], (L, CMP_HIDDEN, HEAD_DIM), CMP_HIDDEN ** -0.5),
        "cmp_wv1": nrm(ks[9], (L, CMP_BLOCK * HEAD_DIM, CMP_HIDDEN), (CMP_BLOCK * HEAD_DIM) ** -0.5),
        "cmp_wv2": nrm(ks[10], (L, CMP_HIDDEN, HEAD_DIM), CMP_HIDDEN ** -0.5),
        "ret_norm_w": 1.0 + nrm(ks[11], (L, RET_HEADS, RET_V_DIM), 0.02),
        "w_out": nrm(ks[12], (L, MIX_WIDTH, D_MODEL), MIX_WIDTH ** -0.5),
        "ln2_w": 1.0 + nrm(ks[13], (L, D_MODEL), 0.02),
        "w_up": nrm(ks[14], (L, D_MODEL, D_FF), D_MODEL ** -0.5),
        "w_down": nrm(ks[15], (L, D_FF, D_MODEL), D_FF ** -0.5),
    }

def first_block(x, ln1_w, w_in, q_norm_w, k_norm_w, cmp_pe_k, cmp_pe_v, cmp_wk1, cmp_wk2,
              cmp_wv1, cmp_wv2, ret_norm_w, w_out, ln2_w, w_up, w_down):
    split_points = [int(p) for p in np.cumsum(IN_SIZES)[:-1]]
    h = x
    for l in range(DEPTH):
        xn = rms_norm(h, ln1_w[l])
        proj = xn @ w_in[l]
        (nq_, nkc, nvc, nks, nvs, nkw, nvw, ngate,
         rq, rk, rv, rg) = jnp.split(proj, split_points, axis=-1)
        o_nsa = nsa_mixer(nq_, nkc, nvc, nks, nvs, nkw, nvw, ngate, q_norm_w[l], k_norm_w[l],
                          cmp_pe_k[l], cmp_pe_v[l], cmp_wk1[l], cmp_wk2[l], cmp_wv1[l], cmp_wv2[l])
        o_ret = retention_mixer(rq, rk, rv, rg, ret_norm_w[l])
        mix = jnp.concatenate([o_nsa, o_ret], axis=-1)
        h = h + mix @ w_out[l]
        hn = rms_norm(h, ln2_w[l])
        h = h + jnp.square(jax.nn.relu(hn @ w_up[l])) @ w_down[l]
    return h


MLSTM_HEADS = 4
MLSTM_WIDTH = D_MODEL
MLSTM_VDIM = MLSTM_WIDTH // MLSTM_HEADS
MLSTM_QKDIM = MLSTM_VDIM // 2
MLSTM_CONV = 4
MLSTM_CHUNK = 64
S5_WIDTH = D_MODEL // 2
S5_GROUP = 16
S5_GROUPS = S5_WIDTH // S5_GROUP
S5_STATE = 64
S5_DT_MIN = 1e-3
S5_DT_MAX = 1e-1
FFN_HIDDEN = ((8 * D_MODEL // 3 + 127) // 128) * 128
FFN_CONV = 3
ALPHA = (2.0 * DEPTH) ** 0.25
BETA = (8.0 * DEPTH) ** -0.25
LN_EPS = 1e-5
IN_SIZES_2 = (MLSTM_WIDTH, MLSTM_WIDTH, MLSTM_HEADS, MLSTM_HEADS, S5_WIDTH, D_MODEL, D_MODEL)
IN_WIDTH_2 = sum(IN_SIZES_2)
IN_SPLITS = tuple(int(s) for s in np.cumsum(IN_SIZES_2)[:-1])
F_OFF = 2 * MLSTM_WIDTH + MLSTM_HEADS


def _standardize(x):
    xf = x.astype(jnp.float32)
    mu = jnp.mean(xf, axis=-1, keepdims=True)
    var = jnp.mean(jnp.square(xf - mu), axis=-1, keepdims=True)
    return ((xf - mu) * lax.rsqrt(var + LN_EPS)).astype(x.dtype)

def _layer_norm(x, gain, bias):
    return _standardize(x) * gain + bias

def _causal_dwconv(x, w, b):
    K = w.shape[0]
    S = x.shape[1]
    xp = jnp.pad(x, ((0, 0), (K - 1, 0), (0, 0)))
    y = b
    for j in range(K):
        y = y + w[j] * xp[:, j:j + S]
    return y

def _mlstm_chunkwise(q, k, v, i_pre, f_pre):
    Bsz, H, S, dk = q.shape
    dv = v.shape[-1]
    L = MLSTM_CHUNK
    nc = S // L
    f32 = jnp.float32
    q = q.astype(f32) * (MLSTM_QKDIM ** -0.5)
    k = k.astype(f32)
    v = v.astype(f32)
    ig = i_pre.astype(f32)
    logf = jax.nn.log_sigmoid(f_pre.astype(f32))

    def to_chunks(a):
        return jnp.moveaxis(a.reshape((Bsz, H, nc, L) + a.shape[3:]), 2, 0)

    causal = jnp.tril(jnp.ones((L, L), dtype=bool))

    def step(carry, xs):
        C, n, m = carry
        qb, kb, vb, ib, fb = xs
        b = jnp.cumsum(fb, axis=-1)
        D = b[..., :, None] - b[..., None, :] + ib[..., None, :]
        D = jnp.where(causal, D, -jnp.inf)
        inter = b + m[..., None]
        m_t = jnp.maximum(inter, jnp.max(D, axis=-1))
        wmat = jnp.exp(D - m_t[..., None])
        sc_inter = jnp.exp(inter - m_t)
        s = jnp.einsum('bhtd,bhsd->bhts', qb, kb) * wmat
        num = jnp.einsum('bhts,bhsv->bhtv', s, vb) + sc_inter[..., None] * jnp.einsum('bhtd,bhdv->bhtv', qb, C)
        den = jnp.sum(s, axis=-1) + sc_inter * jnp.einsum('bhtd,bhd->bht', qb, n)
        h = num / jnp.maximum(jnp.abs(den), jnp.exp(-m_t))[..., None]
        b_last = b[..., -1]
        g = b_last[..., None] - b + ib
        m_new = jnp.maximum(b_last + m, jnp.max(g, axis=-1))
        wk = jnp.exp(g - m_new[..., None])
        decay = jnp.exp(b_last + m - m_new)
        kw = kb * wk[..., None]
        C_new = decay[..., None, None] * C + jnp.einsum('bhsd,bhsv->bhdv', kw, vb)
        n_new = decay[..., None] * n + jnp.sum(kw, axis=2)
        return (C_new, n_new, m_new), h

    init = (jnp.zeros((Bsz, H, dk, dv), f32), jnp.zeros((Bsz, H, dk), f32), jnp.zeros((Bsz, H), f32))
    _, hc = lax.scan(step, init, (to_chunks(q), to_chunks(k), to_chunks(v), to_chunks(ig), to_chunks(logf)))
    return jnp.moveaxis(hc, 0, 2).reshape(Bsz, H, S, dv)

def _s5_ssm(u, lam_re, lam_im, log_dt, b_re, b_im, c_re, c_im, d):
    Bsz, S, W = u.shape
    f32 = jnp.float32
    uf = u.astype(f32)
    lam_re = lam_re.astype(f32)
    lam_im = lam_im.astype(f32)
    dt = jnp.exp(log_dt.astype(f32))[:, None]
    mag = jnp.exp(lam_re * dt)
    ar = mag * jnp.cos(lam_im * dt)
    ai = mag * jnp.sin(lam_im * dt)
    den = lam_re * lam_re + lam_im * lam_im
    zr = ((ar - 1.0) * lam_re + ai * lam_im) / den
    zi = (ai * lam_re - (ar - 1.0) * lam_im) / den
    bbr = zr[..., None] * b_re - zi[..., None] * b_im
    bbi = zr[..., None] * b_im + zi[..., None] * b_re
    ug = uf.reshape(Bsz, S, S5_GROUPS, S5_GROUP)
    bu_r = jnp.einsum('bsgc,gpc->bsgp', ug, bbr)
    bu_i = jnp.einsum('bsgc,gpc->bsgp', ug, bbi)
    a_r = jnp.broadcast_to(ar, bu_r.shape)
    a_i = jnp.broadcast_to(ai, bu_r.shape)

    def combine(e1, e2):
        a1r, a1i, b1r, b1i = e1
        a2r, a2i, b2r, b2i = e2
        return (a1r * a2r - a1i * a2i,
                a1r * a2i + a1i * a2r,
                a2r * b1r - a2i * b1i + b2r,
                a2r * b1i + a2i * b1r + b2i)

    _, _, xr, xi = lax.associative_scan(combine, (a_r, a_i, bu_r, bu_i), axis=1)
    y = jnp.einsum('gcp,bsgp->bsgc', c_re, xr) - jnp.einsum('gcp,bsgp->bsgc', c_im, xi)
    y = y.reshape(Bsz, S, W) + d * uf
    return y.astype(u.dtype)

def _hybrid_mixer(h, w_in, b_in, w_mlstm_conv, b_mlstm_conv, w_mlstm_q, w_mlstm_k, mlstm_norm_gain,
                  w_mlstm_down, s5_lam_re, s5_lam_im, s5_log_dt, s5_b_re, s5_b_im, s5_c_re, s5_c_im,
                  s5_d, w_s5_glu, w_mix_out):
    Bsz, S, _ = h.shape
    proj = h @ w_in + b_in
    xm, om, ip, fp, us, ga, gb = jnp.split(proj, IN_SPLITS, axis=-1)
    xc = jax.nn.silu(_causal_dwconv(xm, w_mlstm_conv, b_mlstm_conv)).reshape(Bsz, S, MLSTM_HEADS, MLSTM_VDIM)
    q = jnp.einsum('bshc,hcd->bhsd', xc, w_mlstm_q)
    k = jnp.einsum('bshc,hcd->bhsd', xc, w_mlstm_k)
    v = xm.reshape(Bsz, S, MLSTM_HEADS, MLSTM_VDIM).transpose(0, 2, 1, 3)
    hm = _mlstm_chunkwise(q, k, v, ip.transpose(0, 2, 1), fp.transpose(0, 2, 1))
    hm = _standardize(hm).transpose(0, 2, 1, 3).reshape(Bsz, S, MLSTM_WIDTH).astype(h.dtype)
    y_a = (hm * mlstm_norm_gain * jax.nn.sigmoid(om)) @ w_mlstm_down
    ys = jax.nn.gelu(_s5_ssm(us, s5_lam_re, s5_lam_im, s5_log_dt, s5_b_re, s5_b_im, s5_c_re, s5_c_im, s5_d))
    val, gate = jnp.split(ys @ w_s5_glu, 2, axis=-1)
    y_b = val * jax.nn.sigmoid(gate)
    y = jax.nn.sigmoid(ga) * y_a + jax.nn.sigmoid(gb) * y_b
    return y @ w_mix_out

def _conv_glu_ffn(h, w_ffn_up, w_ffn_conv, b_ffn_conv, w_ffn_down):
    val, gate = jnp.split(h @ w_ffn_up, 2, axis=-1)
    gate = jax.nn.gelu(_causal_dwconv(gate, w_ffn_conv, b_ffn_conv))
    return (gate * val) @ w_ffn_down

def second_inputs(seed: int = 0) -> dict:
    key = jax.random.key(seed)
    ks = iter(jax.random.split(key, 40))
    f32 = jnp.float32
    L = DEPTH

    def nrm(shape, scale):
        return scale * jax.random.normal(next(ks), shape, f32)

    x = nrm((BATCH, SEQ, D_MODEL), 1.0)
    c = nrm((BATCH, D_MODEL), 1.0)
    w_ada = nrm((L, D_MODEL, 6 * D_MODEL), 0.5 * D_MODEL ** -0.5)
    b_ada = nrm((L, 6 * D_MODEL), 0.02)
    w_in = nrm((L, D_MODEL, IN_WIDTH_2), D_MODEL ** -0.5)
    f_bias = jnp.linspace(3.0, 6.0, MLSTM_HEADS, dtype=f32)
    b_in = nrm((L, IN_WIDTH_2), 0.02).at[:, F_OFF:F_OFF + MLSTM_HEADS].add(f_bias)
    w_mlstm_conv = nrm((L, MLSTM_CONV, MLSTM_WIDTH), MLSTM_CONV ** -0.5)
    b_mlstm_conv = nrm((L, MLSTM_WIDTH), 0.02)
    w_mlstm_q = nrm((L, MLSTM_HEADS, MLSTM_VDIM, MLSTM_QKDIM), MLSTM_VDIM ** -0.5)
    w_mlstm_k = nrm((L, MLSTM_HEADS, MLSTM_VDIM, MLSTM_QKDIM), MLSTM_VDIM ** -0.5)
    mlstm_norm_gain = 1.0 + nrm((L, MLSTM_WIDTH), 0.02)
    w_mlstm_down = nrm((L, MLSTM_WIDTH, D_MODEL), MLSTM_WIDTH ** -0.5)
    s5_lam_re = -0.5 + nrm((L, S5_GROUPS, S5_STATE), 0.01)
    s5_lam_im = math.pi * jnp.arange(S5_STATE, dtype=f32) + nrm((L, S5_GROUPS, S5_STATE), 0.01)
    s5_log_dt = math.log(S5_DT_MIN) + jax.random.uniform(next(ks), (L, S5_GROUPS), f32) * (math.log(S5_DT_MAX) - math.log(S5_DT_MIN))
    s5_b_re = nrm((L, S5_GROUPS, S5_STATE, S5_GROUP), (2.0 * S5_GROUP) ** -0.5)
    s5_b_im = nrm((L, S5_GROUPS, S5_STATE, S5_GROUP), (2.0 * S5_GROUP) ** -0.5)
    s5_c_re = nrm((L, S5_GROUPS, S5_GROUP, S5_STATE), (2.0 * S5_STATE) ** -0.5)
    s5_c_im = nrm((L, S5_GROUPS, S5_GROUP, S5_STATE), (2.0 * S5_STATE) ** -0.5)
    s5_d = nrm((L, S5_WIDTH), 1.0)
    w_s5_glu = nrm((L, S5_WIDTH, 2 * D_MODEL), S5_WIDTH ** -0.5)
    w_mix_out = nrm((L, D_MODEL, D_MODEL), BETA * D_MODEL ** -0.5)
    ln1_gain = 1.0 + nrm((L, D_MODEL), 0.02)
    ln1_bias = nrm((L, D_MODEL), 0.02)
    w_ffn_up = nrm((L, D_MODEL, 2 * FFN_HIDDEN), D_MODEL ** -0.5)
    w_ffn_conv = nrm((L, FFN_CONV, FFN_HIDDEN), FFN_CONV ** -0.5)
    b_ffn_conv = nrm((L, FFN_HIDDEN), 0.02)
    w_ffn_down = nrm((L, FFN_HIDDEN, D_MODEL), BETA * FFN_HIDDEN ** -0.5)
    ln2_gain = 1.0 + nrm((L, D_MODEL), 0.02)
    ln2_bias = nrm((L, D_MODEL), 0.02)
    return {'x': x, 'c': c, 'w_ada': w_ada, 'b_ada': b_ada, 'w_in': w_in, 'b_in': b_in,
            'w_mlstm_conv': w_mlstm_conv, 'b_mlstm_conv': b_mlstm_conv, 'w_mlstm_q': w_mlstm_q,
            'w_mlstm_k': w_mlstm_k, 'mlstm_norm_gain': mlstm_norm_gain, 'w_mlstm_down': w_mlstm_down,
            's5_lam_re': s5_lam_re, 's5_lam_im': s5_lam_im, 's5_log_dt': s5_log_dt, 's5_b_re': s5_b_re,
            's5_b_im': s5_b_im, 's5_c_re': s5_c_re, 's5_c_im': s5_c_im, 's5_d': s5_d, 'w_s5_glu': w_s5_glu,
            'w_mix_out': w_mix_out, 'ln1_gain': ln1_gain, 'ln1_bias': ln1_bias, 'w_ffn_up': w_ffn_up,
            'w_ffn_conv': w_ffn_conv, 'b_ffn_conv': b_ffn_conv, 'w_ffn_down': w_ffn_down,
            'ln2_gain': ln2_gain, 'ln2_bias': ln2_bias}

def second_block(x, c, w_ada, b_ada, w_in, b_in, w_mlstm_conv, b_mlstm_conv, w_mlstm_q, w_mlstm_k,
              mlstm_norm_gain, w_mlstm_down, s5_lam_re, s5_lam_im, s5_log_dt, s5_b_re, s5_b_im,
              s5_c_re, s5_c_im, s5_d, w_s5_glu, w_mix_out, ln1_gain, ln1_bias, w_ffn_up, w_ffn_conv,
              b_ffn_conv, w_ffn_down, ln2_gain, ln2_bias):
    c_act = jax.nn.silu(c)
    for l in range(DEPTH):
        mod = c_act @ w_ada[l] + b_ada[l]
        sh1, sc1, g1, sh2, sc2, g2 = [m[:, None, :] for m in jnp.split(mod, 6, axis=-1)]
        h = _standardize(x) * (1.0 + sc1) + sh1
        mix = _hybrid_mixer(h, w_in[l], b_in[l], w_mlstm_conv[l], b_mlstm_conv[l], w_mlstm_q[l],
                            w_mlstm_k[l], mlstm_norm_gain[l], w_mlstm_down[l], s5_lam_re[l],
                            s5_lam_im[l], s5_log_dt[l], s5_b_re[l], s5_b_im[l], s5_c_re[l],
                            s5_c_im[l], s5_d[l], w_s5_glu[l], w_mix_out[l])
        x = _layer_norm(ALPHA * x + (1.0 + g1) * mix, ln1_gain[l], ln1_bias[l])
        h = _standardize(x) * (1.0 + sc2) + sh2
        f = _conv_glu_ffn(h, w_ffn_up[l], w_ffn_conv[l], b_ffn_conv[l], w_ffn_down[l])
        x = _layer_norm(ALPHA * x + (1.0 + g2) * f, ln2_gain[l], ln2_bias[l])
    return x


_first_inputs = second_inputs


def second_inputs(seed=0):
    import zlib

    import numpy as np

    out = dict(_first_inputs(seed))
    spreads = {}
    factors = {'b_ada': 2.938,
     'b_mlstm_conv': 8.0,
     'mlstm_norm_gain': 29.745,
     's5_lam_re': 64.0,
     's5_lam_im': 55.416,
     's5_log_dt': 64.0,
     's5_b_re': 64.0,
     's5_b_im': 64.0,
     's5_c_re': 64.0,
     's5_c_im': 64.0,
     'ln1_gain': 7.391,
     'ln1_bias': 7.711,
     'b_ffn_conv': 8.0,
     'ln2_gain': 7.514,
     'ln2_bias': 8.033}
    for name, (base, spread) in spreads.items():
        noise = np.random.default_rng([zlib.crc32(name.encode()), seed]).standard_normal(out[name].shape)
        drawn = base * np.exp(spread * noise) if base else spread * noise
        out[name] = __import__('jax').numpy.asarray(drawn.astype(out[name].dtype))
    for name, factor in factors.items():
        out[name] = (out[name] * factor).astype(out[name].dtype)
    return out


_narrow_inputs = second_inputs


def second_inputs(seed=0):
    out = dict(_narrow_inputs(seed))
    wider = {'mlstm_norm_gain': 3.38,
     's5_d': 3.25,
     'ln1_gain': 3.12,
     'ln1_bias': 3.14,
     'b_ffn_conv': 8.13,
     'ln2_gain': 3.08,
     'ln2_bias': 3.08}
    for name, times in wider.items():
        mean = out[name].mean()
        out[name] = (mean + times * (out[name] - mean)).astype(out[name].dtype)
    return out


def setup_inputs(seed=0):
    out = dict(first_inputs(seed))
    for name, value in second_inputs(seed + 1).items():
        if name != "x":
            out[name + "_2"] = value
    return out


def reference(
    x, ln1_w, w_in, q_norm_w, k_norm_w, cmp_pe_k, cmp_pe_v, cmp_wk1, cmp_wk2, cmp_wv1, cmp_wv2,
    ret_norm_w, w_out, ln2_w, w_up, w_down, c_2, w_ada_2, b_ada_2, w_in_2, b_in_2,
    w_mlstm_conv_2, b_mlstm_conv_2, w_mlstm_q_2, w_mlstm_k_2, mlstm_norm_gain_2, w_mlstm_down_2,
    s5_lam_re_2, s5_lam_im_2, s5_log_dt_2, s5_b_re_2, s5_b_im_2, s5_c_re_2, s5_c_im_2, s5_d_2,
    w_s5_glu_2, w_mix_out_2, ln1_gain_2, ln1_bias_2, w_ffn_up_2, w_ffn_conv_2, b_ffn_conv_2,
    w_ffn_down_2, ln2_gain_2, ln2_bias_2,
):
    x = first_block(
        x, ln1_w, w_in, q_norm_w, k_norm_w, cmp_pe_k, cmp_pe_v, cmp_wk1, cmp_wk2, cmp_wv1,
        cmp_wv2, ret_norm_w, w_out, ln2_w, w_up, w_down,
    )
    return second_block(
        x, c_2, w_ada_2, b_ada_2, w_in_2, b_in_2, w_mlstm_conv_2, b_mlstm_conv_2, w_mlstm_q_2,
        w_mlstm_k_2, mlstm_norm_gain_2, w_mlstm_down_2, s5_lam_re_2, s5_lam_im_2, s5_log_dt_2,
        s5_b_re_2, s5_b_im_2, s5_c_re_2, s5_c_im_2, s5_d_2, w_s5_glu_2, w_mix_out_2, ln1_gain_2,
        ln1_bias_2, w_ffn_up_2, w_ffn_conv_2, b_ffn_conv_2, w_ffn_down_2, ln2_gain_2,
        ln2_bias_2,
    )


_drawn_inputs = setup_inputs


def setup_inputs(seed=0):
    import zlib

    import numpy as np

    out = dict(_drawn_inputs(seed))
    spreads = {}
    factors = {'q_norm_w': 8.0,
     'k_norm_w': 8.0,
     'cmp_pe_k': 30.894,
     'cmp_pe_v': 7.093,
     'ret_norm_w': 3.652}
    for name, (base, spread) in spreads.items():
        noise = np.random.default_rng([zlib.crc32(name.encode()), seed]).standard_normal(out[name].shape)
        drawn = base * np.exp(spread * noise) if base else spread * noise
        out[name] = __import__('jax').numpy.asarray(drawn.astype(out[name].dtype))
    for name, factor in factors.items():
        out[name] = (out[name] * factor).astype(out[name].dtype)
    return out
```

```python
import math
from contextlib import ExitStack

import numpy as np

import concourse.bass as bass
from concourse import mybir

F32 = mybir.dt.float32
F32R = mybir.dt.float32r
ALU = mybir.AluOpType
ACT = mybir.ActivationFunctionType
AX = mybir.AxisListType.X

P = 128
S = 512
NT = S // P
D = 1024
DC = D // P
TILE_BLOCKS = 16
TILE_COLS = TILE_BLOCKS * P

HEADS, GROUPS, REP, DH = 8, 2, 4, 64
NCMP, NCMP_PAD, CMP_HID = 31, 32, 256
RET_H, RET_DK, RET_DV = 4, 64, 128
FF1_GROUPS = [8, 8, 8, 8]
ML_H, ML_DK, ML_DV = 4, 128, 256
S5_CHUNKS = 16
FF2_GROUPS = [8, 8, 6]
ALPHA = 2.0 ** 0.25
RMS_EPS, LN_EPS = 1e-6, 1e-5
NEG = -1.0e30
ROUND = 12582912.0

WIN = (["kc", "vc", "q0", "q1", "q2", "q3", "ks", "kw", "vs", "vw", "gate", "rq0", "rq1", "rk0", "rk1"]
       + [f"rv{i}" for i in range(4)] + [f"rg{i}" for i in range(4)])
NORMED = [n for n in WIN if n in ("kc", "ks", "kw") or (n[0] == "q" and n != "gate")]
ROPED = [n for n in WIN if n in NORMED or n[:2] in ("rq", "rk")]
TURNED = [n for n in WIN if n in ("vs", "vw", "gate") or n[:2] == "rv"]


SPILLED = [f"{nm}{n}" for nm in ("xm", "om", "ga", "gb") for n in range(DC)]


def plan_chunks():
    ch = [(n, 8) for n in WIN] + [(f"wout{n}", 8) for n in range(DC)]
    for g, kg in enumerate(FF1_GROUPS):
        ch += [(f"up{g}.{j}", 8) for j in range(kg)] + [(f"dn{g}.{n}", kg) for n in range(DC)]
    ch += [(f"us{c}", 8) for c in range(4)] + [("if", 8)]
    ch += [(n, 8) for n in SPILLED]
    for h in range(ML_H):
        ch += [(f"mq{h}", 2), (f"mk{h}", 2)]
    for n in range(DC):
        ch += [(f"md{n}", 8), (f"gv{n}", 4), (f"gg{n}", 4)]
    ch += [(f"mix{n}", 8) for n in range(DC)]
    for g, kg in enumerate(FF2_GROUPS):
        for j in range(kg):
            ch += [(f"fv{g}.{j}", 8), (f"fg{g}.{j}", 8)]
        ch += [(f"fd{g}.{n}", kg) for n in range(DC)]
    return ch


CHUNKS = plan_chunks()
INDEX = {name: g for g, (name, _) in enumerate(CHUNKS)}
FIRST_BLOCK = np.concatenate([[0], np.cumsum([k for _, k in CHUNKS])]).tolist()
NTILES = FIRST_BLOCK[-1] // TILE_BLOCKS
assert FIRST_BLOCK[-1] % TILE_BLOCKS == 0


def last_tile(g):
    return (FIRST_BLOCK[g + 1] - 1) // TILE_BLOCKS


def last_chunk_of_tile(t):
    b = TILE_BLOCKS * (t + 1) - 1
    return next(g for g in range(len(CHUNKS)) if FIRST_BLOCK[g] <= b < FIRST_BLOCK[g + 1])


PAR = {}
for _name, _n in [("ln1", 8), ("qn", 1), ("kn", 3), ("retn", 4), ("ln2", 8), ("pek", 16), ("pev", 16),
                  ("b_us", 4), ("b_if", 1), ("b_xm", 8), ("b_om", 8), ("b_ga", 8), ("b_gb", 8),
                  ("cw", 32), ("cb", 8), ("mg", 8), ("lre", 16), ("lim", 16), ("ldt", 16), ("s5d", 4),
                  ("fcw", 66), ("fcb", 22), ("bada", 48)]:
    PAR[_name] = (sum(v[1] for v in PAR.values()), _n)
NPAR = sum(v[1] for v in PAR.values())

CON = {}
for _name, _n in [("ident", 128), ("mean64", 128), ("rot", 128), ("tri", 128), ("sel", 512),
                  ("eps", 2)]:
    CON[_name] = (sum(v[1] for v in CON.values()), _n)
NCON = sum(v[1] for v in CON.values())


def constants():
    p = np.arange(P)
    con = np.zeros((P, NCON), np.float64)

    def put(name, a):
        con[:a.shape[0], CON[name][0]:CON[name][0] + a.shape[1]] = a
    put("ident", np.eye(P))
    put("mean64", (p[:, None] // 64 == p[None, :] // 64) / 64.0)
    rot = np.zeros((P, P))
    for m in range(P):
        rot[m + 32 if m % 64 < 32 else m - 32, m] = -1.0 if m % 64 < 32 else 1.0
    put("rot", rot)
    put("tri", np.where(p[None, :] >= p[:, None], 0.0, NEG))
    sel = np.zeros((4, 4, P))
    for h in range(4):
        sel[h, h] = 1.0
    put("sel", sel.reshape(4, 512))
    put("eps", np.tile([[RMS_EPS, LN_EPS]], (P, 1)))
    inv = np.float32(10000.0) ** (-np.arange(32, dtype=np.float32) / np.float32(32))
    ang = (np.arange(S, dtype=np.float32)[:, None] * inv[None, :]).astype(np.float64).T
    rope = np.stack([np.tile(np.cos(ang), (4, 1)), np.tile(np.sin(ang), (4, 1))], 1)
    causal = np.where(np.arange(896)[None, :] - 384 <= p[:, None], 0.0, NEG)
    c = np.arange(384)[None, :]
    window = np.where((c <= p[:, None] + 256) & (c > p[:, None]), 0.0, NEG)
    tok = np.arange(NT)[None, :, None] * P + p[:, None, None]
    n = np.arange(NCMP_PAD)[None, None, :]
    ok = (n * 16 + 31 <= tok) & (n < NCMP)
    cmp_mask = np.stack([np.where(ok, 0.0, NEG), ok * 1.0], 1)
    gamma = 1.0 - 2.0 ** (-5.0 - np.arange(RET_H))
    d = np.arange(S)[None, None, :] - p[:, None, None]
    decay = np.where(d >= 0, gamma[None, :, None] ** np.maximum(d, 0), 0.0) * RET_DK ** -0.5
    masks = np.concatenate([causal, window, cmp_mask.reshape(P, -1)], 1)
    return {"con": con, "rope": rope.reshape(P, 1024), "masks": masks, "decay": decay.reshape(P, 2048)}


def build(nc, d, out, stop=99):
    ctx = ExitStack()
    with ctx:
        sems = {}

        def sem(name):
            if name not in sems:
                sems[name] = ctx.enter_context(nc.semaphore(name))
            return sems[name]

        base = [16512]

        def region(nbytes):
            at = base[0]
            base[0] += nbytes
            assert base[0] <= 229344, base[0]
            return at

        def at(name, shape, off, dt=F32):
            return nc.alloc_sbuf_tensor_at(name, shape, dt, offset=off)

        def new(name, shape, dt=F32):
            n = 4 * int(np.prod(shape[1:]))
            return at(name, shape, region((n + 31) // 32 * 32), dt)

        RAW = 2
        raw = [new(f"raw{i}", [P, TILE_COLS]) for i in range(RAW)]
        whi = [new(f"whi{i}", [P, TILE_COLS], F32R) for i in range(2)]
        wlo = [new(f"wlo{i}", [P, TILE_COLS], F32R) for i in range(2)]
        offA = region(32768)
        Ahi, Alo = at("Ahi", [P, 8, S], offA, F32R), at("Alo", [P, 8, S], offA + 16384, F32R)
        offB = region(32768)
        Bhi, Blo = at("Bhi", [P, 8, S], offB, F32R), at("Blo", [P, 8, S], offB + 16384, F32R)
        offX = region(16384)
        X = at("X", [P, NT, D], offX)
        offY = region(16384)
        Y = at("Y", [P, DC, S], offY)
        N = at("N", [P, NT, D], offY)
        con = new("con", [P, NCON])
        par = new("par", [P, NPAR])
        mod = new("mod", [P, 48])
        st6 = new("st6", [P, 2, 6])
        st6c = new("st6c", [P, 4, 2, 6])
        mv = new("mv", [P, NT, 2])
        sd = new("sd", [P, NT])
        dd = new("dd", [P, 8])
        offF = base[0]
        Fb = [new(f"F{i}", [P, S]) for i in range(2)]
        offR = base[0]
        room = 229344 - offR

        def c_(name, rows=P):
            a, n = CON[name]
            return con[0:rows, a:a + n]

        def p_(name, i=0, n=1, rows=P):
            a = PAR[name][0] + i
            return par[0:rows, a:a + n]

        ident = c_("ident")
        eps = {"rms": con[:, CON["eps"][0]:CON["eps"][0] + 1], "ln": con[:, CON["eps"][0] + 1:CON["eps"][0] + 2]}

        cur = [offR]

        def rest(name, shape, dt=F32):
            n = 4 * int(np.prod(shape[1:]))
            t = at(name, shape, cur[0], dt)
            cur[0] += (n + 31) // 32 * 32
            assert cur[0] <= 229344, (name, cur[0])
            return t

        Q = rest("Q", [P, 4, S])
        K = rest("K", [P, 3, S])
        RQ = rest("RQ", [P, 2, S])
        RK = rest("RK", [P, 2, S])
        RG = rest("RG", [P, 4, S])
        VT = rest("VT", [P, 2, NT, P])
        RV = rest("RV", [P, NT, 4, P])
        VC = rest("VC", [P, S])
        GT = rest("GT", [P, NT, 24])
        F4 = [at(f"F4{i}", [P, S], offX + 2048 * i) for i in range(4)]
        SQ = at("SQ", [P, S], offX + 8192)
        RS = at("RS", [P, S], offX + 10240)
        rope = at("rope", [P, 2, S], offX + 12288)
        w1 = [at("w1k", [P, 16, CMP_HID], offB), at("w1v", [P, 16, CMP_HID], offB + 16384)]
        kc2 = at("kc2", [P, 2, S], offY)
        vc2 = at("vc2", [P, 2, S], offY + 4096)
        kcp = [at("kcp", [P, 16, 2, NCMP], offY + 8192), at("vcp", [P, 16, 2, NCMP], offY + 8192 + 3968)]
        o = offX
        oacc = at("oacc", [P, NT, S], o)
        HK = [at("HK", [P, 2, 2, NCMP], o + 8192), at("HV", [P, 2, 2, NCMP], o + 8704)]
        HVr = at("HVr", [P, 2, 2, 4, NCMP_PAD], o + 9216)
        KCM = at("KCM", [P, 2, NCMP_PAD], o + 11264)
        VB = at("VB", [P, 2, REP, DH], offY)
        w2k = at("w2k", [P, 2, P], o + 12288)
        w2v = at("w2v", [P, 2, DH], o + 13312)
        SUM = at("SUM", [P, 64], o + 13824)
        MX = at("MX", [P, 64], o + 14080)
        NM = at("NM", [P, 64], o + 14336)
        m8 = [at(f"m8{i}", [P, 8], o + 14592 + 32 * i) for i in range(4)]
        o = offA
        masks = at("masks", [P, 1536], o)
        decay = at("decay", [P, 4, S], o + 6144)
        sS = [at(f"sS{i}", [P, S], o + 14336 + 2048 * i) for i in range(2)]
        Pr = [at(f"Pr{i}", [P, S], o + 18432 + 2048 * i) for i in range(2)]
        PT = [at(f"PT{i}", [P, NT, P], o + 22528 + 2048 * i) for i in range(2)]
        cS = at("cS", [P, HEADS, NCMP_PAD], o + 26624)
        cP = at("cP", [P, HEADS, NCMP_PAD], o + 27648)
        cT = at("cT", [P, 2, P], o + 28672)
        tmp5 = at("tmp5", [P, S], o + 29696)
        RW = [at(f"RW{i}", [P, 1280], o + 14336 + 5120 * i) for i in range(2)]
        YN = at("YN", [P, NT, P], o + 14336 + 10240)

        cur[0] = offR
        adaw = [rest(f"adaw{i}", [P, D]) for i in range(3)]
        cB = rest("cB", [P, D])
        offJ = cur[0]
        junk = rest("junk", [P, D])
        G4 = [rest(f"G4{i}", [P, S]) for i in range(4)]
        ring_step = [rest("cos_t", [P, 16, P]), rest("sin_t", [P, 16, P])]
        s16 = rest("s16", [P, 20, 16])
        pw = rest("pw", [P, 9, 2, 16])
        seg = rest("seg", [P, 2, 16, 4])
        offBC = cur[0]
        bri = [rest("bre", [P, 16, 16]), rest("bim", [P, 16, 16])]
        cri = [rest("cre", [P, 4, P]), rest("cim", [P, 4, P])]
        stage = [at(f"stage{i}", [P, S], offBC + 2048 * i) for i in range(3)]
        dbl = [at("dbl0", [P, 16, 64], offJ), at("dbl1", [P, 16, 64], offF)]

        cur[0] = offR
        YShi, YSlo = rest("YShi", [P, 4, S], F32R), rest("YSlo", [P, 4, S], F32R)
        offU = cur[0]
        U = rest("U", [P, 4, S])
        BT = [at("BTr", [P, S5_CHUNKS, P], offB), at("BTi", [P, S5_CHUNKS, P], offB + 8192)]
        CT = [at("CTr", [P, S5_CHUNKS, P], offB + 16384), at("CTi", [P, S5_CHUNKS, P], offB + 24576)]
        y8 = [at(f"y8{i}", [P, S], offY + 2048 * i) for i in range(8)]
        xx = [rest(f"xx{i}", [P, S]) for i in range(2)]
        assert cur[0] <= offJ + 12288
        IF = at("IF", [P, S], offY)
        ifr = [at(f"ifr{i}", [P, S], offY + 2048 * (1 + i)) for i in range(4)]
        cur[0] = offU
        XM = [at(f"XM{i}", [P, 2, S + 3], offA + 4160 * i) for i in range(2)]
        SO = at("SO", [P, 2, 2, S], offA + 8320)
        XCh, XCl = rest("XCh", [P, 2, S], F32R), rest("XCl", [P, 2, S], F32R)
        QK = rest("QK", [P, 2, S])
        V = rest("V", [P, NT, ML_DV + 1])
        W = rest("W", [P, 1280])
        cur2 = [offY + 2048]

        def iny(name, shape):
            n = 4 * int(np.prod(shape[1:]))
            t = at(name, shape, cur2[0])
            cur2[0] += (n + 31) // 32 * 32
            assert cur2[0] <= offY + 16384, name
            return t
        negM = IF
        NB = iny("NB", [P, S])
        NBd = iny("NBd", [P, NT, P])
        H = iny("H", [P, NT, ML_DV])
        AEC = iny("AEC", [P, 2, NT, 4])
        E = [rest(f"E{i}", [P, S]) for i in range(2)]
        CA = [rest("CA0", [P, S])]
        cur[0] = offU
        G8 = [rest(f"G8{i}", [P, S]) for i in range(3)]
        gates = rest("gates", [P, 3, 2, S])
        GB = rest("GB", [P, 2, D])
        GP = rest("GP", [P, S + 2])
        FV = rest("FV", [P, S])
        FG = rest("FG", [P, S])

        banks = [ctx.enter_context(nc.psum_tensor(f"bank{i}", [P, S], F32)) for i in range(8)]
        pools = {"G": banks[0:2], "T": banks[2:6], "O": banks[6:8]}
        used = {k: 0 for k in pools}
        product = {}

        def rd(t):
            return t.bitcast(F32)

        spill = nc.dram_tensor("spill", (len(SPILLED), P, S), F32, kind="Internal").ap()
        block = ctx.enter_context(nc.Block())

        def full(name):
            pool, b, k = product[name]
            return sem(f"full_{pool}{b}"), k

        def taken(name):
            pool, b, k = product[name]
            return sem(f"free_{pool}{b}"), k

        def bank_of(name):
            pool, b, _ = product[name]
            return pools[pool][b]

        class Count:

            def __init__(self):
                self.given, self.waited = {}, {}

            def did(self, name):
                self.given[name] = self.given.get(name, 0) + 1
                return self.given[name]

            def due(self, name, k=1):
                self.waited[name] = self.waited.get(name, 0) + k
                return self.waited[name]

        @block.tensor
        def _(pe):
            T = Count()

            def bank(pool):
                n = used[pool]
                b, k = n % len(pools[pool]), n // len(pools[pool])
                if k:
                    pe.wait_ge(sem(f"free_{pool}{b}"), k)
                used[pool] += 1
                return pools[pool][b], (pool, b, k + 1)

            def done(ins, name, where):
                ins.then_inc(sem(f"full_{where[0]}{where[1]}"), 1)
                product[name] = where

            def gemm(name, hi, lo, before=None):
                g = INDEX[name]
                kn = CHUNKS[g][1]
                ps, where = bank("G")
                for k in range(kn):
                    b = FIRST_BLOCK[g] + k
                    t, c = b // TILE_BLOCKS, b % TILE_BLOCKS
                    if c == 0:
                        pe.wait_ge(sem("lo_split"), t + 1)
                    if before:
                        pe.wait_ge(sem(before), T.due(before))
                    wh, wl = (w[t % 2][:, c * P:(c + 1) * P] for w in (whi, wlo))
                    pe.matmul(ps[:], wh, hi[:, k], start=(k == 0), stop=False)
                    pe.matmul(ps[:], wh, lo[:, k], start=False, stop=False)
                    ins = pe.matmul(ps[:], wl, hi[:, k], start=False, stop=(k == kn - 1))
                done(ins, name, where)

            def turn(name, srcs, pool="T", width=P, rows=P, cols=P):
                ps, where = bank(pool)
                for i, s in enumerate(srcs):
                    ins = pe.transpose(ps[0:cols, i * width:i * width + rows], s, ident[0:rows, 0:rows])
                done(ins, name, where)

            def normed_in(s):
                pe.wait_ge(sem("norm_rows"), T.due("norm_rows", NT))
                for c in range(DC):
                    turn(f"xT{s}.{c}", [N[:, i, c * P:(c + 1) * P] for i in range(NT)])

            pe.wait_ge(sem("con_in"), T.due("con_in", 16))
            normed_in(0)

            def post1(n, c):
                if n in NORMED:
                    pe.wait_ge(*taken(n))
                    ps, where = bank("T")
                    done(pe.matmul(ps[:], c_("mean64"), SQ[:], start=True, stop=True), f"ssq_{n}", where)
                elif n in TURNED:
                    pe.wait_ge(*taken(n))
                    if n == "gate":
                        turn_gate(n, c)
                    else:
                        turn(f"turn_{n}", [F4[c % 4][:, i * P:(i + 1) * P] for i in range(NT)])

            def turn_gate(n, c):
                ps, where = bank("T")
                for i in range(NT):
                    ins = pe.transpose(ps[:, i * 24:(i + 1) * 24], F4[c % 4][0:24, i * P:(i + 1) * P],
                                       ident[0:24, 0:24])
                done(ins, f"turn_{n}", where)

            def post2(n, c):
                if n in ROPED:
                    pe.wait_ge(sem("rope_in"), T.due("rope_in"))
                    ps, where = bank("T")
                    done(pe.matmul(ps[:], c_("rot"), F4[c % 4][:], start=True, stop=True), f"rot_{n}", where)

            for c, n in enumerate(WIN):
                gemm(n, Ahi, Alo, "A_ready" if c == 0 else None)
                if c >= 1:
                    post1(WIN[c - 1], c - 1)
                if c >= 2:
                    post2(WIN[c - 2], c - 2)

            if stop <= 1:
                return
            pe.wait_ge(sem("w1_in"), T.due("w1_in", 64))
            for w in range(2):
                pe.wait_ge(sem("cmp_in"), T.due("cmp_in"))
                for hc in range(2):
                    ps, where = bank("T")
                    for l in range(16):
                        ins = pe.matmul(ps[:, 0:2 * NCMP], w1[w][:, l, hc * P:(hc + 1) * P],
                                        kcp[w][:, l].rearrange("p a b -> p (a b)"), start=(l == 0), stop=(l == 15))
                    done(ins, f"hid{w}.{hc}", where)
            pe.wait_ge(*taken("hid0.1"))
            ps, where = bank("T")
            for hc in range(2):
                ins = pe.matmul(ps[:, 0:2 * NCMP], w2k[:, hc, :], HK[0][:, hc].rearrange("p a b -> p (a b)"),
                                start=(hc == 0), stop=(hc == 1))
            done(ins, "kcmp", where)
            pe.wait_ge(sem("hidv_ready"), T.due("hidv_ready"))
            ps, where = bank("T")
            for g in range(GROUPS):
                for hc in range(2):
                    ins = pe.matmul(ps[:, g * DH:(g + 1) * DH], HVr[:, hc, g].rearrange("p a b -> p (a b)"),
                                    w2v[:, hc, :], start=(hc == 0), stop=(hc == 1))
            done(ins, "vcmp", where)
            pe.wait_ge(*taken("kcmp"))
            pe.wait_ge(*taken("vcmp"))

            for i in range(NT):
                for g in range(GROUPS):
                    ps, where = bank("T")
                    for r in range(REP):
                        ins = pe.matmul(ps[:, r * NCMP_PAD:(r + 1) * NCMP_PAD],
                                        Q[64 * g:64 * g + 64, r, i * P:(i + 1) * P], KCM[64 * g:64 * g + 64, g, :],
                                        start=True, stop=True)
                    done(ins, f"cs{i}.{g}", where)
                pe.wait_ge(sem("cp_ready"), T.due("cp_ready"))
                turn(f"ct{i}", [cP[:, 4 * g:4 * g + 4, :].rearrange("p a b -> p (a b)") for g in range(2)])
                pe.wait_ge(*taken(f"ct{i}"))
                ps, where = bank("O")
                for g in range(GROUPS):
                    ins = pe.matmul(ps[:, g * 256:(g + 1) * 256], cT[:, g, :], VB[:, g].rearrange("p r e -> p (r e)"),
                                    start=True, stop=True)
                done(ins, f"co{i}", where)

            units = [(i, b, hh) for i in range(NT) for b in range(2) for hh in range(HEADS)]
            obank = {}

            def keys(i, b):
                nk = i + 1 if b == 0 else min(i + 1, 3)
                return i + 1 - nk, nk

            def scores(u):
                i, b, hh = units[u]
                g, r = divmod(hh, REP)
                k0, nk = keys(i, b)
                ps, where = bank("T")
                done(pe.matmul(ps[:, 0:nk * P], Q[64 * g:64 * g + 64, r, i * P:(i + 1) * P],
                               K[64 * g:64 * g + 64, 1 + b, k0 * P:(k0 + nk) * P], start=True, stop=True),
                     f"s{u}", where)

            def probs(u):
                i, b, hh = units[u]
                pe.wait_ge(sem("p_ready"), T.due("p_ready"))
                turn(f"pt{u}", [Pr[u % 2][:, j * P:(j + 1) * P] for j in range(keys(i, b)[1])])

            def values(u):
                i, b, hh = units[u]
                g = hh // REP
                k0, nk = keys(i, b)
                pe.wait_ge(*taken(f"pt{u}"))
                if hh == 0:
                    obank[0], obank[1] = bank("O")
                for j in range(nk):
                    ins = pe.matmul(obank[0][:, hh * DH:(hh + 1) * DH], PT[u % 2][:, j, :],
                                    VT[:, b, k0 + j, g * DH:(g + 1) * DH], start=(j == 0), stop=(j == nk - 1))
                if hh == HEADS - 1:
                    done(ins, f"o{i}.{b}", obank[1])
                else:
                    ins.then_inc(sem("pv_done"), 1)
            for u in range(len(units) + 2):
                if u < len(units):
                    scores(u)
                if 1 <= u <= len(units):
                    probs(u - 1)
                if u >= 2:
                    values(u - 2)
            pe.wait_ge(sem("oacc_ready"), T.due("oacc_ready", 2 * NT))
            for c in range(4):
                turn(f"mixT{c}", [oacc[:, i, c * P:(c + 1) * P] for i in range(NT)])

            for h in range(RET_H):
                c, off = divmod(h, 2)
                rows = slice(64 * off, 64 * off + 64)
                for j in range(NT):
                    ps, where = bank("T")
                    done(pe.matmul(ps[:, 0:S - j * P], RK[rows, c, j * P:(j + 1) * P], RQ[rows, c, j * P:S],
                                   start=True, stop=True), f"rs{h}.{j}", where)
                pe.wait_ge(sem("rw_ready"), T.due("rw_ready", NT))
                ps, where = bank("O")
                for i in range(NT):
                    for j in range(i + 1):
                        at_ = [0, 512, 896, 1152][j] + (i - j) * P
                        ins = pe.matmul(ps[:, i * P:(i + 1) * P], RW[h % 2][:, at_:at_ + P], RV[:, j, h, :],
                                        start=(j == 0), stop=(j == i))
                done(ins, f"ry{h}", where)
                pe.wait_ge(sem("yn_ready"), T.due("yn_ready"))
                turn(f"mixT{4 + h}", [YN[:, i, :] for i in range(NT)])

            def turned_back(name, buf, accumulated=None):
                if accumulated:
                    pe.wait_ge(sem(accumulated[0]), accumulated[1])
                else:
                    pe.wait_ge(*taken(name))
                turn(f"{name}T", [buf[:, i * P:(i + 1) * P] for i in range(NT)])

            for n in range(DC):
                gemm(f"wout{n}", Bhi, Blo, "B_ready" if n == 0 else None)
                if n:
                    turned_back(f"wout{n - 1}", G4[(n - 1) % 4])
            turned_back(f"wout{DC - 1}", G4[(DC - 1) % 4])

            if stop <= 2:
                return
            normed_in(1)
            for g, kg in enumerate(FF1_GROUPS):
                for j in range(kg):
                    gemm(f"up{g}.{j}", Ahi, Alo, "A_ready" if g == 0 and j == 0 else None)
                for n in range(DC):
                    gemm(f"dn{g}.{n}", Bhi, Blo, "B_ready" if n == 0 else None)
                    if g == 3 and n:
                        turned_back(f"dn{n - 1}", Y[:, n - 1], ("dn_used", 24 + n))
            turned_back(f"dn{DC - 1}", Y[:, DC - 1], ("dn_used", 32))

            if stop <= 3:
                return
            normed_in(2)
            for c in range(4):
                gemm(f"us{c}", Ahi, Alo, "A_ready" if c == 0 else None)
            gemm("if", Ahi, Alo)

            pe.wait_ge(sem("bb_ready"), T.due("bb_ready"))
            for x in range(2):
                turn(f"cT{x}", [cri[x][:, cc, :] for cc in range(4)])
            for x in range(2):
                for q in range(4):
                    turn(f"bt{x}.{q}", [BT[x][:, 4 * q + m, :] for m in range(4)])
                    if q in (1, 3) and 2 * x + q // 2 < 3:
                        gemm(SPILLED[2 * x + q // 2], Ahi, Alo)
            pe.wait_ge(sem("bt_ready"), T.due("bt_ready", 2))
            for k in range(S5_CHUNKS + 1):
                if k < S5_CHUNKS:
                    for x in range(2):
                        ps, where = bank("T")
                        done(pe.matmul(ps[:], BT[x][:, k, :], U[:, k // 4, :], start=True, stop=True),
                             f"bu{x}.{k}", where)
                    gemm(SPILLED[3 + 2 * k if k < 13 else 16 + k], Ahi, Alo)
                if k:
                    cc, m = divmod(k - 1, 4)
                    pe.wait_ge(sem("xs_ready"), T.due("xs_ready"))
                    if m == 0:
                        ops, owhere = bank("O")
                    for x in range(2):
                        ins = pe.matmul(ops[:], CT[x][:, k - 1, :], xx[x][:], start=(m == 0 and x == 0),
                                        stop=(m == 3 and x == 1))
                    if m == 3:
                        done(ins, f"s5y{cc}", owhere)
                    else:
                        ins.then_inc(sem("xs_used"), 1)
                if k < 13:
                    gemm(SPILLED[4 + 2 * k], Ahi, Alo)

            if stop <= 4:
                return
            def mlstm_values(h):
                pe.wait_ge(sem("mw_ready"), T.due("mw_ready", NT))
                for i in range(NT):
                    ps, where = bank("O")
                    for j in range(i + 1):
                        at_ = [0, 512, 896, 1152][j] + (i - j) * P
                        ins = pe.matmul(ps[:, 0:ML_DV + 1], W[:, at_:at_ + P], V[:, j, :],
                                        start=(j == 0), stop=(j == i))
                    done(ins, f"mn{h}.{i}", where)

            def mlstm_back(h):
                pe.wait_ge(sem("hn_ready"), T.due("hn_ready", NT))
                for c in range(2):
                    turn(f"hT{h}.{c}", [H[:, i, c * P:(c + 1) * P] for i in range(NT)])

            pe.wait_ge(sem("ifr_ready"), T.due("ifr_ready"))
            ps, where = bank("T")
            for x in range(2):
                for i in range(NT):
                    ins = pe.transpose(ps[:, (x * NT + i) * 4:(x * NT + i) * 4 + 4],
                                       ifr[2 + x][0:4, i * P:(i + 1) * P], ident[0:4, 0:4])
            done(ins, "aec", where)
            for h in range(ML_H):
                if h == 0:
                    pe.wait_ge(sem("negM_ready"), T.due("negM_ready"))
                ps, where = bank("T")
                done(pe.matmul(ps[:], con[0:4, CON["sel"][0] + h * P:CON["sel"][0] + (h + 1) * P], negM[0:4, :],
                               start=True, stop=True), f"nb{h}", where)
                pe.wait_ge(sem(f"xm_in{h % 2}"), T.due(f"xm_in{h % 2}", 32))
                for c in range(2):
                    turn(f"v{h}.{c}", [XM[h % 2][:, c, 3 + i * P:3 + (i + 1) * P] for i in range(NT)])
                if h:
                    mlstm_values(h - 1)
                pe.wait_ge(sem("xc_ready"), T.due("xc_ready", 2))
                gemm(f"mq{h}", XCh, XCl)
                gemm(f"mk{h}", XCh, XCl)
                pe.wait_ge(*taken(f"mq{h}"))
                pe.wait_ge(*taken(f"mk{h}"))
                for j in range(NT):
                    ps, where = bank("T")
                    done(pe.matmul(ps[:, 0:S - j * P], QK[:, 1, j * P:(j + 1) * P], QK[:, 0, j * P:S],
                                   start=True, stop=True), f"ms{h}.{j}", where)
                pe.wait_ge(*taken(f"v{h}.0"))
                pe.wait_ge(*taken(f"v{h}.1"))
                if h:
                    mlstm_back(h - 1)
            mlstm_values(ML_H - 1)
            mlstm_back(ML_H - 1)

            if stop <= 5:
                return
            pe.wait_ge(sem("ys_ready"), T.due("ys_ready", 4))
            for n in range(DC):
                gemm(f"md{n}", Bhi, Blo, "B_ready" if n == 0 else None)
                gemm(f"gv{n}", YShi, YSlo)
                gemm(f"gg{n}", YShi, YSlo)
            for n in range(DC):
                gemm(f"mix{n}", Ahi, Alo, "A_ready" if n == 0 else None)
                if n:
                    turned_back(f"mix{n - 1}", G8[(n - 1) % 2])
            turned_back(f"mix{DC - 1}", G8[(DC - 1) % 2])

            if stop <= 6:
                return
            normed_in(3)
            for g, kg in enumerate(FF2_GROUPS):
                for j in range(kg):
                    gemm(f"fv{g}.{j}", Ahi, Alo, "A_ready" if g == 0 and j == 0 else None)
                    gemm(f"fg{g}.{j}", Ahi, Alo)
                for n in range(DC):
                    gemm(f"fd{g}.{n}", Bhi, Blo, "B_ready" if n == 0 else None)
                    if g == 2 and n:
                        turned_back(f"fd{n - 1}", Y[:, n - 1], ("fd_used", 16 + n))
            turned_back(f"fd{DC - 1}", Y[:, DC - 1], ("fd_used", 24))

        @block.scalar
        def _(act):
            A = Count()
            split = [0]

            def hi_upto(t):
                while split[0] <= min(t, NTILES - 1):
                    n = split[0]
                    act.wait_ge(sem(f"raw_in{n % RAW}"), 16 * (n // RAW + 1))
                    if n >= 2:
                        pool, b, k = product[CHUNKS[last_chunk_of_tile(n - 2)][0]]
                        act.wait_ge(sem(f"full_{pool}{b}"), k)
                    act.activation(whi[n % 2][:], raw[n % RAW][:], ACT.Copy).then_inc(sem("hi_split"), 1)
                    split[0] += 1

            def take(name):
                hi_upto(last_tile(INDEX[name]) + 1)
                act.wait_ge(*full(name))
                return bank_of(name)

            def normed_out(s):
                hi_upto(last_tile(INDEX[["kc", "up0.0", "us0", "fv0.0"][s]]) + 1)
                if s == 2:
                    act.wait_ge(sem("mod_ready"), A.due("mod_ready"))
                for c in range(DC):
                    n = f"xT{s}.{c}"
                    act.wait_ge(*full(n))
                    ps = bank_of(n)
                    if c >= 2:
                        act.wait_ge(sem("A_ready"), [0, 8, 16, 32][s] + c - 1)
                    if s < 2:
                        ins = act.activation(Fb[c % 2][:], ps[:], ACT.Copy, scale=p_(["ln1", "ln2"][s], c))
                    else:
                        m = (s - 2) * 24
                        ins = act.activation(Fb[c % 2][:], ps[:], ACT.Identity, scale=mod[:, m + 8 + c:m + 9 + c],
                                             bias=mod[:, m + c:m + c + 1])
                    ins.then_inc(taken(n)[0], 1)

            def sqrt_sd():
                act.wait_ge(sem("var_ready"), A.due("var_ready"))
                act.activation(sd[:], sd[:], ACT.Sqrt).then_inc(sem("sd_ready"), 1)
                act.wait_ge(sem("sd_ready"), A.did("sd_ready"))

            act.wait_ge(sem("con_in"), A.due("con_in", 16))
            act.wait_ge(sem("par_in"), A.due("par_in", 16))
            hi_upto(0)
            sqrt_sd()
            normed_out(0)

            def a_post1(n, c):
                if n in NORMED:
                    act.wait_ge(*full(f"ssq_{n}"))
                    ps = bank_of(f"ssq_{n}")
                    if NORMED.index(n):
                        act.wait_ge(sem("rs_used"), A.due("rs_used"))
                    ins = act.activation(RS[:], ps[:], ACT.Sqrt, bias=eps["rms"])
                    ins.then_inc(taken(f"ssq_{n}")[0], 1)
                elif n in TURNED:
                    act.wait_ge(*full(f"turn_{n}"))
                    ps = bank_of(f"turn_{n}")
                    if n == "gate":
                        ins = act.activation(GT[:], ps[:, 0:96].rearrange("p (i c) -> p i c", i=NT), ACT.Copy)
                    elif n[0] == "v":
                        ins = act.activation(VT[:, "sw".index(n[1])], ps[:].rearrange("p (i c) -> p i c", i=NT),
                                             ACT.Copy)
                    else:
                        ins = act.activation(RV[:, :, int(n[2])], ps[:].rearrange("p (i c) -> p i c", i=NT),
                                             ACT.Copy)
                    ins.then_inc(taken(f"turn_{n}")[0], 1)

            for c, n in enumerate(WIN):
                ps = take(n)
                f = F4[c % 4]
                if c >= 4:
                    old = WIN[c - 4]
                    if old in ROPED:
                        act.wait_ge(sem("roped"), ROPED.index(old) + 1)
                    elif old in TURNED:
                        act.wait_ge(*full(f"turn_{old}"))
                if n in NORMED:
                    if NORMED.index(n):
                        act.wait_ge(*full(f"ssq_{NORMED[NORMED.index(n) - 1]}"))
                    act.activation(SQ[:], ps[:], ACT.Square)
                    act.activation(f[:], ps[:], ACT.Copy).then_inc(taken(n)[0], 1)
                elif n == "vc":
                    act.activation(VC[:], ps[:], ACT.Copy).then_inc(taken(n)[0], 1)
                elif n == "gate":
                    act.activation(f[:], ps[:], ACT.Sigmoid).then_inc(taken(n)[0], 1)
                elif n in TURNED:
                    act.activation(f[:], ps[:], ACT.Copy).then_inc(taken(n)[0], 1)
                elif n[:2] == "rg":
                    act.activation(RG[:, int(n[2])], ps[:], ACT.Silu).then_inc(taken(n)[0], 1)
                else:
                    act.activation(f[:], ps[:], ACT.Copy).then_inc(taken(n)[0], 1)
                if c >= 1:
                    a_post1(WIN[c - 1], c - 1)
                if n == "ks":
                    act.wait_ge(*taken("vc"))
                    act.wait_ge(sem("roped"), 1)
                    for t, src in ((kc2, K[:, 0]), (vc2, VC[:])):
                        for g in range(2):
                            act.dma_start(t[0:64, g, :], src[64 * g:64 * g + 64, :]).then_inc(sem("two_rows"), 16)
                            act.dma_start(t[64:128, g, 0:S - 1], src[64 * g:64 * g + 64, 1:S])\
                               .then_inc(sem("two_rows"), 16)

            if stop <= 1:
                return
            act.wait_ge(sem("xfree"), A.due("xfree"))
            for w in range(2):
                for hc in range(2):
                    act.wait_ge(*full(f"hid{w}.{hc}"))
                    ps = bank_of(f"hid{w}.{hc}")
                    ins = act.activation(HK[w][:, hc].rearrange("p a b -> p (a b)"), ps[:, 0:2 * NCMP], ACT.Silu)
                    ins.then_inc(taken(f"hid{w}.{hc}")[0], 1)
            act.wait_ge(*full("kcmp"))
            ps = bank_of("kcmp")
            act.wait_ge(sem("kcm_zero"), A.due("kcm_zero"))
            act.activation(KCM[:, :, 0:NCMP], ps[:, 0:2 * NCMP].rearrange("p (a b) -> p a b", a=2), ACT.Copy).then_inc(taken("kcmp")[0], 1)
            act.wait_ge(*full("vcmp"))
            ps = bank_of("vcmp")
            act.wait_ge(sem("vb_zero"), A.due("vb_zero"))
            for r in range(REP):
                rows = slice(32 * r, 32 * r + 32)
                ins = act.activation(VB[rows, :, r, :], ps[rows, 0:P].rearrange("p (a b) -> p a b", a=2), ACT.Copy)
            ins.then_inc(taken("vcmp")[0], 1)

            for i in range(NT):
                act.wait_ge(sem("cs_ready"), A.due("cs_ready"))
                act.activation(cP[:], cS[:], ACT.Exp, scale=DH ** -0.5).then_inc(sem("ce_ready"), 1)
                act.wait_ge(sem("ce_ready"), A.did("ce_ready"))
                act.wait_ge(*full(f"ct{i}"))
                ps = bank_of(f"ct{i}")
                act.activation(cT[:], ps[:, 0:2 * P].rearrange("p (a b) -> p a b", a=2), ACT.Copy).then_inc(taken(f"ct{i}")[0], 1)

            units = [(i, b, hh) for i in range(NT) for b in range(2) for hh in range(HEADS)]

            def nkeys(u):
                i, b, _ = units[u]
                return i + 1 if b == 0 else min(i + 1, 3)

            def exps(u):
                act.wait_ge(sem("s_ready"), A.due("s_ready"))
                if u >= 2:
                    act.wait_ge(*full(f"pt{u - 2}"))
                n = nkeys(u) * P
                act.activation(Pr[u % 2][:, 0:n], sS[u % 2][:, 0:n], ACT.Exp, scale=DH ** -0.5,
                                      bias=NM[:, u:u + 1], accum_out=SUM[:, u:u + 1]).then_inc(sem("p_ready"), 1)
                act.wait_ge(sem("p_ready"), A.did("p_ready"))

            def pts(u):
                nk = nkeys(u)
                act.wait_ge(*full(f"pt{u}"))
                ps = bank_of(f"pt{u}")
                if u >= 2:
                    v = u - 2
                    if units[v][2] == HEADS - 1:
                        act.wait_ge(*full(f"o{units[v][0]}.{units[v][1]}"))
                    else:
                        act.wait_ge(sem("pv_done"), v + 1 - v // HEADS)
                act.activation(PT[u % 2][:, 0:nk], ps[:, 0:nk * P].rearrange("p (a b) -> p a b", a=nk),
                                      ACT.Copy).then_inc(taken(f"pt{u}")[0], 1)
            for u in range(len(units) + 1):
                if u < len(units):
                    exps(u)
                if u >= 1:
                    pts(u - 1)
            for h in range(RET_H):
                act.wait_ge(sem("rvar_ready"), A.due("rvar_ready"))
                act.activation(sd[:], sd[:], ACT.Sqrt).then_inc(sem("sd_ready"), 1)
                act.wait_ge(sem("sd_ready"), A.did("sd_ready"))

            def back_out(name, buf, scale=1.0, wait=None):
                ps = take(name)
                if wait is not None:
                    act.wait_ge(*full(wait))
                act.activation(buf, ps[:], ACT.Copy, scale=scale).then_inc(taken(name)[0], 1)

            for n in range(DC):
                back_out(f"wout{n}", G4[n % 4][:], wait=f"wout{n - 4}T" if n >= 4 else None)
            if stop <= 2:
                return
            sqrt_sd()
            normed_out(1)
            act.wait_ge(sem("cB_in"), A.due("cB_in", 16))
            act.activation(cB[:], cB[:], ACT.Silu).then_inc(sem("cB_ready"), 1)
            act.wait_ge(sem("cB_ready"), A.did("cB_ready"))
            act.activation(s16[:, 0], p_("ldt", 0, 16), ACT.Exp).then_inc(sem("s5_a"), 1)
            act.wait_ge(sem("s5_a"), A.did("s5_a"))
            for g, kg in enumerate(FF1_GROUPS):
                for j in range(kg):
                    ps = take(f"up{g}.{j}")
                    u = g * 8 + j
                    if u >= 2:
                        act.wait_ge(sem("up_used"), u - 1)
                    if u < 2:
                        act.wait_ge(*full(f"wout{4 + 2 + u}T"))
                    act.activation(G4[2 + u % 2][:], ps[:], ACT.Relu).then_inc(taken(f"up{g}.{j}")[0], 1)
                for n in range(DC):
                    ps = take(f"dn{g}.{n}")
                    v = g * 8 + n
                    if v >= 2:
                        act.wait_ge(sem("dn_used"), v - 1)
                    act.activation(G4[v % 2][:], ps[:], ACT.Copy).then_inc(taken(f"dn{g}.{n}")[0], 1)
                    if v == 3:
                        act.wait_ge(sem("s5_d"), A.due("s5_d", 2))
                        act.activation(s16[:, 3], s16[:, 1], ACT.Exp).then_inc(sem("s5_a"), 1)
                        act.wait_ge(sem("s5_a"), A.did("s5_a"))
                        act.activation(s16[:, 4], s16[:, 5], ACT.Sin).then_inc(sem("s5_a"), 1)
                        act.wait_ge(sem("s5_a"), A.did("s5_a"))
                        act.activation(s16[:, 7], s16[:, 6], ACT.Sin).then_inc(sem("s5_a"), 1)
                        act.wait_ge(sem("s5_a"), A.did("s5_a"))

            if stop <= 3:
                return
            sqrt_sd()
            normed_out(2)
            for c in range(4):
                ps = take(f"us{c}")
                act.activation(U[:, c], ps[:], ACT.Identity, bias=p_("b_us", c)).then_inc(taken(f"us{c}")[0], 1)
            ps = take("if")
            act.activation(IF[:], ps[:], ACT.Identity, bias=p_("b_if")).then_inc(taken("if")[0], 1)
            hi_upto(last_tile(INDEX[SPILLED[2]]))
            act.wait_ge(sem("bb_ready"), A.due("bb_ready"))
            act.wait_ge(*full("cT1"))
            for k, name in enumerate(SPILLED + [""]):
                if name:
                    ps = take(name)
                    if k >= 3:
                        act.wait_ge(sem(f"spilled{k % 3}"), 16 * (k // 3))
                    kind, n = name[:2], int(name[2:])
                    act.activation(stage[k % 3][:], ps[:], ACT.Identity if kind == "xm" else ACT.Sigmoid,
                                          bias=p_(f"b_{kind}", n)).then_inc(taken(name)[0], 1)
                if k:
                    act.wait_ge(*taken(SPILLED[k - 1]))
                    act.dma_start(spill[k - 1], stage[(k - 1) % 3][:]).then_inc(sem(f"spilled{(k - 1) % 3}"), 16)
                if k in (14, 22, 28):
                    act.wait_ge(sem("s5f_ready"), A.due("s5f_ready"))
                    act.activation(Fb[0][:], U[:, (k - 14) // 7], ACT.Gelu_apprx_tanh).then_inc(sem("s5g_ready"), 1)
                    act.wait_ge(sem("s5g_ready"), A.did("s5g_ready"))
            act.wait_ge(sem("s5f_ready"), A.due("s5f_ready"))
            act.activation(Fb[0][:], U[:, 3], ACT.Gelu_apprx_tanh).then_inc(sem("s5g_ready"), 1)
            act.wait_ge(sem("s5g_ready"), A.did("s5g_ready"))
            if stop <= 4:
                return
            act.wait_ge(sem("if_d"), A.due("if_d"))
            act.activation(ifr[0][32:36], ifr[0][32:36], ACT.Exp, scale=-1.0).then_inc(sem("act_step"), 1)
            act.wait_ge(sem("act_step"), A.did("act_step"))
            act.activation(ifr[0][32:36], ifr[0][32:36], ACT.Ln, bias=1.0).then_inc(sem("if_a"), 1)
            act.wait_ge(sem("if_a"), A.did("if_a"))
            act.wait_ge(sem("if_d"), A.due("if_d"))
            act.activation(ifr[1][0:4], ifr[3][32:36], ACT.Copy).then_inc(sem("if_a"), 1)
            act.wait_ge(sem("if_a"), A.did("if_a"))
            act.wait_ge(sem("if_d"), A.due("if_d"))
            act.activation(ifr[3][0:4], ifr[1][0:4], ACT.Exp).then_inc(sem("ifr_ready"), 1)
            act.wait_ge(sem("ifr_ready"), A.did("ifr_ready"))
            act.wait_ge(*full("aec"))
            ps = bank_of("aec")
            act.activation(AEC[:].rearrange("p a b c -> p (a b c)"), ps[:, 0:32], ACT.Copy).then_inc(taken("aec")[0], 1)
            for h in range(ML_H + 1):
                if h < ML_H:
                    for c in range(2):
                        act.wait_ge(sem("cv_ready"), A.due("cv_ready"))
                        act.activation(Fb[0][:], CA[0][:], ACT.Silu).then_inc(sem("cs2_ready"), 1)
                        act.wait_ge(sem("cs2_ready"), A.did("cs2_ready"))
                    for c in range(2):
                        act.wait_ge(*full(f"v{h}.{c}"))
                        ps = bank_of(f"v{h}.{c}")
                        if h and c == 0:
                            act.wait_ge(*full(f"mn{h - 1}.{NT - 1}"))
                        act.activation(V[:, :, c * P:(c + 1) * P], ps[:].rearrange("p (i c) -> p i c", i=NT),
                                              ACT.Copy).then_inc(taken(f"v{h}.{c}")[0], 1)
                    for x, n in enumerate((f"mq{h}", f"mk{h}")):
                        ps = take(n)
                        if h and x == 0:
                            act.wait_ge(*full(f"ms{h - 1}.{NT - 1}"))
                        act.activation(QK[:, x], ps[:], ACT.Copy, scale=[ML_DK ** -0.5, 1.0][x]).then_inc(taken(n)[0], 1)
                if h:
                    act.wait_ge(sem("rvar_ready"), A.due("rvar_ready"))
                    act.activation(sd[:], sd[:], ACT.Sqrt).then_inc(sem("sd_ready"), 1)
                    act.wait_ge(sem("sd_ready"), A.did("sd_ready"))
                if h < ML_H:
                    act.wait_ge(sem("nb_ready"), A.due("nb_ready", 1))
                    for j in range(NT):
                        n = S - j * P
                        if h or j >= 2:
                            act.wait_ge(sem("e_used"), A.due("e_used"))
                        if n > P:
                            act.activation(E[j % 2][:, P:n], NB[:, (j + 1) * P:S], ACT.Exp,
                                           bias=AEC[:, 0, j, h:h + 1])
                        act.activation(E[j % 2][:, 0:P], NBd[:, j, :], ACT.Exp, bias=AEC[:, 0, j, h:h + 1]).then_inc(sem("e_ready"), 1)
                        act.wait_ge(sem("e_ready"), A.did("e_ready"))
            if stop <= 5:
                return
            for n in range(DC):
                for x, (nm, fn, bias) in enumerate([("md", ACT.Copy, None), ("gv", ACT.Copy, None),
                                                    ("gg", ACT.Sigmoid, None)]):
                    ps = take(f"{nm}{n}")
                    if x == 0:
                        act.wait_ge(sem("g8_free"), A.due("g8_free"))
                    kw = {"bias": p_(bias, n)} if bias else {}
                    act.activation(G8[x][:], ps[:], fn, **kw).then_inc(taken(f"{nm}{n}")[0], 1)
            act.wait_ge(sem("g8_free"), A.due("g8_free"))
            for n in range(DC):
                back_out(f"mix{n}", G8[n % 2][:], scale=mod[:, 16 + n:17 + n],
                         wait=f"mix{n - 2}T" if n >= 2 else None)
            if stop <= 6:
                return
            for i in range(2):
                sqrt_sd()
            normed_out(3)
            for g, kg in enumerate(FF2_GROUPS):
                for j in range(kg):
                    ps = take(f"fv{g}.{j}")
                    if g or j:
                        act.wait_ge(sem("fb_done"), A.due("fb_done"))
                    act.activation(FV[:], ps[:], ACT.Copy).then_inc(taken(f"fv{g}.{j}")[0], 1)
                    ps = take(f"fg{g}.{j}")
                    act.activation(GP[:, 2:2 + S], ps[:], ACT.Copy).then_inc(taken(f"fg{g}.{j}")[0], 1)
                    act.wait_ge(sem("fc_ready"), A.due("fc_ready"))
                    act.activation(FG[:], FG[:], ACT.Gelu_apprx_tanh).then_inc(sem("fg_ready"), 1)
                    act.wait_ge(sem("fg_ready"), A.did("fg_ready"))
                for n in range(DC):
                    ps = take(f"fd{g}.{n}")
                    v = g * 8 + n
                    if v >= 2:
                        act.wait_ge(sem("fd_used"), v - 1)
                    act.activation(G8[v % 2][:], ps[:], ACT.Copy, scale=mod[:, 40 + n:41 + n]).then_inc(taken(f"fd{g}.{n}")[0], 1)
            sqrt_sd()

        @block.gpsimd
        def _(pool):
            last = {1: WIN[-1], 2: "wout7", 3: "dn3.7", 4: "gb7", 5: "mk3", 6: "mix7"}.get(stop)
            for t in range(min(NTILES, last_tile(INDEX[last]) + 2) if last else NTILES):
                pool.wait_ge(sem("hi_split"), t + 1)
                pool.tensor_tensor(wlo[t % 2][:], raw[t % RAW][:], rd(whi[t % 2][:]), ALU.subtract)\
                    .then_inc(sem("lo_split"), 1)

        @block.vector
        def _(dve):
            v = Count()
            tt, ts, stt = dve.tensor_tensor, dve.tensor_scalar, dve.scalar_tensor_tensor

            def stats(i, s, rms):
                for x in range(2):
                    dve.bn_stats(st6[:, x, :], X[:, i, x * S:(x + 1) * S]).then_inc(sem("dve_step"), 1)
                    dve.wait_ge(sem("dve_step"), v.did("dve_step"))
                dve.bn_aggr(mv[:, i, :], st6[:].rearrange("p a b -> p (a b)")).then_inc(sem("dve_step"), 1)
                dve.wait_ge(sem("dve_step"), v.did("dve_step"))

            def norm_rows(s, dst, signal=True):
                rms = s < 2
                for i in range(NT):
                    if s == 0:
                        dve.wait_ge(sem(f"x_in{i}"), 16)
                    stats(i, s, rms)
                if rms:
                    tt(sd[:], mv[:, :, 0], mv[:, :, 0], ALU.mult).then_inc(sem("dve_step"), 1)
                    dve.wait_ge(sem("dve_step"), v.did("dve_step"))
                    tt(sd[:], sd[:], mv[:, :, 1], ALU.add).then_inc(sem("dve_step"), 1)
                    dve.wait_ge(sem("dve_step"), v.did("dve_step"))
                    ts(sd[:], sd[:], RMS_EPS, None, ALU.add).then_inc(sem("var_ready"), 1)
                    dve.wait_ge(sem("var_ready"), v.did("var_ready"))
                else:
                    ts(sd[:], mv[:, :, 1], LN_EPS, None, ALU.add).then_inc(sem("var_ready"), 1)
                    dve.wait_ge(sem("var_ready"), v.did("var_ready"))
                dve.wait_ge(sem("sd_ready"), v.due("sd_ready"))
                dve.reciprocal(sd[:], sd[:]).then_inc(sem("dve_step"), 1)
                dve.wait_ge(sem("dve_step"), v.did("dve_step"))
                for i in range(NT):
                    if rms:
                        ins = ts(dst[:, i, :], X[:, i, :], sd[:, i:i + 1], None, ALU.mult)
                    else:
                        ins = ts(dst[:, i, :], X[:, i, :], mv[:, i, 0:1], sd[:, i:i + 1], ALU.subtract, ALU.mult)
                    if signal:
                        ins.then_inc(sem("norm_rows"), 1)
                        dve.wait_ge(sem("norm_rows"), v.did("norm_rows"))
                    else:
                        ins.then_inc(sem("dve_step"), 1)
                        dve.wait_ge(sem("dve_step"), v.did("dve_step"))

            def split_to(hi, lo, f, name):
                dve.tensor_copy(hi, f).then_inc(sem("dve_step"), 1)
                dve.wait_ge(sem("dve_step"), v.did("dve_step"))
                tt(lo, f, rd(hi), ALU.subtract).then_inc(sem(name), 1)
                dve.wait_ge(sem(name), v.did(name))

            def normed_in(s):
                for c in range(DC):
                    pool_, b, k = product[f"xT{s}.{c}"]
                    dve.wait_ge(sem(f"free_{pool_}{b}"), k)
                    dve.tensor_copy(Ahi[:, c], Fb[c % 2][:]).then_inc(sem("dve_step"), 1)
                    dve.wait_ge(sem("dve_step"), v.did("dve_step"))
                    tt(Alo[:, c], Fb[c % 2][:], rd(Ahi[:, c]), ALU.subtract).then_inc(sem("A_ready"), 1)
                    dve.wait_ge(sem("A_ready"), v.did("A_ready"))

            dve.wait_ge(sem("con_in"), v.due("con_in", 16))
            dve.wait_ge(sem("par_in"), v.due("par_in", 16))
            norm_rows(0, N)
            dve.sem_inc(sem("n0_done"), 1)
            normed_in(0)

            def rope_chunk(n, c):
                f = F4[c % 4]
                dst = {"k": K, "q": Q}.get(n[0]) if n[0] != "r" else (RQ if n[1] == "q" else RK)
                idx = {"kc": 0, "ks": 1, "kw": 2}.get(n, int(n[-1]) if n[-1].isdigit() else 0)
                o = dst[:, idx]
                dve.wait_ge(*full(f"rot_{n}"))
                ps = bank_of(f"rot_{n}")
                if n == ROPED[0]:
                    dve.wait_ge(sem("rope_tab"), v.due("rope_tab", 16))
                tt(o, f[:], rope[:, 0], ALU.mult).then_inc(sem("dve_step"), 1)
                dve.wait_ge(sem("dve_step"), v.did("dve_step"))
                tt(Fb[0][:], ps[:], rope[:, 1], ALU.mult).then_inc(taken(f"rot_{n}")[0], 1)
                dve.wait_ge(*taken(f"rot_{n}"))
                tt(o, o, Fb[0][:], ALU.add).then_inc(sem("roped"), 1)
                dve.wait_ge(sem("roped"), v.did("roped"))

            for c, n in enumerate(WIN + ["", ""]):
                if 1 <= c <= len(WIN) and WIN[c - 1] in NORMED:
                    m = WIN[c - 1]
                    dve.wait_ge(*taken(f"ssq_{m}"))
                    dve.reciprocal(RS[:], RS[:]).then_inc(sem("dve_step"), 1)
                    dve.wait_ge(sem("dve_step"), v.did("dve_step"))
                    w = p_("qn") if m[0] == "q" else p_("kn", ["kc", "ks", "kw"].index(m))
                    f = F4[(c - 1) % 4]
                    stt(f[:], f[:], w, RS[:], ALU.mult, ALU.mult).then_inc(sem("rope_in"), 1)
                    dve.wait_ge(sem("rope_in"), v.did("rope_in"))
                    dve.sem_inc(sem("rs_used"), 1)
                elif 1 <= c <= len(WIN) and WIN[c - 1] in ROPED:
                    dve.wait_ge(*taken(WIN[c - 1]))
                    dve.sem_inc(sem("rope_in"), 1)
                    v.did("rope_in")
                if c >= 2 and WIN[c - 2] in ROPED:
                    rope_chunk(WIN[c - 2], c - 2)

            if stop <= 1:
                return
            dve.wait_ge(sem("two_rows"), v.due("two_rows", 8 * 16))
            for w, (src, pe_) in enumerate(((kc2, "pek"), (vc2, "pev"))):
                view = src[:].rearrange("p g (n l) -> p l g n", l=16)
                for half in range(2):
                    for l in range(8):
                        lp = half * 8 + l
                        ts(kcp[w][:, lp], view[:, 2 * l, :, half:half + NCMP], p_(pe_, lp), None, ALU.add).then_inc(sem("dve_step"), 1)
                        dve.wait_ge(sem("dve_step"), v.did("dve_step"))
                dve.sem_inc(sem("cmp_in"), 1)
            dve.wait_ge(*taken("turn_rv3"))
            dve.sem_inc(sem("xfree"), 1)
            dve.sem_inc(sem("xfree_sp"), 1)
            dve.memset(KCM[:], 0.0).then_inc(sem("kcm_zero"), 1)
            dve.wait_ge(sem("kcm_zero"), v.did("kcm_zero"))
            dve.memset(VB[:], 0.0).then_inc(sem("vb_zero"), 1)
            dve.wait_ge(sem("vb_zero"), v.did("vb_zero"))
            dve.memset(HVr[:], 0.0).then_inc(sem("dve_step"), 1)
            dve.wait_ge(sem("dve_step"), v.did("dve_step"))
            dve.wait_ge(*taken("hid1.1"))
            for hc in range(2):
                for g in range(2):
                    for r in range(4):
                        dve.tensor_copy(HVr[:, hc, g, r, 0:NCMP], HK[1][:, hc, g, :]).then_inc(sem("dve_step"), 1)
                        dve.wait_ge(sem("dve_step"), v.did("dve_step"))
            dve.sem_inc(sem("hidv_ready"), 1)

            dve.wait_ge(sem("mask_in"), v.due("mask_in", 32))
            cm = masks[:, 1280:1536].rearrange("p (x i n) -> p x i n", x=2, i=NT)
            for i in range(NT):
                mb = cm[:, 0, i, :].unsqueeze(1).to_broadcast([P, HEADS, NCMP_PAD])
                m1 = cm[:, 1, i, :].unsqueeze(1).to_broadcast([P, HEADS, NCMP_PAD])
                for g in range(GROUPS):
                    dve.wait_ge(*full(f"cs{i}.{g}"))
                    ps = bank_of(f"cs{i}.{g}")
                    tt(cS[:, 4 * g:4 * g + 4], ps[:, 0:P].rearrange("p (h n) -> p h n", h=REP),
                              mb[:, 4 * g:4 * g + 4], ALU.add).then_inc(taken(f"cs{i}.{g}")[0], 1)
                    dve.wait_ge(*taken(f"cs{i}.{g}"))
                dve.tensor_reduce(m8[0][:], cS[:], AX, ALU.max).then_inc(sem("dve_step"), 1)
                dve.wait_ge(sem("dve_step"), v.did("dve_step"))
                tt(cS[:], cS[:], m8[0][:].unsqueeze(2).to_broadcast([P, HEADS, NCMP_PAD]), ALU.subtract).then_inc(sem("cs_ready"), 1)
                dve.wait_ge(sem("cs_ready"), v.did("cs_ready"))
                dve.wait_ge(sem("ce_ready"), v.due("ce_ready"))
                dve.tensor_reduce(m8[1][:], cP[:], AX, ALU.add).then_inc(sem("dve_step"), 1)
                dve.wait_ge(sem("dve_step"), v.did("dve_step"))
                dve.reciprocal(m8[2][:], m8[1][:]).then_inc(sem("dve_step"), 1)
                dve.wait_ge(sem("dve_step"), v.did("dve_step"))
                tt(m8[3][:], m8[2][:], GT[:, i, 0:8], ALU.mult).then_inc(sem("dve_step"), 1)
                dve.wait_ge(sem("dve_step"), v.did("dve_step"))
                tt(cP[:], cP[:], m1, ALU.mult).then_inc(sem("dve_step"), 1)
                dve.wait_ge(sem("dve_step"), v.did("dve_step"))
                tt(cP[:], cP[:], m8[3][:].unsqueeze(2).to_broadcast([P, HEADS, NCMP_PAD]), ALU.mult).then_inc(sem("cp_ready"), 1)
                dve.wait_ge(sem("cp_ready"), v.did("cp_ready"))
                dve.wait_ge(*full(f"co{i}"))
                ps = bank_of(f"co{i}")
                dve.tensor_copy(oacc[:, i, :], ps[:]).then_inc(taken(f"co{i}")[0], 1)
                dve.wait_ge(*taken(f"co{i}"))

            units = [(i, b, hh) for i in range(NT) for b in range(2) for hh in range(HEADS)]

            def score_max(u):
                i, b, hh = units[u]
                nk = i + 1 if b == 0 else min(i + 1, 3)
                n = nk * P
                dve.wait_ge(*full(f"s{u}"))
                ps = bank_of(f"s{u}")
                if u >= 2:
                    dve.wait_ge(sem("p_ready"), u - 1)
                m = masks[:, 384 - i * P:384 - i * P + n] if b == 0 else masks[:, 896 + 384 - n:896 + 384]
                dve.tensor_tensor_reduce(sS[u % 2][:, 0:n], ps[:, 0:n], m, 1.0, NEG, ALU.add, ALU.max,
                                                MX[:, u:u + 1]).then_inc(taken(f"s{u}")[0], 1)
                dve.wait_ge(*taken(f"s{u}"))
                ts(NM[:, u:u + 1], MX[:, u:u + 1], -DH ** -0.5, None, ALU.mult).then_inc(sem("s_ready"), 1)
                dve.wait_ge(sem("s_ready"), v.did("s_ready"))

            def combine(i, b):
                u0 = (i * 2 + b) * HEADS
                dve.wait_ge(*full(f"o{i}.{b}"))
                ps = bank_of(f"o{i}.{b}")
                dve.reciprocal(m8[0][:], SUM[:, u0:u0 + 8]).then_inc(sem("dve_step"), 1)
                dve.wait_ge(sem("dve_step"), v.did("dve_step"))
                tt(m8[1][:], m8[0][:], GT[:, i, 8 + 8 * b:16 + 8 * b], ALU.mult).then_inc(sem("dve_step"), 1)
                dve.wait_ge(sem("dve_step"), v.did("dve_step"))
                tt(tmp5[:].rearrange("p (h e) -> p h e", h=HEADS),
                          ps[:].rearrange("p (h e) -> p h e", h=HEADS),
                          m8[1][:].unsqueeze(2).to_broadcast([P, HEADS, DH]), ALU.mult).then_inc(taken(f"o{i}.{b}")[0], 1)
                dve.wait_ge(*taken(f"o{i}.{b}"))
                tt(oacc[:, i, :], oacc[:, i, :], tmp5[:], ALU.add).then_inc(sem("oacc_ready"), 1)
                dve.wait_ge(sem("oacc_ready"), v.did("oacc_ready"))
            for u in range(len(units) + 3):
                if u < len(units):
                    score_max(u)
                if u >= 3 and (u - 3) % HEADS == HEADS - 1:
                    i, b, _ = units[u - 3]
                    combine(i, b)
            for c in range(4):
                dve.wait_ge(*full(f"mixT{c}"))
                ps = bank_of(f"mixT{c}")
                dve.tensor_copy(Bhi[:, c], ps[:]).then_inc(sem("dve_step"), 1)
                dve.wait_ge(sem("dve_step"), v.did("dve_step"))
                tt(Blo[:, c], ps[:], rd(Bhi[:, c]), ALU.subtract).then_inc(taken(f"mixT{c}")[0], 1)
                dve.wait_ge(*taken(f"mixT{c}"))
                dve.sem_inc(sem("B_ready"), 1)
                v.did("B_ready")

            for h in range(RET_H):
                for j in range(NT):
                    dve.wait_ge(*full(f"rs{h}.{j}"))
                    ps = bank_of(f"rs{h}.{j}")
                    n = S - j * P
                    a = [0, 512, 896, 1152][j]
                    tt(RW[h % 2][:, a:a + n], ps[:, 0:n], decay[:, h, 0:n], ALU.mult).then_inc(taken(f"rs{h}.{j}")[0], 1)
                    dve.wait_ge(*taken(f"rs{h}.{j}"))
                    dve.sem_inc(sem("rw_ready"), 1)
                dve.wait_ge(*full(f"ry{h}"))
                ps = bank_of(f"ry{h}")
                for i in range(NT):
                    dve.bn_stats(st6[:, 0, :], ps[:, i * P:(i + 1) * P]).then_inc(sem("dve_step"), 1)
                    dve.wait_ge(sem("dve_step"), v.did("dve_step"))
                    dve.bn_aggr(mv[:, i, :], st6[:, 0, :]).then_inc(sem("dve_step"), 1)
                    dve.wait_ge(sem("dve_step"), v.did("dve_step"))
                ts(sd[:], mv[:, :, 1], RMS_EPS, None, ALU.add).then_inc(sem("rvar_ready"), 1)
                dve.wait_ge(sem("rvar_ready"), v.did("rvar_ready"))
                dve.wait_ge(sem("sd_ready"), v.due("sd_ready"))
                dve.reciprocal(sd[:], sd[:]).then_inc(sem("dve_step"), 1)
                dve.wait_ge(sem("dve_step"), v.did("dve_step"))
                for i in range(NT):
                    ins = ts(YN[:, i, :], ps[:, i * P:(i + 1) * P], mv[:, i, 0:1], sd[:, i:i + 1],
                             ALU.subtract, ALU.mult)
                    if i < NT - 1:
                        ins.then_inc(sem("dve_step"), 1)
                        dve.wait_ge(sem("dve_step"), v.did("dve_step"))
                    else:
                        ins.then_inc(taken(f"ry{h}")[0], 1)
                        dve.wait_ge(*taken(f"ry{h}"))
                dve.sem_inc(sem("yn_ready"), 1)
                dve.wait_ge(*full(f"mixT{4 + h}"))
                ps = bank_of(f"mixT{4 + h}")
                stt(Fb[0][:], ps[:], p_("retn", h), RG[:, h], ALU.mult, ALU.mult).then_inc(taken(f"mixT{4 + h}")[0], 1)
                dve.wait_ge(*taken(f"mixT{4 + h}"))
                split_to(Bhi[:, 4 + h], Blo[:, 4 + h], Fb[0][:], "B_ready")
            dve.sem_inc(sem("mix_done"), 1)

            def back_in(name, n, alpha=None):
                dve.wait_ge(*full(f"{name}T"))
                ps = bank_of(f"{name}T")
                x = X[:, :, n * P:(n + 1) * P]
                t = ps[:].rearrange("p (i c) -> p i c", i=NT)
                if alpha is None:
                    ins = tt(x, x, t, ALU.add)
                else:
                    ins = stt(x, x, alpha, t, ALU.mult, ALU.add)
                ins.then_inc(taken(f"{name}T")[0], 1)
                dve.wait_ge(*taken(f"{name}T"))

            dve.wait_ge(sem("x_again"), v.due("x_again", 64))
            for n in range(DC):
                back_in(f"wout{n}", n)
            if stop <= 2:
                dve.sem_inc(sem("x_final"), 1)
                return
            norm_rows(1, N)
            normed_in(1)
            ada = [0]

            def ada_tile():
                t = ada[0]
                if t == 48:
                    return
                ada[0] += 1
                dve.wait_ge(sem(f"ada_in{t % 3}"), 16 * (t // 3 + 1))
                dve.tensor_tensor_reduce(junk[:], adaw[t % 3][:], cB[:], 1.0, 0.0, ALU.mult, ALU.add,
                                                mod[:, t:t + 1]).then_inc(sem("ada_used"), 1)
                dve.wait_ge(sem("ada_used"), v.did("ada_used"))

            def c16(i):
                return s16[:, i]
            lre, lim = p_("lre", 0, 16), p_("lim", 0, 16)
            mag, si, co = c16(3), c16(4), c16(7)
            ar1, ai, den, zr, zi, t1, t2 = (c16(i) for i in range(9, 16))

            def s5_angles():
                dve.wait_ge(sem("s5_a"), v.due("s5_a"))
                tt(c16(1), lre, c16(0), ALU.mult).then_inc(sem("dve_step"), 1)
                dve.wait_ge(sem("dve_step"), v.did("dve_step"))
                tt(c16(2), lim, c16(0), ALU.mult).then_inc(sem("s5_d"), 1)
                dve.wait_ge(sem("s5_d"), v.did("s5_d"))
                ts(c16(8), c16(2), 1.0 / (2 * math.pi), ROUND, ALU.mult, ALU.add).then_inc(sem("dve_step"), 1)
                dve.wait_ge(sem("dve_step"), v.did("dve_step"))
                ts(c16(8), c16(8), ROUND, None, ALU.subtract).then_inc(sem("dve_step"), 1)
                dve.wait_ge(sem("dve_step"), v.did("dve_step"))
                c1 = 6.28125
                c2 = round((2 * math.pi - c1) * 2.0 ** 20) / 2.0 ** 20
                c3 = 2 * math.pi - c1 - c2
                for k in (c1, c2, c3):
                    stt(c16(2), c16(8), -k, c16(2), ALU.mult, ALU.add).then_inc(sem("dve_step"), 1)
                    dve.wait_ge(sem("dve_step"), v.did("dve_step"))
                ts(c16(5), c16(2), math.pi - 1e-6, -math.pi + 1e-6, ALU.min, ALU.max).then_inc(sem("dve_step"), 1)
                dve.wait_ge(sem("dve_step"), v.did("dve_step"))
                stt(c16(6), c16(5), -1.0, c16(5), ALU.mult, ALU.max).then_inc(sem("dve_step"), 1)
                dve.wait_ge(sem("dve_step"), v.did("dve_step"))
                ts(c16(6), c16(6), -1.0, math.pi / 2, ALU.mult, ALU.add).then_inc(sem("s5_d"), 1)
                dve.wait_ge(sem("s5_d"), v.did("s5_d"))

            def s5_factors():
                dve.wait_ge(sem("s5_a"), v.due("s5_a", 3))
                tt(ar1, mag, co, ALU.mult).then_inc(sem("dve_step"), 1)
                dve.wait_ge(sem("dve_step"), v.did("dve_step"))
                ts(ar1, ar1, 1.0, None, ALU.subtract).then_inc(sem("dve_step"), 1)
                dve.wait_ge(sem("dve_step"), v.did("dve_step"))
                tt(ai, mag, si, ALU.mult).then_inc(sem("dve_step"), 1)
                dve.wait_ge(sem("dve_step"), v.did("dve_step"))
                tt(den, lre, lre, ALU.mult).then_inc(sem("dve_step"), 1)
                dve.wait_ge(sem("dve_step"), v.did("dve_step"))
                tt(t1, lim, lim, ALU.mult).then_inc(sem("dve_step"), 1)
                dve.wait_ge(sem("dve_step"), v.did("dve_step"))
                tt(den, den, t1, ALU.add).then_inc(sem("dve_step"), 1)
                dve.wait_ge(sem("dve_step"), v.did("dve_step"))
                dve.reciprocal(den, den).then_inc(sem("dve_step"), 1)
                dve.wait_ge(sem("dve_step"), v.did("dve_step"))
                for z, (a, b_, op) in ((zr, (ar1, ai, ALU.add)), (zi, (ai, ar1, ALU.subtract))):
                    tt(t1, a, lre, ALU.mult).then_inc(sem("dve_step"), 1)
                    dve.wait_ge(sem("dve_step"), v.did("dve_step"))
                    tt(t2, b_, lim, ALU.mult).then_inc(sem("dve_step"), 1)
                    dve.wait_ge(sem("dve_step"), v.did("dve_step"))
                    tt(z, t1, t2, op).then_inc(sem("dve_step"), 1)
                    dve.wait_ge(sem("dve_step"), v.did("dve_step"))
                    tt(z, z, den, ALU.mult).then_inc(sem("dve_step"), 1)
                    dve.wait_ge(sem("dve_step"), v.did("dve_step"))
                dve.tensor_copy(pw[:, 0, 0], co).then_inc(sem("dve_step"), 1)
                dve.wait_ge(sem("dve_step"), v.did("dve_step"))
                dve.tensor_copy(pw[:, 0, 1], si).then_inc(sem("dve_step"), 1)
                dve.wait_ge(sem("dve_step"), v.did("dve_step"))
                for m in range(8):
                    tt(t1, pw[:, m, 0], pw[:, m, 0], ALU.mult).then_inc(sem("dve_step"), 1)
                    dve.wait_ge(sem("dve_step"), v.did("dve_step"))
                    tt(t2, pw[:, m, 1], pw[:, m, 1], ALU.mult).then_inc(sem("dve_step"), 1)
                    dve.wait_ge(sem("dve_step"), v.did("dve_step"))
                    tt(pw[:, m + 1, 0], t1, t2, ALU.subtract).then_inc(sem("dve_step"), 1)
                    dve.wait_ge(sem("dve_step"), v.did("dve_step"))
                    tt(t1, pw[:, m, 0], pw[:, m, 1], ALU.mult).then_inc(sem("dve_step"), 1)
                    dve.wait_ge(sem("dve_step"), v.did("dve_step"))
                    ts(pw[:, m + 1, 1], t1, 2.0, None, ALU.mult).then_inc(sem("dve_step"), 1)
                    dve.wait_ge(sem("dve_step"), v.did("dve_step"))
                sg = seg[:]
                dve.memset(sg[:, 0, :, 0], 1.0).then_inc(sem("dve_step"), 1)
                dve.wait_ge(sem("dve_step"), v.did("dve_step"))
                dve.memset(sg[:, 1, :, 0], 0.0).then_inc(sem("dve_step"), 1)
                dve.wait_ge(sem("dve_step"), v.did("dve_step"))
                for x in range(2):
                    dve.tensor_copy(sg[:, x, :, 1], pw[:, 7, x]).then_inc(sem("dve_step"), 1)
                    dve.wait_ge(sem("dve_step"), v.did("dve_step"))
                    dve.tensor_copy(sg[:, x, :, 2], pw[:, 8, x]).then_inc(sem("dve_step"), 1)
                    dve.wait_ge(sem("dve_step"), v.did("dve_step"))
                tt(t1, pw[:, 7, 0], pw[:, 8, 0], ALU.mult).then_inc(sem("dve_step"), 1)
                dve.wait_ge(sem("dve_step"), v.did("dve_step"))
                tt(t2, pw[:, 7, 1], pw[:, 8, 1], ALU.mult).then_inc(sem("dve_step"), 1)
                dve.wait_ge(sem("dve_step"), v.did("dve_step"))
                tt(sg[:, 0, :, 3], t1, t2, ALU.subtract).then_inc(sem("dve_step"), 1)
                dve.wait_ge(sem("dve_step"), v.did("dve_step"))
                tt(t1, pw[:, 7, 0], pw[:, 8, 1], ALU.mult).then_inc(sem("dve_step"), 1)
                dve.wait_ge(sem("dve_step"), v.did("dve_step"))
                tt(t2, pw[:, 7, 1], pw[:, 8, 0], ALU.mult).then_inc(sem("dve_step"), 1)
                dve.wait_ge(sem("dve_step"), v.did("dve_step"))
                tt(sg[:, 1, :, 3], t1, t2, ALU.add).then_inc(sem("dve_step"), 1)
                dve.wait_ge(sem("dve_step"), v.did("dve_step"))
                for x in range(2):
                    dve.memset(ring_step[x][:, :, 0], 1.0 - x).then_inc(sem("dve_step"), 1)
                    dve.wait_ge(sem("dve_step"), v.did("dve_step"))

            def s5_inputs():
                dve.wait_ge(sem("s5_in"), v.due("s5_in", 64))
                zrb, zib = (z.unsqueeze(2).to_broadcast([P, 16, 16]) for z in (zr, zi))
                b0, b1 = (junk[:, 256 * x:256 * x + 256].rearrange("p (a b) -> p a b", a=16) for x in range(2))
                tt(b0, bri[1][:], zib, ALU.mult).then_inc(sem("dve_step"), 1)
                dve.wait_ge(sem("dve_step"), v.did("dve_step"))
                tt(b1, bri[0][:], zib, ALU.mult).then_inc(sem("dve_step"), 1)
                dve.wait_ge(sem("dve_step"), v.did("dve_step"))
                tt(bri[0][:], bri[0][:], zrb, ALU.mult).then_inc(sem("dve_step"), 1)
                dve.wait_ge(sem("dve_step"), v.did("dve_step"))
                tt(bri[0][:], bri[0][:], b0, ALU.subtract).then_inc(sem("dve_step"), 1)
                dve.wait_ge(sem("dve_step"), v.did("dve_step"))
                tt(bri[1][:], bri[1][:], zrb, ALU.mult).then_inc(sem("dve_step"), 1)
                dve.wait_ge(sem("dve_step"), v.did("dve_step"))
                tt(bri[1][:], bri[1][:], b1, ALU.add).then_inc(sem("dve_step"), 1)
                dve.wait_ge(sem("dve_step"), v.did("dve_step"))

            def s5_double(e, k0, k1):
                w = 1 << e
                n = k1 - k0
                pc, ps_ = (pw[:, e, x, k0:k1].unsqueeze(2).to_broadcast([P, n, w]) for x in range(2))
                c_old, s_old = (ring_step[x][:, k0:k1, 0:w] for x in range(2))
                c_new, s_new = (ring_step[x][:, k0:k1, w:2 * w] for x in range(2))
                a, b = (dbl[x][:, k0:k1, 0:w] for x in range(2))
                tt(a, s_old, ps_, ALU.mult).then_inc(sem("dve_step"), 1)
                dve.wait_ge(sem("dve_step"), v.did("dve_step"))
                tt(b, c_old, ps_, ALU.mult).then_inc(sem("dve_step"), 1)
                dve.wait_ge(sem("dve_step"), v.did("dve_step"))
                tt(c_new, c_old, pc, ALU.mult).then_inc(sem("dve_step"), 1)
                dve.wait_ge(sem("dve_step"), v.did("dve_step"))
                tt(c_new, c_new, a, ALU.subtract).then_inc(sem("dve_step"), 1)
                dve.wait_ge(sem("dve_step"), v.did("dve_step"))
                tt(s_new, s_old, pc, ALU.mult).then_inc(sem("dve_step"), 1)
                dve.wait_ge(sem("dve_step"), v.did("dve_step"))
                tt(s_new, s_new, b, ALU.add).then_inc(sem("dve_step"), 1)
                dve.wait_ge(sem("dve_step"), v.did("dve_step"))

            def s5_piece(n):
                if n == 1:
                    s5_angles()
                elif n == 5:
                    s5_factors()
                elif n == 6:
                    s5_inputs()
                elif 8 <= n < 14:
                    s5_double(n - 8, 0, 16)
                elif 14 <= n < 16:
                    s5_double(6, 8 * n - 112, 8 * n - 104)

            dve.wait_ge(sem("cB_ready"), v.due("cB_ready"))
            for g, kg in enumerate(FF1_GROUPS):
                for j in range(kg):
                    dve.wait_ge(*taken(f"up{g}.{j}"))
                    r = G4[2 + (g * 8 + j) % 2]
                    tt(r[:], r[:], r[:], ALU.mult).then_inc(sem("dve_step"), 1)
                    dve.wait_ge(sem("dve_step"), v.did("dve_step"))
                    dve.tensor_copy(Bhi[:, j], r[:]).then_inc(sem("dve_step"), 1)
                    dve.wait_ge(sem("dve_step"), v.did("dve_step"))
                    tt(Blo[:, j], r[:], rd(Bhi[:, j]), ALU.subtract).then_inc(sem("B_ready"), 1)
                    dve.wait_ge(sem("B_ready"), v.did("B_ready"))
                    dve.sem_inc(sem("up_used"), 1)
                    ada_tile()
                for n in range(DC):
                    dve.wait_ge(*taken(f"dn{g}.{n}"))
                    f = G4[(g * 8 + n) % 2]
                    if g == 0:
                        ins = dve.tensor_copy(Y[:, n], f[:])
                    else:
                        ins = tt(Y[:, n], Y[:, n], f[:], ALU.add)
                    ins.then_inc(sem("dn_used"), 1)
                    dve.wait_ge(sem("dn_used"), v.did("dn_used"))
                    ada_tile()
                    s5_piece(g * 8 + n)
                    if g == 3:
                        if n:
                            back_in(f"dn{n - 1}", n - 1)
            back_in(f"dn{DC - 1}", DC - 1)
            dve.sem_inc(sem("ff1_done"), 1)
            tt(mod[:], mod[:], p_("bada", 0, 48), ALU.add).then_inc(sem("dve_step"), 1)
            dve.wait_ge(sem("dve_step"), v.did("dve_step"))
            for a in (8, 16, 32, 40):
                ts(mod[:, a:a + 8], mod[:, a:a + 8], 1.0, None, ALU.add).then_inc(sem("dve_step"), 1)
                dve.wait_ge(sem("dve_step"), v.did("dve_step"))
            dve.sem_inc(sem("mod_ready"), 1)
            if stop <= 3:
                dve.sem_inc(sem("x_final"), 1)
                return
            norm_rows(2, N)
            normed_in(2)

            for x in range(2):
                dve.memset(BT[x][:], 0.0).then_inc(sem("dve_step"), 1)
                dve.wait_ge(sem("dve_step"), v.did("dve_step"))
                dve.memset(CT[x][:], 0.0).then_inc(sem("dve_step"), 1)
                dve.wait_ge(sem("dve_step"), v.did("dve_step"))
                for m in range(4):
                    for p2 in range(2):
                        rows, a = slice(64 * p2, 64 * p2 + 64), 32 * m + 16 * p2
                        dve.tensor_copy(BT[x][rows, m::4, a:a + 16], bri[x][rows, m::4, :]).then_inc(sem("dve_step"), 1)
                        dve.wait_ge(sem("dve_step"), v.did("dve_step"))
            dve.sem_inc(sem("bb_ready"), 1)
            for x in range(2):
                dve.wait_ge(*full(f"cT{x}"))
                ps = bank_of(f"cT{x}")
                pv = ps[:].rearrange("p (c n) -> p c n", c=4)
                for m in range(4):
                    for p2 in range(2):
                        rows, a = slice(64 * p2, 64 * p2 + 64), 32 * m + 16 * p2
                        ins = ts(CT[x][rows, m::4, a:a + 16], pv[rows, :, a:a + 16], [1.0, -1.0][x], None, ALU.mult)
                        if (m, p2) == (3, 1):
                            ins.then_inc(taken(f"cT{x}")[0], 1)
                            dve.wait_ge(*taken(f"cT{x}"))
                        else:
                            ins.then_inc(sem("dve_step"), 1)
                            dve.wait_ge(sem("dve_step"), v.did("dve_step"))
            for x in range(2):
                for q in range(4):
                    dve.wait_ge(*full(f"bt{x}.{q}"))
                    ps = bank_of(f"bt{x}.{q}")
                    dve.tensor_copy(BT[x][:, 4 * q:4 * q + 4, :].rearrange("p a b -> p (a b)"), ps[:]).then_inc(taken(f"bt{x}.{q}")[0], 1)
                    dve.wait_ge(*taken(f"bt{x}.{q}"))
            dve.sem_inc(sem("bt_ready"), 1)
            dve.sem_inc(sem("bt_ready"), 1)
            C, SN, ta, tb, zr_, zi_ = y8[1], y8[2], y8[3], y8[4], y8[5], y8[6]

            def s5_out(cc):
                dve.wait_ge(*full(f"s5y{cc}"))
                ps = bank_of(f"s5y{cc}")
                stt(U[:, cc], U[:, cc], p_("s5d", cc), ps[:], ALU.mult, ALU.add).then_inc(taken(f"s5y{cc}")[0], 1)
                dve.wait_ge(*taken(f"s5y{cc}"))
                dve.sem_inc(sem("s5f_ready"), 1)

            for k in range(S5_CHUNKS):
                cc, m = divmod(k, 4)
                C4, S4, a4, b4 = (t[:].rearrange("p (s t) -> p s t", s=4) for t in (C, SN, ta, tb))
                gc, gs = (seg[:, x, k, :].unsqueeze(2).to_broadcast([P, 4, P]) for x in range(2))
                c1, s1 = (ring_step[x][:, k, :].unsqueeze(1).to_broadcast([P, 4, P]) for x in range(2))
                tt(a4, gs, s1, ALU.mult).then_inc(sem("dve_step"), 1)
                dve.wait_ge(sem("dve_step"), v.did("dve_step"))
                tt(C4, gc, c1, ALU.mult).then_inc(sem("dve_step"), 1)
                dve.wait_ge(sem("dve_step"), v.did("dve_step"))
                tt(C4, C4, a4, ALU.subtract).then_inc(sem("dve_step"), 1)
                dve.wait_ge(sem("dve_step"), v.did("dve_step"))
                tt(b4, gs, c1, ALU.mult).then_inc(sem("dve_step"), 1)
                dve.wait_ge(sem("dve_step"), v.did("dve_step"))
                tt(S4, gc, s1, ALU.mult).then_inc(sem("dve_step"), 1)
                dve.wait_ge(sem("dve_step"), v.did("dve_step"))
                tt(S4, S4, b4, ALU.add).then_inc(sem("dve_step"), 1)
                dve.wait_ge(sem("dve_step"), v.did("dve_step"))
                dve.wait_ge(*full(f"bu0.{k}"))
                dve.wait_ge(*full(f"bu1.{k}"))
                br, bi = bank_of(f"bu0.{k}"), bank_of(f"bu1.{k}")
                tt(ta[:], br[:], C[:], ALU.mult).then_inc(sem("dve_step"), 1)
                dve.wait_ge(sem("dve_step"), v.did("dve_step"))
                tt(tb[:], bi[:], SN[:], ALU.mult).then_inc(sem("dve_step"), 1)
                dve.wait_ge(sem("dve_step"), v.did("dve_step"))
                tt(ta[:], ta[:], tb[:], ALU.add).then_inc(sem("dve_step"), 1)
                dve.wait_ge(sem("dve_step"), v.did("dve_step"))
                dve.tensor_tensor_scan(zr_[:], c16(3)[:, k:k + 1].to_broadcast([P, S]), ta[:], 0.0,
                                              ALU.mult, ALU.add).then_inc(sem("dve_step"), 1)
                dve.wait_ge(sem("dve_step"), v.did("dve_step"))
                tt(tb[:], bi[:], C[:], ALU.mult).then_inc(taken(f"bu1.{k}")[0], 1)
                dve.wait_ge(*taken(f"bu1.{k}"))
                tt(ta[:], br[:], SN[:], ALU.mult).then_inc(taken(f"bu0.{k}")[0], 1)
                dve.wait_ge(*taken(f"bu0.{k}"))
                tt(ta[:], tb[:], ta[:], ALU.subtract).then_inc(sem("dve_step"), 1)
                dve.wait_ge(sem("dve_step"), v.did("dve_step"))
                dve.tensor_tensor_scan(zi_[:], c16(3)[:, k:k + 1].to_broadcast([P, S]), ta[:], 0.0,
                                              ALU.mult, ALU.add).then_inc(sem("dve_step"), 1)
                dve.wait_ge(sem("dve_step"), v.did("dve_step"))
                if k:
                    if k % 4 == 0:
                        dve.wait_ge(*full(f"s5y{cc - 1}"))
                    else:
                        dve.wait_ge(sem("xs_used"), v.due("xs_used"))
                tt(ta[:], zr_[:], C[:], ALU.mult).then_inc(sem("dve_step"), 1)
                dve.wait_ge(sem("dve_step"), v.did("dve_step"))
                tt(tb[:], zi_[:], SN[:], ALU.mult).then_inc(sem("dve_step"), 1)
                dve.wait_ge(sem("dve_step"), v.did("dve_step"))
                tt(xx[0][:], ta[:], tb[:], ALU.subtract).then_inc(sem("dve_step"), 1)
                dve.wait_ge(sem("dve_step"), v.did("dve_step"))
                tt(ta[:], zr_[:], SN[:], ALU.mult).then_inc(sem("dve_step"), 1)
                dve.wait_ge(sem("dve_step"), v.did("dve_step"))
                tt(tb[:], zi_[:], C[:], ALU.mult).then_inc(sem("dve_step"), 1)
                dve.wait_ge(sem("dve_step"), v.did("dve_step"))
                tt(xx[1][:], ta[:], tb[:], ALU.add).then_inc(sem("xs_ready"), 1)
                dve.wait_ge(sem("xs_ready"), v.did("xs_ready"))
                if k % 4 == 0 and k:
                    s5_out(cc - 1)
                if k % 4 == 2 and k > 4:
                    dve.wait_ge(sem("s5g_ready"), v.due("s5g_ready"))
                    split_to(YShi[:, cc - 1], YSlo[:, cc - 1], Fb[0][:], "ys_ready")
            s5_out(3)
            dve.wait_ge(sem("s5g_ready"), v.due("s5g_ready"))
            split_to(YShi[:, 3], YSlo[:, 3], Fb[0][:], "ys_ready")
            if stop <= 4:
                return

            dve.wait_ge(*taken("if"))
            f_, g_ = IF[32:36, :], ifr[0][32:36, :]
            stt(g_, f_, -1.0, f_, ALU.mult, ALU.max).then_inc(sem("if_d"), 1)
            dve.wait_ge(sem("if_d"), v.did("if_d"))
            dve.wait_ge(sem("if_a"), v.due("if_a"))
            ts(ifr[1][32:36, :], f_, 0.0, None, ALU.min).then_inc(sem("dve_step"), 1)
            dve.wait_ge(sem("dve_step"), v.did("dve_step"))
            tt(ifr[2][32:36, :], ifr[1][32:36, :], g_, ALU.subtract).then_inc(sem("dve_step"), 1)
            dve.wait_ge(sem("dve_step"), v.did("dve_step"))
            dve.memset(dd[32:36, 2:3], 1.0).then_inc(sem("dve_step"), 1)
            dve.wait_ge(sem("dve_step"), v.did("dve_step"))
            dve.tensor_tensor_scan(ifr[3][32:36, :], dd[32:36, 2:3].to_broadcast([4, S]), ifr[2][32:36, :],
                                          0.0, ALU.mult, ALU.add).then_inc(sem("if_d"), 1)
            dve.wait_ge(sem("if_d"), v.did("if_d"))
            dve.wait_ge(sem("if_a"), v.due("if_a"))
            tt(ifr[2][0:4, :], IF[0:4, :], ifr[1][0:4, :], ALU.subtract).then_inc(sem("dve_step"), 1)
            dve.wait_ge(sem("dve_step"), v.did("dve_step"))
            dve.tensor_tensor_scan(ifr[0][0:4, :], ifr[2][0:4, :], ifr[2][0:4, :], 0.0, ALU.max, ALU.max).then_inc(sem("dve_step"), 1)
            dve.wait_ge(sem("dve_step"), v.did("dve_step"))
            stt(ifr[1][0:4, :], ifr[1][0:4, :], -1.0, ifr[0][0:4, :], ALU.mult, ALU.subtract).then_inc(sem("dve_step"), 1)
            dve.wait_ge(sem("dve_step"), v.did("dve_step"))
            dve.sem_inc(sem("if_d"), 1)
            ts(negM[0:4, :], ifr[0][0:4, :], -1.0, None, ALU.mult).then_inc(sem("negM_ready"), 1)
            dve.wait_ge(sem("negM_ready"), v.did("negM_ready"))
            dve.wait_ge(*full(SPILLED[-1]))
            dve.memset(XM[0][:, :, 0:3], 0.0).then_inc(sem("dve_step"), 1)
            dve.wait_ge(sem("dve_step"), v.did("dve_step"))
            dve.memset(XM[1][:, :, 0:3], 0.0).then_inc(sem("xm_zero"), 1)
            dve.wait_ge(sem("xm_zero"), v.did("xm_zero"))
            dve.wait_ge(*taken("aec"))
            dve.memset(V[:, :, ML_DV:ML_DV + 1], 1.0).then_inc(sem("dve_step"), 1)
            dve.wait_ge(sem("dve_step"), v.did("dve_step"))

            def values_out(h):
                for i in range(NT):
                    dve.wait_ge(*full(f"mn{h}.{i}"))
                    ps = bank_of(f"mn{h}.{i}")
                    ts(dd[:, 5:6], ps[:, ML_DV:ML_DV + 1], -1.0, AEC[:, 1, i, h:h + 1], ALU.mult, ALU.max).then_inc(sem("dve_step"), 1)
                    dve.wait_ge(sem("dve_step"), v.did("dve_step"))
                    tt(dd[:, 3:4], dd[:, 5:6], ps[:, ML_DV:ML_DV + 1], ALU.max).then_inc(sem("dve_step"), 1)
                    dve.wait_ge(sem("dve_step"), v.did("dve_step"))
                    dve.reciprocal(dd[:, 4:5], dd[:, 3:4]).then_inc(sem("dve_step"), 1)
                    dve.wait_ge(sem("dve_step"), v.did("dve_step"))
                    if h and i == 0:
                        dve.wait_ge(*full(f"hT{h - 1}.1"))
                    ts(H[:, i, :], ps[:, 0:ML_DV], dd[:, 4:5], None, ALU.mult).then_inc(taken(f"mn{h}.{i}")[0], 1)
                    dve.wait_ge(*taken(f"mn{h}.{i}"))
                    dve.bn_stats(st6[:, 0, :], H[:, i, :]).then_inc(sem("dve_step"), 1)
                    dve.wait_ge(sem("dve_step"), v.did("dve_step"))
                    dve.bn_aggr(mv[:, i, :], st6[:, 0, :]).then_inc(sem("dve_step"), 1)
                    dve.wait_ge(sem("dve_step"), v.did("dve_step"))
                ts(sd[:], mv[:, :, 1], LN_EPS, None, ALU.add).then_inc(sem("rvar_ready"), 1)
                dve.wait_ge(sem("rvar_ready"), v.did("rvar_ready"))
                dve.wait_ge(sem("sd_ready"), v.due("sd_ready"))
                dve.reciprocal(sd[:], sd[:]).then_inc(sem("dve_step"), 1)
                dve.wait_ge(sem("dve_step"), v.did("dve_step"))
                for i in range(NT):
                    ts(H[:, i, :], H[:, i, :], mv[:, i, 0:1], sd[:, i:i + 1], ALU.subtract, ALU.mult).then_inc(sem("hn_ready"), 1)
                    dve.wait_ge(sem("hn_ready"), v.did("hn_ready"))

            def head_out(h):
                dve.wait_ge(sem(f"so_in{h % 2}"), v.due(f"so_in{h % 2}", 32))
                for c in range(2):
                    k = 2 * h + c
                    dve.wait_ge(*full(f"hT{h}.{c}"))
                    ps = bank_of(f"hT{h}.{c}")
                    stt(Fb[1][:], ps[:], p_("mg", k), SO[:, h % 2, c], ALU.mult, ALU.mult).then_inc(taken(f"hT{h}.{c}")[0], 1)
                    dve.wait_ge(*taken(f"hT{h}.{c}"))
                    split_to(Bhi[:, k], Blo[:, k], Fb[1][:], "B_ready")
                dve.sem_inc(sem("so_used"), 1)

            for h in range(ML_H):
                dve.wait_ge(sem(f"xm_in{h % 2}"), 32 * (h // 2 + 1))
                for c in range(2):
                    k = 2 * h + c
                    a = CA[0]
                    ts(a[:], XM[h % 2][:, c, 0:S], p_("cw", 4 * k), p_("cb", k), ALU.mult, ALU.add).then_inc(sem("dve_step"), 1)
                    dve.wait_ge(sem("dve_step"), v.did("dve_step"))
                    for t in range(1, 4):
                        stt(a[:], XM[h % 2][:, c, t:t + S], p_("cw", 4 * k + t), a[:], ALU.mult, ALU.add).then_inc(sem("dve_step"), 1)
                        dve.wait_ge(sem("dve_step"), v.did("dve_step"))
                    dve.sem_inc(sem("cv_ready"), 1)
                    dve.wait_ge(sem("cs2_ready"), v.due("cs2_ready"))
                    if h and c == 0:
                        dve.wait_ge(*full(f"mk{h - 1}"))
                    split_to(XCh[:, c], XCl[:, c], Fb[0][:], "xc_ready")
                dve.sem_inc(sem("conv_done"), 1)
                dve.wait_ge(*full(f"nb{h}"))
                ps = bank_of(f"nb{h}")
                dve.tensor_copy(NB[:], ps[:]).then_inc(sem("dve_step"), 1)
                dve.wait_ge(sem("dve_step"), v.did("dve_step"))
                tt(NBd[:], ps[:].rearrange("p (i c) -> p i c", i=NT),
                          c_("tri").unsqueeze(1).to_broadcast([P, NT, P]), ALU.add).then_inc(taken(f"nb{h}")[0], 1)
                dve.wait_ge(*taken(f"nb{h}"))
                dve.sem_inc(sem("nb_ready"), 1)
                if h:
                    values_out(h - 1)
                for j in range(NT):
                    n = S - j * P
                    a = [0, 512, 896, 1152][j]
                    dve.wait_ge(*full(f"ms{h}.{j}"))
                    ps = bank_of(f"ms{h}.{j}")
                    dve.wait_ge(sem("e_ready"), v.due("e_ready"))
                    tt(W[:, a:a + n], ps[:, 0:n], E[j % 2][:, 0:n], ALU.mult).then_inc(taken(f"ms{h}.{j}")[0], 1)
                    dve.wait_ge(*taken(f"ms{h}.{j}"))
                    dve.sem_inc(sem("mw_ready"), 1)
                    if h < ML_H - 1 or j < NT - 2:
                        dve.sem_inc(sem("e_used"), 1)
                if h:
                    head_out(h - 1)
            values_out(ML_H - 1)
            head_out(ML_H - 1)
            if stop <= 5:
                return
            dve.sem_inc(sem("heads_done"), 1)
            dve.sem_inc(sem("g8_free"), 1)
            for n in range(DC):
                dve.wait_ge(*taken(f"gg{n}"))
                dve.wait_ge(sem(f"gates_in{n % 3}"), 32 * (n // 3 + 1))
                tt(Y[:, n], G8[0][:], gates[:, n % 3, 0], ALU.mult).then_inc(sem("dve_step"), 1)
                dve.wait_ge(sem("dve_step"), v.did("dve_step"))
                tt(G8[1][:], G8[1][:], G8[2][:], ALU.mult).then_inc(sem("dve_step"), 1)
                dve.wait_ge(sem("dve_step"), v.did("dve_step"))
                tt(G8[1][:], G8[1][:], gates[:, n % 3, 1], ALU.mult).then_inc(sem("dve_step"), 1)
                dve.wait_ge(sem("dve_step"), v.did("dve_step"))
                tt(Y[:, n], Y[:, n], G8[1][:], ALU.add).then_inc(sem("dve_step"), 1)
                dve.wait_ge(sem("dve_step"), v.did("dve_step"))
                dve.sem_inc(sem("g8_free"), 1)
                split_to(Ahi[:, n], Alo[:, n], Y[:, n], "A_ready")
            for n in range(DC):
                back_in(f"mix{n}", n, ALPHA)
            if stop <= 6:
                dve.sem_inc(sem("x_final"), 1)
                return

            def layer_norm(x):
                norm_rows(3, X, signal=False)
                dve.wait_ge(sem("gb_in"), v.due("gb_in", 32))
                for i in range(NT):
                    tt(X[:, i, :], X[:, i, :], GB[:, 0], ALU.mult).then_inc(sem("dve_step"), 1)
                    dve.wait_ge(sem("dve_step"), v.did("dve_step"))
                    tt(X[:, i, :], X[:, i, :], GB[:, 1], ALU.add).then_inc(sem("x_final"), 1)
                    dve.wait_ge(sem("x_final"), v.did("x_final"))
                if not x:
                    dve.sem_inc(sem("gb_used"), 1)
            layer_norm(0)
            norm_rows(3, N)
            normed_in(3)
            dve.memset(GP[:, 0:2], 0.0).then_inc(sem("dve_step"), 1)
            dve.wait_ge(sem("dve_step"), v.did("dve_step"))
            for g, kg in enumerate(FF2_GROUPS):
                for j in range(kg):
                    k = g * 8 + j
                    dve.wait_ge(*taken(f"fg{g}.{j}"))
                    ts(FG[:], GP[:, 0:S], p_("fcw", 3 * k), p_("fcb", k), ALU.mult, ALU.add).then_inc(sem("dve_step"), 1)
                    dve.wait_ge(sem("dve_step"), v.did("dve_step"))
                    stt(FG[:], GP[:, 1:1 + S], p_("fcw", 3 * k + 1), FG[:], ALU.mult, ALU.add).then_inc(sem("dve_step"), 1)
                    dve.wait_ge(sem("dve_step"), v.did("dve_step"))
                    stt(FG[:], GP[:, 2:2 + S], p_("fcw", 3 * k + 2), FG[:], ALU.mult, ALU.add).then_inc(sem("fc_ready"), 1)
                    dve.wait_ge(sem("fc_ready"), v.did("fc_ready"))
                    dve.wait_ge(sem("fg_ready"), v.due("fg_ready"))
                    tt(FG[:], FG[:], FV[:], ALU.mult).then_inc(sem("dve_step"), 1)
                    dve.wait_ge(sem("dve_step"), v.did("dve_step"))
                    split_to(Bhi[:, j], Blo[:, j], FG[:], "B_ready")
                    dve.sem_inc(sem("fb_done"), 1)
                for n in range(DC):
                    dve.wait_ge(*taken(f"fd{g}.{n}"))
                    f = G8[(g * 8 + n) % 2]
                    if g == 0:
                        ins = dve.tensor_copy(Y[:, n], f[:])
                    else:
                        ins = tt(Y[:, n], Y[:, n], f[:], ALU.add)
                    ins.then_inc(sem("fd_used"), 1)
                    dve.wait_ge(sem("fd_used"), v.did("fd_used"))
                    if g == 2:
                        if n:
                            back_in(f"fd{n - 1}", n - 1, ALPHA)
            back_in(f"fd{DC - 1}", DC - 1, ALPHA)
            layer_norm(1)

        @block.sync
        def _(sp):
            L = Count()

            def tiles(a, b):
                for t in range(a, b):
                    if t >= RAW:
                        sp.wait_ge(sem("lo_split"), t - RAW + 1)
                    sp.dma_start(raw[t % RAW][:], d["ws"][t]).then_inc(sem(f"raw_in{t % RAW}"), 16)

            def at_chunk(name):
                return FIRST_BLOCK[INDEX[name]] // TILE_BLOCKS
            xv = d["x"].rearrange("(i p) n -> i p n", p=P)
            for i in range(NT):
                sp.dma_start(X[:, i, :], xv[i]).then_inc(sem(f"x_in{i}"), 16)
            sp.dma_start(con[:], d["con"]).then_inc(sem("con_in"), 16)
            sp.dma_start(par[:], d["par"]).then_inc(sem("par_in"), 16)
            tiles(0, 2)
            for w, nm in enumerate(("w1k", "w1v")):
                sp.dma_start(w1[w][:], d[nm].rearrange("p (a b) -> p a b", a=16)).then_inc(sem("w1_in"), 16)
            sp.wait_ge(sem("n0_done"), L.due("n0_done"))
            sp.dma_start(rope[:], d["rope"].rearrange("p (a b) -> p a b", a=2)).then_inc(sem("rope_tab"), 16)
            n_win = last_tile(INDEX[WIN[-1]]) + 2
            tiles(2, n_win)

            def store(each):
                ov = out.rearrange("(i p) n -> i p n", p=P)
                for i in range(NT):
                    if each or i == 0:
                        sp.wait_ge(sem("x_final"), L.due("x_final", 1 + NT if each and i == 0 else 1))
                    sp.dma_start(ov[i], X[:, i, :]).then_inc(sem("out_done"), 16)
                sp.wait_ge(sem("out_done"), 64)

            sp.wait_ge(*full(WIN[-1]))
            sp.dma_start(masks[:], d["masks"]).then_inc(sem("mask_in"), 16)
            sp.dma_start(decay[:], d["decay"].rearrange("p (a b) -> p a b", a=4)).then_inc(sem("mask_in"), 16)
            sp.wait_ge(sem("xfree_sp"), L.due("xfree_sp"))
            sp.dma_start(w2k[:], d["w2k"].rearrange("p (a b) -> p a b", a=2)).then_inc(sem("w1_in"), 16)
            sp.dma_start(w2v[:], d["w2v"].rearrange("p (a b) -> p a b", a=2)).then_inc(sem("w1_in"), 16)
            sp.wait_ge(sem("mix_done"), L.due("mix_done"))
            for i in range(NT):
                sp.dma_start(X[:, i, :], xv[i]).then_inc(sem("x_again"), 16)
            n_out = last_tile(INDEX["wout7"]) + 2
            tiles(n_win, n_out)
            if stop <= 2:
                store(False)
                return
            sp.dma_start(cB[:], d["c"].partition_broadcast(P)).then_inc(sem("cB_in"), 16)
            for x in range(2):
                sp.dma_start(bri[x][:], d[["bre", "bim"][x]].rearrange("p (a b) -> p a b", a=16))\
                  .then_inc(sem("s5_in"), 16)
                sp.dma_start(cri[x][:], d[["cre", "cim"][x]].rearrange("p (a b) -> p a b", a=4))\
                  .then_inc(sem("s5_in"), 16)
            for t in range(48):
                if t >= 3:
                    sp.wait_ge(sem("ada_used"), t - 2)
                sp.dma_start(adaw[t % 3][:], d["ada"][t // 2][:, t % 2 * D:(t % 2 + 1) * D])\
                  .then_inc(sem(f"ada_in{t % 3}"), 16)
                if t % 2:
                    tiles(n_out + t // 2, n_out + t // 2 + 1)
            n_ff1 = last_tile(INDEX["dn3.7"]) + 2
            tiles(n_out + 24, n_ff1)
            if stop <= 3:
                store(False)
                return
            n_s5 = last_tile(INDEX[SPILLED[-1]]) + 2
            tiles(n_ff1, n_s5)

            def whole_spill():
                for x in range(3):
                    sp.wait_ge(sem(f"spilled{x}"), 16 * len(range(x, len(SPILLED), 3)))

            sp.wait_ge(*full(SPILLED[-1]))
            sp.wait_ge(sem("xm_zero"), L.due("xm_zero"))
            whole_spill()
            for h in range(ML_H):
                if h >= 2:
                    sp.wait_ge(sem("conv_done"), L.due("conv_done", 2 if h == 2 else 1))
                    sp.wait_ge(*taken(f"v{h - 2}.1"))
                for c in range(2):
                    sp.dma_start(XM[h % 2][:, c, 3:3 + S], spill[SPILLED.index(f"xm{2 * h + c}")])\
                      .then_inc(sem(f"xm_in{h % 2}"), 16)
                if h >= 2:
                    sp.wait_ge(sem("so_used"), L.due("so_used"))
                for c in range(2):
                    sp.dma_start(SO[:, h % 2, c], spill[SPILLED.index(f"om{2 * h + c}")])\
                      .then_inc(sem(f"so_in{h % 2}"), 16)
                if h >= 1:
                    tiles(n_s5 + h - 1, n_s5 + h)
            n_heads = n_s5 + 3
            if stop <= 5:
                return
            sp.wait_ge(sem("heads_done"), L.due("heads_done"))
            for x, nm in enumerate(("ln1g", "ln1b")):
                sp.dma_start(GB[:, x], d[nm].partition_broadcast(P)).then_inc(sem("gb_in"), 16)
            n_mix = last_tile(INDEX["mix7"]) + 2
            for n in range(DC):
                if n >= 3:
                    sp.wait_ge(sem("g8_free"), n - 1)
                for x, nm in enumerate(("ga", "gb")):
                    sp.dma_start(gates[:, n % 3, x], spill[SPILLED.index(f"{nm}{n}")])\
                      .then_inc(sem(f"gates_in{n % 3}"), 16)
                tiles(n_heads + n, n_heads + n + 1)
            tiles(n_heads + DC, n_mix)
            if stop <= 6:
                store(False)
                return
            sp.wait_ge(sem("gb_used"), L.due("gb_used"))
            for x, nm in enumerate(("ln2g", "ln2b")):
                sp.dma_start(GB[:, x], d[nm].partition_broadcast(P)).then_inc(sem("gb_in"), 16)
            tiles(n_mix, NTILES)
            store(True)


def stream_weights(w):
    sizes = [512] + [128] * 6 + [24, 256, 256, 512, 512]
    off = np.concatenate([[0], np.cumsum(sizes)])
    part = {n: w["w_in"][:, off[i]:off[i + 1]] for i, n in enumerate(
        ["q", "kc", "vc", "ks", "vs", "kw", "vw", "gate", "rq", "rk", "rv", "rg"])}
    w2 = w["w_in_2"]
    part2 = {"xm": w2[:, 0:1024], "om": w2[:, 1024:2048], "us": w2[:, 2056:2568], "ga": w2[:, 2568:3592],
             "gb": w2[:, 3592:4616]}

    def cols(a, n):
        return a[:, n * P:(n + 1) * P]

    def of(name):
        head, _, rest_ = name.partition(".")
        if name in ("kc", "vc", "ks", "kw", "vs", "vw"):
            return part[name]
        if name[0] == "q":
            r = int(name[1])
            q = part["q"].reshape(D, GROUPS, REP, DH)[:, :, r]
            return q.reshape(D, P)
        if name == "gate":
            return np.concatenate([part["gate"], np.zeros((D, P - 24), np.float32)], 1)
        if name[:2] in ("rq", "rk", "rv", "rg"):
            return cols(part[name[:2]], int(name[2]))
        if name[:4] == "wout":
            return cols(w["w_out"], int(name[4]))
        if name[:2] == "up":
            return cols(w["w_up"], 8 * int(head[2:]) + int(rest_))
        if name[:2] == "dn":
            g = int(head[2:])
            return cols(w["w_down"][g * 1024:(g + 1) * 1024], int(rest_))
        if name == "if":
            z = np.zeros((D, P), np.float32)
            z[:, 0:4], z[:, 32:36] = w2[:, 2048:2052], w2[:, 2052:2056]
            return z
        if name[:2] in part2:
            return cols(part2[name[:2]], int(name[2:]))
        if name[:2] == "mq":
            return w["w_mlstm_q_2"][int(name[2])]
        if name[:2] == "mk":
            return w["w_mlstm_k_2"][int(name[2])]
        if name[:2] == "md":
            return cols(w["w_mlstm_down_2"], int(name[2]))
        if name[:2] == "gv":
            return cols(w["w_s5_glu_2"], int(name[2]))
        if name[:2] == "gg":
            return cols(w["w_s5_glu_2"], 8 + int(name[2]))
        if name[:3] == "mix":
            return cols(w["w_mix_out_2"], int(name[3]))
        if name[:2] == "fv":
            return cols(w["w_ffn_up_2"], 8 * int(head[2:]) + int(rest_))
        if name[:2] == "fg":
            return cols(w["w_ffn_up_2"], 22 + 8 * int(head[2:]) + int(rest_))
        g = int(head[2:])
        return cols(w["w_ffn_down_2"][g * 1024:(g + 1) * 1024], int(rest_))

    blocks = []
    for name, kn in CHUNKS:
        a = of(name)
        assert a.shape == (kn * P, P), (name, a.shape)
        blocks.append(a.reshape(kn, P, P))
    b = np.concatenate(blocks, 0).reshape(NTILES, TILE_BLOCKS, P, P)
    return np.ascontiguousarray(b.transpose(0, 2, 1, 3).reshape(NTILES, P, TILE_COLS))


def lay_out(inputs):
    w = {k: np.asarray(a) for k, a in inputs.items()}
    flat = ("x",)
    w = {k: (a[0] if a.ndim > 1 else a) for k, a in w.items()}
    bin2 = w["b_in_2"]

    def col(a):
        return a.reshape(-1, P).T

    def states(a):
        return a.reshape(S5_CHUNKS, P).T
    bif = np.zeros(P, np.float32)
    bif[0:4], bif[32:36] = bin2[2048:2052], bin2[2052:2056]
    cols = {
        "ln1": col(w["ln1_w"]), "qn": np.concatenate([w["q_norm_w"]] * 2)[:, None],
        "kn": np.concatenate([w["k_norm_w"]] * 2, 1).T, "retn": w["ret_norm_w"].T, "ln2": col(w["ln2_w"]),
        "pek": w["cmp_pe_k"].reshape(16, P).T, "pev": w["cmp_pe_v"].reshape(16, P).T,
        "b_us": col(bin2[2056:2568]), "b_if": bif[:, None], "b_xm": col(bin2[0:1024]),
        "b_om": col(bin2[1024:2048]), "b_ga": col(bin2[2568:3592]), "b_gb": col(bin2[3592:4616]),
        "cw": w["w_mlstm_conv_2"].reshape(4, 8, P).transpose(2, 1, 0).reshape(P, 32),
        "cb": col(w["b_mlstm_conv_2"]), "mg": col(w["mlstm_norm_gain_2"]),
        "lre": states(w["s5_lam_re_2"]), "lim": states(w["s5_lam_im_2"]),
        "ldt": states(np.repeat(w["s5_log_dt_2"], 64)), "s5d": col(w["s5_d_2"]),
        "fcw": w["w_ffn_conv_2"].reshape(3, 22, P).transpose(2, 1, 0).reshape(P, 66),
        "fcb": col(w["b_ffn_conv_2"]), "bada": col(w["b_ada_2"]),
    }
    par = np.concatenate([cols[n] for n in PAR], 1)
    assert par.shape == (P, NPAR)

    def tall(a, k):
        return a.reshape(k, P, -1).transpose(1, 0, 2).reshape(P, -1)

    def c_dup(a):
        a = tall(a.reshape(512, 64), 4).reshape(P, 4, 64)
        return np.concatenate([a, a], 2).reshape(P, 512)
    out = {
        "x": w["x"], "ws": stream_weights(w), "par": par,
        "ada": np.ascontiguousarray(w["w_ada_2"].T).reshape(24, 2, P, D).transpose(0, 2, 1, 3).reshape(24, P, 2 * D),
        "c": w["c_2"], "w1k": tall(w["cmp_wk1"], 16), "w1v": tall(w["cmp_wv1"], 16),
        "w2k": np.concatenate([w["cmp_wk2"].reshape(2, P, DH)] * 2, 2).transpose(1, 0, 2).reshape(P, 2 * P),
        "w2v": tall(w["cmp_wv2"], 2),
        "bre": w["s5_b_re_2"].reshape(16, P, 16).transpose(1, 0, 2).reshape(P, 256),
        "bim": w["s5_b_im_2"].reshape(16, P, 16).transpose(1, 0, 2).reshape(P, 256),
        "cre": c_dup(w["s5_c_re_2"]), "cim": c_dup(w["s5_c_im_2"]),
        "ln1g": w["ln1_gain_2"], "ln1b": w["ln1_bias_2"], "ln2g": w["ln2_gain_2"], "ln2b": w["ln2_bias_2"],
    }
    out.update({k: a.astype(np.float32) for k, a in constants().items()})
    return {k: np.ascontiguousarray(a) for k, a in out.items()}


def kernel(**inputs):
    import concourse.bacc as bacc
    from concourse.bass_utils import run_bass_kernel_spmd

    arrays = lay_out(inputs)
    nc = bacc.Bacc("TRN2", target_bir_lowering=False, num_devices=1)
    d = {k: nc.dram_tensor(f"in_{k}", a.shape, F32, kind="ExternalInput").ap() for k, a in arrays.items()}
    out = nc.dram_tensor("out_x", (S, D), F32, kind="ExternalOutput").ap()
    build(nc, d, out)
    r = run_bass_kernel_spmd(nc, [{f"in_{k}": a for k, a in arrays.items()}], core_ids=[0])
    return r.results[0]["out_x"].reshape(1, S, D)
```

```python
import math
from contextlib import ExitStack

import numpy as np

import concourse.bass as bass
from concourse import mybir

F32 = mybir.dt.float32
F32R = mybir.dt.float32r
ALU = mybir.AluOpType
ACT = mybir.ActivationFunctionType
AX = mybir.AxisListType.X

P = 128
S = 512
NT = S // P
D = 1024
DC = D // P
TILE_BLOCKS = 16
TILE_COLS = TILE_BLOCKS * P

HEADS, GROUPS, REP, DH = 8, 2, 4, 64
NCMP, NCMP_PAD, CMP_HID = 31, 32, 256
RET_H, RET_DK, RET_DV = 4, 64, 128
FF1_GROUPS = [8, 8, 8, 8]
ML_H, ML_DK, ML_DV = 4, 128, 256
S5_CHUNKS = 16
FF2_GROUPS = [8, 8, 6]
ALPHA = 2.0 ** 0.25
RMS_EPS, LN_EPS = 1e-6, 1e-5
NEG = -1.0e30
ROUND = 12582912.0

WIN = (["kc", "vc", "q0", "q1", "q2", "q3", "ks", "kw", "vs", "vw", "gate", "rq0", "rq1", "rk0", "rk1"]
       + [f"rv{i}" for i in range(4)] + [f"rg{i}" for i in range(4)])
NORMED = [n for n in WIN if n in ("kc", "ks", "kw") or (n[0] == "q" and n != "gate")]
ROPED = [n for n in WIN if n in NORMED or n[:2] in ("rq", "rk")]
TURNED = [n for n in WIN if n in ("vs", "vw", "gate") or n[:2] == "rv"]


SPILLED = [f"{nm}{n}" for nm in ("xm", "om", "ga", "gb") for n in range(DC)]


def plan_chunks():
    ch = [(n, 8) for n in WIN] + [(f"wout{n}", 8) for n in range(DC)]
    for g, kg in enumerate(FF1_GROUPS):
        ch += [(f"up{g}.{j}", 8) for j in range(kg)] + [(f"dn{g}.{n}", kg) for n in range(DC)]
    ch += [(f"us{c}", 8) for c in range(4)] + [("if", 8)]
    ch += [(n, 8) for n in SPILLED]
    for h in range(ML_H):
        ch += [(f"mq{h}", 2), (f"mk{h}", 2)]
    for n in range(DC):
        ch += [(f"gv{n}", 4), (f"gg{n}", 4), (f"md{n}", 8)]
    ch += [(f"mix{n}", 8) for n in range(DC)]
    for g, kg in enumerate(FF2_GROUPS):
        for j in range(kg):
            ch += [(f"fv{g}.{j}", 8), (f"fg{g}.{j}", 8)]
        ch += [(f"fd{g}.{n}", kg) for n in range(DC)]
    return ch


CHUNKS = plan_chunks()
INDEX = {name: g for g, (name, _) in enumerate(CHUNKS)}
FIRST_BLOCK = np.concatenate([[0], np.cumsum([k for _, k in CHUNKS])]).tolist()
NTILES = FIRST_BLOCK[-1] // TILE_BLOCKS
assert FIRST_BLOCK[-1] % TILE_BLOCKS == 0


def last_tile(g):
    return (FIRST_BLOCK[g + 1] - 1) // TILE_BLOCKS


def last_chunk_of_tile(t):
    b = TILE_BLOCKS * (t + 1) - 1
    return next(g for g in range(len(CHUNKS)) if FIRST_BLOCK[g] <= b < FIRST_BLOCK[g + 1])


PAR = {}
for _name, _n in [("ln1", 8), ("qn", 1), ("kn", 3), ("retn", 4), ("ln2", 8), ("pek", 16), ("pev", 16),
                  ("b_us", 4), ("b_if", 1), ("b_xm", 8), ("b_om", 8), ("b_ga", 8), ("b_gb", 8),
                  ("cw", 32), ("cb", 8), ("mg", 8), ("lre", 16), ("lim", 16), ("ldt", 16), ("s5d", 4),
                  ("fcw", 66), ("fcb", 22), ("bada", 48)]:
    PAR[_name] = (sum(v[1] for v in PAR.values()), _n)
NPAR = sum(v[1] for v in PAR.values())

CON = {}
for _name, _n in [("ident", 128), ("mean64", 128), ("rot", 128), ("tri", 128), ("sel", 512),
                  ("eps", 2)]:
    CON[_name] = (sum(v[1] for v in CON.values()), _n)
NCON = sum(v[1] for v in CON.values())


def constants():
    p = np.arange(P)
    con = np.zeros((P, NCON), np.float64)

    def put(name, a):
        con[:a.shape[0], CON[name][0]:CON[name][0] + a.shape[1]] = a
    put("ident", np.eye(P))
    put("mean64", (p[:, None] // 64 == p[None, :] // 64) / 64.0)
    rot = np.zeros((P, P))
    for m in range(P):
        rot[m + 32 if m % 64 < 32 else m - 32, m] = -1.0 if m % 64 < 32 else 1.0
    put("rot", rot)
    put("tri", np.where(p[None, :] >= p[:, None], 0.0, NEG))
    sel = np.zeros((4, 4, P))
    for h in range(4):
        sel[h, h] = 1.0
    put("sel", sel.reshape(4, 512))
    put("eps", np.tile([[RMS_EPS, LN_EPS]], (P, 1)))
    inv = np.float32(10000.0) ** (-np.arange(32, dtype=np.float32) / np.float32(32))
    ang = (np.arange(S, dtype=np.float32)[:, None] * inv[None, :]).astype(np.float64).T
    rope = np.stack([np.tile(np.cos(ang), (4, 1)), np.tile(np.sin(ang), (4, 1))], 1)
    causal = np.where(np.arange(896)[None, :] - 384 <= p[:, None], 0.0, NEG)
    c = np.arange(384)[None, :]
    window = np.where((c <= p[:, None] + 256) & (c > p[:, None]), 0.0, NEG)
    tok = np.arange(NT)[None, :, None] * P + p[:, None, None]
    n = np.arange(NCMP_PAD)[None, None, :]
    ok = (n * 16 + 31 <= tok) & (n < NCMP)
    cmp_mask = np.stack([np.where(ok, 0.0, NEG), ok * 1.0], 1)
    gamma = 1.0 - 2.0 ** (-5.0 - np.arange(RET_H))
    d = np.arange(S)[None, None, :] - p[:, None, None]
    decay = np.where(d >= 0, gamma[None, :, None] ** np.maximum(d, 0), 0.0) * RET_DK ** -0.5
    masks = np.concatenate([causal, window, cmp_mask.reshape(P, -1)], 1)
    return {"con": con, "rope": rope.reshape(P, 1024), "masks": masks, "decay": decay.reshape(P, 2048)}


def build(nc, d, out, stop=99):
    ctx = ExitStack()
    with ctx:
        sems = {}

        def sem(name):
            if name not in sems:
                sems[name] = ctx.enter_context(nc.semaphore(name))
            return sems[name]

        base = [16512]

        def region(nbytes):
            at = base[0]
            base[0] += nbytes
            assert base[0] <= 229344, base[0]
            return at

        def at(name, shape, off, dt=F32):
            return nc.alloc_sbuf_tensor_at(name, shape, dt, offset=off)

        def new(name, shape, dt=F32):
            n = 4 * int(np.prod(shape[1:]))
            return at(name, shape, region((n + 31) // 32 * 32), dt)

        RAW = 2
        raw = [new(f"raw{i}", [P, TILE_COLS]) for i in range(RAW)]
        whi = [new(f"whi{i}", [P, TILE_COLS], F32R) for i in range(2)]
        wlo = [new(f"wlo{i}", [P, TILE_COLS], F32R) for i in range(2)]
        offA = region(32768)
        Ahi, Alo = at("Ahi", [P, 8, S], offA, F32R), at("Alo", [P, 8, S], offA + 16384, F32R)
        offB = region(32768)
        Bhi, Blo = at("Bhi", [P, 8, S], offB, F32R), at("Blo", [P, 8, S], offB + 16384, F32R)
        offX = region(16384)
        X = at("X", [P, NT, D], offX)
        offY = region(16384)
        Y = at("Y", [P, DC, S], offY)
        N = at("N", [P, NT, D], offY)
        con = new("con", [P, NCON])
        par = new("par", [P, NPAR])
        mod = new("mod", [P, 48])
        st6 = new("st6", [P, 2, 6])
        st4 = new("st4", [P, NT, 4, 6])
        nmr = new("nmr", [P, NT])
        mv = new("mv", [P, NT, 2])
        sd = new("sd", [P, NT])
        dd = new("dd", [P, 8])
        AEC = new("AEC", [P, 2, NT, 4])
        offF = base[0]
        Fb = [new(f"F{i}", [P, S]) for i in range(2)]
        offR = base[0]
        room = 229344 - offR

        def c_(name, rows=P):
            a, n = CON[name]
            return con[0:rows, a:a + n]

        def p_(name, i=0, n=1, rows=P):
            a = PAR[name][0] + i
            return par[0:rows, a:a + n]

        ident = c_("ident")
        eps = {"rms": con[:, CON["eps"][0]:CON["eps"][0] + 1], "ln": con[:, CON["eps"][0] + 1:CON["eps"][0] + 2]}

        cur = [offR]

        def rest(name, shape, dt=F32):
            n = 4 * int(np.prod(shape[1:]))
            t = at(name, shape, cur[0], dt)
            cur[0] += (n + 31) // 32 * 32
            assert cur[0] <= 229344, (name, cur[0])
            return t

        Q = rest("Q", [P, 4, S])
        K = rest("K", [P, 3, S])
        RQ = rest("RQ", [P, 2, S])
        RK = rest("RK", [P, 2, S])
        RG = rest("RG", [P, 4, S])
        VT = rest("VT", [P, 2, NT, P])
        RV = rest("RV", [P, NT, 4, P])
        VC = rest("VC", [P, S])
        GT = rest("GT", [P, NT, 24])
        F4 = [at(f"F4{i}", [P, S], offX + 2048 * i) for i in range(4)]
        SQ = at("SQ", [P, S], offX + 8192)
        RS = at("RS", [P, S], offX + 10240)
        rope = at("rope", [P, 2, S], offX + 12288)
        w1 = [at("w1k", [P, 16, CMP_HID], offB), at("w1v", [P, 16, CMP_HID], offB + 16384)]
        kc2 = at("kc2", [P, 2, S], offY)
        vc2 = at("vc2", [P, 2, S], offY + 4096)
        kcp = [at("kcp", [P, 16, 2, NCMP], offY + 8192), at("vcp", [P, 16, 2, NCMP], offY + 8192 + 3968)]
        o = offX
        cS = [at(f"cS{i}", [P, HEADS, NCMP_PAD], o + 1024 * i) for i in range(2)]
        cP = [at(f"cP{i}", [P, HEADS, NCMP_PAD], o + 2048 + 1024 * i) for i in range(2)]
        cT = at("cT", [P, NT, 2, P], o + 4096)
        HK = [at("HK", [P, 2, 2, NCMP], o + 8192), at("HV", [P, 2, 2, NCMP], o + 8704)]
        HS = [at(f"HS{i}", [P, CMP_HID], o + 1024 * i) for i in range(2)]
        HVr = at("HVr", [P, 2, 2, 4, NCMP_PAD], o + 9216)
        KCM = at("KCM", [P, 2, NCMP_PAD], o + 11264)
        VB = at("VB", [P, 2, REP, DH], offY)
        w2k = at("w2k", [P, 2, P], o + 12288)
        w2v = at("w2v", [P, 2, DH], o + 13312)
        SUM = at("SUM", [P, 64], o + 13824)
        MX = at("MX", [P, 64], o + 14080)
        NM = at("NM", [P, 64], o + 14336)
        m8 = [at(f"m8{i}", [P, 8], o + 14592 + 32 * i) for i in range(4)]
        o = offA
        masks = at("masks", [P, 1536], o)
        decay = at("decay", [P, 4, S], o + 6144)
        sS = [at(f"sS{i}", [P, S], o + 14336 + 2048 * i) for i in range(3)]
        Pr = [at(f"Pr{i}", [P, S], o + 20480 + 2048 * i) for i in range(3)]
        PT = [at(f"PT{i}", [P, NT, P], o + 26624 + 2048 * i) for i in range(3)]
        RW = [at(f"RW{i}", [P, 1280], o + 14336 + 5120 * i) for i in range(2)]
        YN = at("YN", [P, NT, P], o + 14336 + 10240)

        cur[0] = offR
        adaw = [rest(f"adaw{i}", [P, D]) for i in range(3)]
        cB = rest("cB", [P, D])
        offJ = cur[0]
        junk = rest("junk", [P, D])
        G4 = [rest(f"G4{i}", [P, S]) for i in range(4)]
        ring_step = [rest("cos_t", [P, 16, P]), rest("sin_t", [P, 16, P])]
        s16 = rest("s16", [P, 20, 16])
        pw = rest("pw", [P, 9, 2, 16])
        seg = rest("seg", [P, 2, 16, 4])
        offBC = cur[0]
        bri = [rest("bre", [P, 16, 16]), rest("bim", [P, 16, 16])]
        cri = [rest("cre", [P, 4, P]), rest("cim", [P, 4, P])]
        stage = [at(f"stage{i}", [P, S], offBC + 2048 * i) for i in range(3)]
        dbl = [at("dbl0", [P, 16, 64], offJ), at("dbl1", [P, 16, 64], offF)]

        cur[0] = offR
        YShi, YSlo = rest("YShi", [P, 4, S], F32R), rest("YSlo", [P, 4, S], F32R)
        offU = cur[0]
        U = rest("U", [P, 4, S])
        BT = [at("BTr", [P, S5_CHUNKS, P], offB), at("BTi", [P, S5_CHUNKS, P], offB + 8192)]
        CT = [at("CTr", [P, S5_CHUNKS, P], offB + 16384), at("CTi", [P, S5_CHUNKS, P], offB + 24576)]
        y8 = [at(f"y8{i}", [P, S], offY + 2048 * i) for i in range(8)]
        xx = [rest(f"xx{i}", [P, S]) for i in range(2)]
        assert cur[0] <= offJ + 12288
        IF = at("IF", [P, S], offY)
        gr = [at("gr", [P, S], offY + 14336), Fb[1]]
        cur[0] = offU
        XM = [at(f"XM{i}", [P, 2, S + 3], offA + 4160 * i) for i in range(2)]
        SO = at("SO", [P, 2, 2, S], offA + 8320)
        XCh, XCl = rest("XCh", [P, 2, S], F32R), rest("XCl", [P, 2, S], F32R)
        QK = rest("QK", [P, 2, S])
        V = rest("V", [P, NT, ML_DV + 1])
        W = rest("W", [P, 1280])
        cur2 = [offY + 2048]

        def iny(name, shape):
            n = 4 * int(np.prod(shape[1:]))
            t = at(name, shape, cur2[0])
            cur2[0] += (n + 31) // 32 * 32
            assert cur2[0] <= offY + 16384, name
            return t
        negM = IF
        NBd = iny("NBd", [P, NT, P])
        H = iny("H", [P, NT, ML_DV])
        E = [rest(f"E{i}", [P, 1280]) for i in range(2)]
        CA = rest("CA", [P, 2, S])
        cur[0] = offU
        G8 = [rest(f"G8{i}", [P, S]) for i in range(3)]
        gates = rest("gates", [P, 3, 2, S])
        GB = rest("GB", [P, 2, D])
        GP = rest("GP", [P, S + 2])
        FV = rest("FV", [P, S])
        FG = rest("FG", [P, S])

        banks = [ctx.enter_context(nc.psum_tensor(f"bank{i}", [P, S], F32)) for i in range(8)]
        TRI = [0, 512, 896, 1152]
        pools = {"G": banks[0:2], "T": banks[2:6], "O": banks[6:8]}
        used = {k: 0 for k in pools}
        product = {}

        def rd(t):
            return t.bitcast(F32)

        spill = nc.dram_tensor("spill", (len(SPILLED), P, S), F32, kind="Internal").ap()
        UNITS = [(i, hh, b) for i in range(NT) for hh in range(HEADS) for b in range(2)]

        def keys(i, b):
            nk = i + 1 if b == 0 else min(i + 1, 3)
            return i + 1 - nk, nk

        def values_done(u):
            if u % (2 * HEADS) == 2 * HEADS - 1:
                return full(f"o{UNITS[u][0]}")
            return sem("pv_done"), u + 1 - u // (2 * HEADS)

        block = ctx.enter_context(nc.Block())

        def full(name):
            pool, b, k = product[name]
            return sem(f"full_{pool}{b}"), k

        def taken(name):
            pool, b, k = product[name]
            return sem(f"free_{pool}{b}"), k

        def bank_of(name):
            pool, b, _ = product[name]
            return pools[pool][b]

        class Count:

            def __init__(self):
                self.given, self.waited = {}, {}

            def did(self, name):
                self.given[name] = self.given.get(name, 0) + 1
                return self.given[name]

            def due(self, name, k=1):
                self.waited[name] = self.waited.get(name, 0) + k
                return self.waited[name]

        @block.tensor
        def _(pe):
            T = Count()

            def bank(pool):
                n = used[pool]
                b, k = n % len(pools[pool]), n // len(pools[pool])
                if k:
                    pe.wait_ge(sem(f"free_{pool}{b}"), k)
                used[pool] += 1
                return pools[pool][b], (pool, b, k + 1)

            def done(ins, name, where):
                ins.then_inc(sem(f"full_{where[0]}{where[1]}"), 1)
                product[name] = where

            def gemm(name, hi, lo, before=None):
                g = INDEX[name]
                kn = CHUNKS[g][1]
                ps, where = bank("G")
                for k in range(kn):
                    b = FIRST_BLOCK[g] + k
                    t, c = b // TILE_BLOCKS, b % TILE_BLOCKS
                    if c == 0:
                        pe.wait_ge(sem("lo_split"), t + 1)
                    if before:
                        pe.wait_ge(sem(before), T.due(before))
                    wh, wl = (w[t % 2][:, c * P:(c + 1) * P] for w in (whi, wlo))
                    pe.matmul(ps[:], wh, hi[:, k], start=(k == 0), stop=False)
                    pe.matmul(ps[:], wh, lo[:, k], start=False, stop=False)
                    ins = pe.matmul(ps[:], wl, hi[:, k], start=False, stop=(k == kn - 1))
                done(ins, name, where)

            def turn(name, srcs, pool="T", width=P, rows=P, cols=P):
                ps, where = bank(pool)
                for i, s in enumerate(srcs):
                    ins = pe.transpose(ps[0:cols, i * width:i * width + rows], s, ident[0:rows, 0:rows])
                done(ins, name, where)

            def normed_in(s):
                pe.wait_ge(sem("norm_rows"), T.due("norm_rows", 2))
                pe.wait_ge(sem("norm_rows_a"), T.due("norm_rows_a", 2))
                for c in range(DC):
                    turn(f"xT{s}.{c}", [N[:, i, c * P:(c + 1) * P] for i in range(NT)])

            pe.wait_ge(sem("con_in"), T.due("con_in", 16))
            normed_in(0)

            def post1(n, c):
                if n in NORMED:
                    pe.wait_ge(*taken(n))
                    ps, where = bank("T")
                    done(pe.matmul(ps[:], c_("mean64"), SQ[:], start=True, stop=True), f"ssq_{n}", where)
                elif n in TURNED:
                    pe.wait_ge(*taken(n))
                    if n == "gate":
                        turn_gate(n, c)
                    else:
                        turn(f"turn_{n}", [F4[c % 4][:, i * P:(i + 1) * P] for i in range(NT)])

            def turn_gate(n, c):
                ps, where = bank("T")
                for i in range(NT):
                    ins = pe.transpose(ps[:, i * 24:(i + 1) * 24], F4[c % 4][0:24, i * P:(i + 1) * P],
                                       ident[0:24, 0:24])
                done(ins, f"turn_{n}", where)

            def post2(n, c):
                if n in ROPED:
                    pe.wait_ge(sem("rope_in"), T.due("rope_in"))
                    ps, where = bank("T")
                    done(pe.matmul(ps[:], c_("rot"), F4[c % 4][:], start=True, stop=True), f"rot_{n}", where)

            for c, n in enumerate(WIN):
                gemm(n, Ahi, Alo, "A_ready" if c == 0 else None)
                if c >= 1:
                    post1(WIN[c - 1], c - 1)
                if c >= 2:
                    post2(WIN[c - 2], c - 2)

            if stop <= 1:
                return
            pe.wait_ge(sem("w1_in"), T.due("w1_in", 32))
            for w in range(2):
                pe.wait_ge(sem("cmp_in"), T.due("cmp_in"))
                ps, where = bank("T")
                for l in range(16):
                    ins = pe.matmul(ps[0:2 * NCMP, 0:CMP_HID], kcp[w][:, l].rearrange("p a b -> p (a b)"),
                                    w1[w][:, l, :], start=(l == 0), stop=(l == 15))
                done(ins, f"hid{w}", where)
                if w:
                    pe.wait_ge(*taken("hid0"))
                    turn("hidT0", [HS[0][0:2 * NCMP, hc * P:(hc + 1) * P] for hc in range(2)], width=64,
                         rows=2 * NCMP)
            pe.wait_ge(*taken("hid1"))
            turn("hidT1", [HS[1][0:2 * NCMP, hc * P:(hc + 1) * P] for hc in range(2)], width=64, rows=2 * NCMP)
            pe.wait_ge(sem("w1_in"), T.due("w1_in", 32))
            pe.wait_ge(*taken("hidT0"))
            ps, where = bank("T")
            for hc in range(2):
                ins = pe.matmul(ps[:, 0:2 * NCMP], w2k[:, hc, :], HK[0][:, hc].rearrange("p a b -> p (a b)"),
                                start=(hc == 0), stop=(hc == 1))
            done(ins, "kcmp", where)
            pe.wait_ge(sem("hidv_ready"), T.due("hidv_ready"))
            ps, where = bank("T")
            for g in range(GROUPS):
                for hc in range(2):
                    ins = pe.matmul(ps[:, g * DH:(g + 1) * DH], HVr[:, hc, g].rearrange("p a b -> p (a b)"),
                                    w2v[:, hc, :], start=(hc == 0), stop=(hc == 1))
            done(ins, "vcmp", where)
            pe.wait_ge(*taken("kcmp"))
            pe.wait_ge(*taken("vcmp"))

            for i in range(NT + 2):
                if i < NT:
                    for g in range(GROUPS):
                        ps, where = bank("T")
                        for r in range(REP):
                            ins = pe.matmul(ps[:, r * NCMP_PAD:(r + 1) * NCMP_PAD],
                                            Q[64 * g:64 * g + 64, r, i * P:(i + 1) * P],
                                            KCM[64 * g:64 * g + 64, g, :], start=True, stop=True)
                        done(ins, f"cs{i}.{g}", where)
                if i >= 2:
                    pe.wait_ge(sem("cp_ready"), T.due("cp_ready"))
                    turn(f"ct{i - 2}", [cP[i % 2][:, 4 * g:4 * g + 4, :].rearrange("p a b -> p (a b)")
                                        for g in range(2)], "G")

            def scores(u):
                i, hh, b = UNITS[u]
                g, r = divmod(hh, REP)
                k0, nk = keys(i, b)
                ps, where = bank("G")
                done(pe.matmul(ps[:, 0:nk * P], Q[64 * g:64 * g + 64, r, i * P:(i + 1) * P],
                               K[64 * g:64 * g + 64, 1 + b, k0 * P:(k0 + nk) * P], start=True, stop=True),
                     f"s{u}", where)

            def probs(u):
                i, hh, b = UNITS[u]
                pe.wait_ge(sem("p_ready"), T.due("p_ready"))
                turn(f"pt{u}", [Pr[u % 3][:, j * P:(j + 1) * P] for j in range(keys(i, b)[1])])

            obank = {}

            def values(u):
                i, hh, b = UNITS[u]
                g, r = divmod(hh, REP)
                k0, nk = keys(i, b)
                pe.wait_ge(*taken(f"pt{u}"))
                if hh == 0 and b == 0:
                    obank[0], obank[1] = bank("O")
                rows = slice(64 * (hh % 2), 64 * (hh % 2) + 64)
                o = obank[0][rows, hh // 2 * P:(hh // 2 + 1) * P]
                if b == 0:
                    pe.wait_ge(*taken(f"ct{i}"))
                    pe.matmul(o, VB[:, g, r, :], cT[:, i, g, :], start=True, stop=False)
                for j in range(nk):
                    ins = pe.matmul(o, VT[:, b, k0 + j, g * DH:(g + 1) * DH], PT[u % 3][:, j, :],
                                    start=False, stop=(b == 1 and j == nk - 1))
                if hh == HEADS - 1 and b == 1:
                    done(ins, f"o{i}", obank[1])
                else:
                    ins.then_inc(sem("pv_done"), 1)
            for u in range(len(UNITS) + 4):
                if u < len(UNITS):
                    scores(u)
                if 2 <= u < len(UNITS) + 2:
                    probs(u - 2)
                if u >= 4:
                    values(u - 4)

            for h in range(RET_H + 2):
                if h < RET_H:
                    c, off = divmod(h, 2)
                    rows = slice(64 * off, 64 * off + 64)
                    for j in range(NT):
                        ps, where = bank("T")
                        done(pe.matmul(ps[:, 0:S - j * P], RK[rows, c, j * P:(j + 1) * P], RQ[rows, c, j * P:S],
                                       start=True, stop=True), f"rs{h}.{j}", where)
                if h >= 2:
                    pe.wait_ge(sem("yn_ready"), T.due("yn_ready"))
                    turn(f"mixT{2 + h}", [YN[:, i, :] for i in range(NT)], "G")
                if 1 <= h <= RET_H:
                    pe.wait_ge(sem("rw_ready"), T.due("rw_ready", NT))
                    ps, where = bank("O")
                    for i in range(NT):
                        for j in range(i + 1):
                            at_ = [0, 512, 896, 1152][j] + (i - j) * P
                            ins = pe.matmul(ps[:, i * P:(i + 1) * P], RW[(h - 1) % 2][:, at_:at_ + P],
                                            RV[:, j, h - 1, :], start=(j == 0), stop=(j == i))
                    done(ins, f"ry{h - 1}", where)

            def turned_back(name, buf, accumulated=None):
                if accumulated:
                    pe.wait_ge(sem(accumulated[0]), accumulated[1])
                else:
                    pe.wait_ge(*taken(name))
                turn(f"{name}T", [buf[:, i * P:(i + 1) * P] for i in range(NT)])

            for n in range(DC):
                gemm(f"wout{n}", Bhi, Blo, "B_ready" if n == 0 else None)
                if n:
                    turned_back(f"wout{n - 1}", G4[(n - 1) % 4])
            turned_back(f"wout{DC - 1}", G4[(DC - 1) % 4])

            if stop <= 2:
                return
            normed_in(1)
            for g, kg in enumerate(FF1_GROUPS):
                for j in range(kg):
                    gemm(f"up{g}.{j}", Ahi, Alo, "A_ready" if g == 0 and j == 0 else None)
                for n in range(DC):
                    gemm(f"dn{g}.{n}", Bhi, Blo, "B_ready" if n == 0 else None)
                    if g == 3 and n:
                        turned_back(f"dn{n - 1}", Y[:, n - 1], ("dn_used", 24 + n))
            turned_back(f"dn{DC - 1}", Y[:, DC - 1], ("dn_used", 32))

            if stop <= 3:
                return
            normed_in(2)
            for c in range(4):
                gemm(f"us{c}", Ahi, Alo, "A_ready" if c == 0 else None)
            gemm("if", Ahi, Alo)

            pe.wait_ge(sem("bb_ready"), T.due("bb_ready"))
            for x in range(2):
                turn(f"cT{x}", [cri[x][:, cc, :] for cc in range(4)])
            for x in range(2):
                for q in range(4):
                    turn(f"bt{x}.{q}", [BT[x][:, 4 * q + m, :] for m in range(4)])
                    if q in (1, 3) and 2 * x + q // 2 < 3:
                        gemm(SPILLED[2 * x + q // 2], Ahi, Alo)
            pe.wait_ge(sem("bt_ready"), T.due("bt_ready", 2))
            for k in range(S5_CHUNKS + 1):
                if k < S5_CHUNKS:
                    for x in range(2):
                        ps, where = bank("T")
                        done(pe.matmul(ps[:], BT[x][:, k, :], U[:, k // 4, :], start=True, stop=True),
                             f"bu{x}.{k}", where)
                    gemm(SPILLED[3 + 2 * k if k < 13 else 16 + k], Ahi, Alo)
                if k == 10:
                    pe.wait_ge(sem("ifr_ready"), T.due("ifr_ready"))
                    ps, where = bank("T")
                    for x in range(2):
                        for i in range(NT):
                            ins = pe.transpose(ps[:, (x * NT + i) * 4:(x * NT + i) * 4 + 4],
                                               gr[1 - x][0:4, i * P:(i + 1) * P], ident[0:4, 0:4])
                    done(ins, "aec", where)
                if k:
                    cc, m = divmod(k - 1, 4)
                    pe.wait_ge(sem("xs_ready"), T.due("xs_ready"))
                    if m == 0:
                        ops, owhere = bank("O")
                    for x in range(2):
                        ins = pe.matmul(ops[:], CT[x][:, k - 1, :], xx[x][:], start=(m == 0 and x == 0),
                                        stop=(m == 3 and x == 1))
                    if m == 3:
                        done(ins, f"s5y{cc}", owhere)
                    else:
                        ins.then_inc(sem("xs_used"), 1)
                if k < 13:
                    gemm(SPILLED[4 + 2 * k], Ahi, Alo)

            if stop <= 4:
                return
            def mlstm_values(h):
                pe.wait_ge(*taken(f"v{h}.0"))
                pe.wait_ge(*taken(f"v{h}.1"))
                pe.wait_ge(sem("mw_ready"), T.due("mw_ready", NT))
                for i in range(NT):
                    ps, where = bank("O" if i < 2 else "G")
                    for j in range(i + 1):
                        at_ = [0, 512, 896, 1152][j] + (i - j) * P
                        ins = pe.matmul(ps[:, 0:ML_DV + 1], W[:, at_:at_ + P], V[:, j, :],
                                        start=(j == 0), stop=(j == i))
                    done(ins, f"mn{h}.{i}", where)

            def mlstm_back(h):
                for i in range(NT):
                    pe.wait_ge(*taken(f"mn{h}.{i}"))
                for c in range(2):
                    turn(f"hT{h}.{c}", [H[:, i, c * P:(c + 1) * P] for i in range(NT)], "O")

            def mlstm_front(h):
                ps, where = bank("T")
                done(pe.matmul(ps[:], con[0:4, CON["sel"][0] + h * P:CON["sel"][0] + (h + 1) * P], negM[0:4, :],
                               start=True, stop=True), f"nb{h}", where)
                pe.wait_ge(sem(f"xm_in{h % 2}"), T.due(f"xm_in{h % 2}", 32))
                for c in range(2):
                    turn(f"v{h}.{c}", [XM[h % 2][:, c, 3 + i * P:3 + (i + 1) * P] for i in range(NT)])

            def mlstm_qk(h):
                pe.wait_ge(sem("xc_ready"), T.due("xc_ready", 2))
                gemm(f"mq{h}", XCh, XCl)
                gemm(f"mk{h}", XCh, XCl)

            def mlstm_scores(h):
                pe.wait_ge(*taken(f"mq{h}"))
                pe.wait_ge(*taken(f"mk{h}"))
                for j in range(NT):
                    ps, where = bank("T")
                    done(pe.matmul(ps[:, 0:S - j * P], QK[:, 1, j * P:(j + 1) * P], QK[:, 0, j * P:S],
                                   start=True, stop=True), f"ms{h}.{j}", where)

            pe.wait_ge(sem("negM_ready"), T.due("negM_ready"))
            mlstm_front(0)
            mlstm_qk(0)
            mlstm_scores(0)
            mlstm_qk(1)
            for h in range(ML_H):
                mlstm_values(h)
                if h < ML_H - 1:
                    mlstm_front(h + 1)
                    mlstm_scores(h + 1)
                mlstm_back(h)
                if h < ML_H - 2:
                    mlstm_qk(h + 2)

            if stop <= 5:
                return
            pe.wait_ge(sem("ys_ready"), T.due("ys_ready", 4))
            for n in range(DC):
                gemm(f"gv{n}", YShi, YSlo)
                gemm(f"gg{n}", YShi, YSlo)
                gemm(f"md{n}", Bhi, Blo, "B_ready" if n == 0 else None)
            for n in range(DC):
                gemm(f"mix{n}", Ahi, Alo, "A_ready" if n == 0 else None)
                if n:
                    turned_back(f"mix{n - 1}", G8[(n - 1) % 2])
            turned_back(f"mix{DC - 1}", G8[(DC - 1) % 2])

            if stop <= 6:
                return
            normed_in(3)
            for g, kg in enumerate(FF2_GROUPS):
                for j in range(kg):
                    gemm(f"fv{g}.{j}", Ahi, Alo, "A_ready" if g == 0 and j == 0 else None)
                    gemm(f"fg{g}.{j}", Ahi, Alo)
                for n in range(DC):
                    gemm(f"fd{g}.{n}", Bhi, Blo, "B_ready" if n == 0 else None)
                    if g == 2 and n:
                        turned_back(f"fd{n - 1}", Y[:, n - 1], ("fd_used", 16 + n))
            turned_back(f"fd{DC - 1}", Y[:, DC - 1], ("fd_used", 24))

        @block.scalar
        def _(act):
            A = Count()
            split = [0]

            def hi_upto(t):
                while split[0] <= min(t, NTILES - 1):
                    n = split[0]
                    act.wait_ge(sem(f"raw_in{n % RAW}"), 16 * (n // RAW + 1))
                    if n >= 2:
                        pool, b, k = product[CHUNKS[last_chunk_of_tile(n - 2)][0]]
                        act.wait_ge(sem(f"full_{pool}{b}"), k)
                    act.activation(whi[n % 2][:], raw[n % RAW][:], ACT.Copy).then_inc(sem("hi_split"), 1)
                    split[0] += 1

            def take(name):
                hi_upto(last_tile(INDEX[name]) + 1)
                act.wait_ge(*full(name))
                return bank_of(name)

            def normed_out(s):
                act.wait_ge(sem("rstd_ready"), A.due("rstd_ready"))
                for i in (2, 3):
                    if s < 2:
                        act.activation(N[:, i, :], X[:, i, :], ACT.Copy, scale=sd[:, i:i + 1]).then_inc(sem("norm_rows_a"), 1)
                        act.wait_ge(sem("norm_rows_a"), A.did("norm_rows_a"))
                    else:
                        act.activation(N[:, i, :], X[:, i, :], ACT.Identity, scale=sd[:, i:i + 1],
                                              bias=nmr[:, i:i + 1]).then_inc(sem("norm_rows_a"), 1)
                        act.wait_ge(sem("norm_rows_a"), A.did("norm_rows_a"))
                hi_upto(last_tile(INDEX[["kc", "up0.0", "us0", "fv0.0"][s]]) + 1)
                if s == 2:
                    act.wait_ge(sem("mod_ready"), A.due("mod_ready"))
                for c in range(DC):
                    n = f"xT{s}.{c}"
                    act.wait_ge(*full(n))
                    ps = bank_of(n)
                    if c >= 2:
                        act.wait_ge(sem("A_ready"), [0, 8, 16, 32][s] + c - 1)
                    if s < 2:
                        ins = act.activation(Fb[c % 2][:], ps[:], ACT.Copy, scale=p_(["ln1", "ln2"][s], c))
                    else:
                        m = (s - 2) * 24
                        ins = act.activation(Fb[c % 2][:], ps[:], ACT.Identity, scale=mod[:, m + 8 + c:m + 9 + c],
                                             bias=mod[:, m + c:m + c + 1])
                    ins.then_inc(taken(n)[0], 1)

            def sqrt_sd():
                act.wait_ge(sem("var_ready"), A.due("var_ready"))
                act.activation(sd[:], sd[:], ACT.Sqrt).then_inc(sem("sd_ready"), 1)
                act.wait_ge(sem("sd_ready"), A.did("sd_ready"))

            act.wait_ge(sem("con_in"), A.due("con_in", 16))
            act.wait_ge(sem("par_in"), A.due("par_in", 16))
            hi_upto(0)
            sqrt_sd()
            normed_out(0)

            def a_post1(n, c):
                if n in NORMED:
                    act.wait_ge(*full(f"ssq_{n}"))
                    ps = bank_of(f"ssq_{n}")
                    if NORMED.index(n):
                        act.wait_ge(sem("rs_used"), A.due("rs_used"))
                    ins = act.activation(RS[:], ps[:], ACT.Sqrt, bias=eps["rms"])
                    ins.then_inc(taken(f"ssq_{n}")[0], 1)
                elif n in TURNED:
                    act.wait_ge(*full(f"turn_{n}"))
                    ps = bank_of(f"turn_{n}")
                    if n == "gate":
                        ins = act.activation(GT[:], ps[:, 0:96].rearrange("p (i c) -> p i c", i=NT), ACT.Copy)
                    elif n[0] == "v":
                        ins = act.activation(VT[:, "sw".index(n[1])], ps[:].rearrange("p (i c) -> p i c", i=NT),
                                             ACT.Copy)
                    else:
                        ins = act.activation(RV[:, :, int(n[2])], ps[:].rearrange("p (i c) -> p i c", i=NT),
                                             ACT.Copy)
                    ins.then_inc(taken(f"turn_{n}")[0], 1)

            for c, n in enumerate(WIN):
                ps = take(n)
                f = F4[c % 4]
                if c >= 4:
                    old = WIN[c - 4]
                    if old in ROPED:
                        act.wait_ge(sem("roped"), ROPED.index(old) + 1)
                    elif old in TURNED:
                        act.wait_ge(*full(f"turn_{old}"))
                if n in NORMED:
                    if NORMED.index(n):
                        act.wait_ge(*full(f"ssq_{NORMED[NORMED.index(n) - 1]}"))
                    act.activation(SQ[:], ps[:], ACT.Square)
                    act.activation(f[:], ps[:], ACT.Copy).then_inc(taken(n)[0], 1)
                elif n == "vc":
                    act.activation(VC[:], ps[:], ACT.Copy).then_inc(taken(n)[0], 1)
                elif n == "gate":
                    act.activation(f[:], ps[:], ACT.Sigmoid).then_inc(taken(n)[0], 1)
                elif n in TURNED:
                    act.activation(f[:], ps[:], ACT.Copy).then_inc(taken(n)[0], 1)
                elif n[:2] == "rg":
                    act.activation(RG[:, int(n[2])], ps[:], ACT.Silu).then_inc(taken(n)[0], 1)
                else:
                    act.activation(f[:], ps[:], ACT.Copy).then_inc(taken(n)[0], 1)
                if c >= 1:
                    a_post1(WIN[c - 1], c - 1)
                if n == "ks":
                    act.wait_ge(*taken("vc"))
                    act.wait_ge(sem("roped"), 1)
                    for t, src in ((kc2, K[:, 0]), (vc2, VC[:])):
                        for g in range(2):
                            act.dma_start(t[0:64, g, :], src[64 * g:64 * g + 64, :]).then_inc(sem("two_rows"), 16)
                            act.dma_start(t[64:128, g, 0:S - 1], src[64 * g:64 * g + 64, 1:S])\
                               .then_inc(sem("two_rows"), 16)

            if stop <= 1:
                return
            act.wait_ge(sem("xfree"), A.due("xfree"))
            for w in range(2):
                act.wait_ge(*full(f"hid{w}"))
                ps = bank_of(f"hid{w}")
                act.activation(HS[w][0:2 * NCMP, :], ps[0:2 * NCMP, 0:CMP_HID], ACT.Silu).then_inc(taken(f"hid{w}")[0], 1)
            for w in range(2):
                act.wait_ge(*full(f"hidT{w}"))
                ps = bank_of(f"hidT{w}")
                act.activation(HK[w][:].rearrange("p h a b -> p h (a b)"),
                                      ps[:, 0:128].rearrange("p (h c) -> p h c", h=2)[:, :, 0:2 * NCMP], ACT.Copy).then_inc(taken(f"hidT{w}")[0], 1)
            act.wait_ge(*full("kcmp"))
            ps = bank_of("kcmp")
            act.wait_ge(sem("kcm_zero"), A.due("kcm_zero"))
            act.activation(KCM[:, :, 0:NCMP], ps[:, 0:2 * NCMP].rearrange("p (a b) -> p a b", a=2), ACT.Copy).then_inc(taken("kcmp")[0], 1)
            act.wait_ge(*full("vcmp"))
            ps = bank_of("vcmp")
            act.wait_ge(sem("vb_zero"), A.due("vb_zero"))
            for r in range(REP):
                rows = slice(32 * r, 32 * r + 32)
                ins = act.activation(VB[rows, :, r, :], ps[rows, 0:P].rearrange("p (a b) -> p a b", a=2), ACT.Copy)
            ins.then_inc(taken("vcmp")[0], 1)

            for i in range(NT + 1):
                if i < NT:
                    act.wait_ge(sem("cs_ready"), A.due("cs_ready"))
                    if i >= 2:
                        act.wait_ge(*full(f"ct{i - 2}"))
                    act.activation(cP[i % 2][:], cS[i % 2][:], ACT.Exp, scale=DH ** -0.5).then_inc(sem("ce_ready"), 1)
                    act.wait_ge(sem("ce_ready"), A.did("ce_ready"))
                if i:
                    act.wait_ge(*full(f"ct{i - 1}"))
                    ps = bank_of(f"ct{i - 1}")
                    act.activation(cT[:, i - 1], ps[:, 0:2 * P].rearrange("p (a b) -> p a b", a=2), ACT.Copy).then_inc(taken(f"ct{i - 1}")[0], 1)

            def exps(u):
                act.wait_ge(sem("s_ready"), A.due("s_ready"))
                if u >= 3:
                    act.wait_ge(*full(f"pt{u - 3}"))
                n = keys(UNITS[u][0], UNITS[u][2])[1] * P
                act.activation(Pr[u % 3][:, 0:n], sS[u % 3][:, 0:n], ACT.Exp, scale=DH ** -0.5,
                                      bias=NM[:, u:u + 1], accum_out=SUM[:, u:u + 1]).then_inc(sem("e_done"), 1)
                act.wait_ge(sem("e_done"), A.did("e_done"))

            def pts(u):
                nk = keys(UNITS[u][0], UNITS[u][2])[1]
                act.wait_ge(*full(f"pt{u}"))
                ps = bank_of(f"pt{u}")
                if u >= 3:
                    act.wait_ge(*values_done(u - 3))
                act.activation(PT[u % 3][:, 0:nk], ps[:, 0:nk * P].rearrange("p (a b) -> p a b", a=nk),
                                      ACT.Copy).then_inc(taken(f"pt{u}")[0], 1)
            for u in range(len(UNITS) + 2):
                if u < len(UNITS):
                    exps(u)
                if u >= 2:
                    pts(u - 2)
            for h in range(RET_H):
                act.wait_ge(sem("rvar_ready"), A.due("rvar_ready"))
                act.activation(sd[:], sd[:], ACT.Sqrt).then_inc(sem("sd_ready"), 1)
                act.wait_ge(sem("sd_ready"), A.did("sd_ready"))

            def back_out(name, buf, scale=1.0, wait=None):
                ps = take(name)
                if wait is not None:
                    act.wait_ge(*full(wait))
                act.activation(buf, ps[:], ACT.Copy, scale=scale).then_inc(taken(name)[0], 1)

            for n in range(DC):
                back_out(f"wout{n}", G4[n % 4][:], wait=f"wout{n - 4}T" if n >= 4 else None)
            if stop <= 2:
                return
            sqrt_sd()
            normed_out(1)
            act.wait_ge(sem("cB_in"), A.due("cB_in", 16))
            act.activation(cB[:], cB[:], ACT.Silu).then_inc(sem("cB_ready"), 1)
            act.wait_ge(sem("cB_ready"), A.did("cB_ready"))
            act.activation(s16[:, 0], p_("ldt", 0, 16), ACT.Exp).then_inc(sem("s5_a"), 1)
            act.wait_ge(sem("s5_a"), A.did("s5_a"))
            for g, kg in enumerate(FF1_GROUPS):
                for j in range(kg):
                    ps = take(f"up{g}.{j}")
                    u = g * 8 + j
                    if u >= 2:
                        act.wait_ge(sem("up_used"), u - 1)
                    if u < 2:
                        act.wait_ge(*full(f"wout{4 + 2 + u}T"))
                    act.activation(G4[2 + u % 2][:], ps[:], ACT.Relu).then_inc(taken(f"up{g}.{j}")[0], 1)
                for n in range(DC):
                    ps = take(f"dn{g}.{n}")
                    v = g * 8 + n
                    if v >= 2:
                        act.wait_ge(sem("dn_used"), v - 1)
                    act.activation(G4[v % 2][:], ps[:], ACT.Copy).then_inc(taken(f"dn{g}.{n}")[0], 1)
                    if v == 3:
                        act.wait_ge(sem("s5_d"), A.due("s5_d", 2))
                        act.activation(s16[:, 3], s16[:, 1], ACT.Exp).then_inc(sem("s5_a"), 1)
                        act.wait_ge(sem("s5_a"), A.did("s5_a"))
                        act.activation(s16[:, 4], s16[:, 5], ACT.Sin).then_inc(sem("s5_a"), 1)
                        act.wait_ge(sem("s5_a"), A.did("s5_a"))
                        act.activation(s16[:, 7], s16[:, 6], ACT.Sin).then_inc(sem("s5_a"), 1)
                        act.wait_ge(sem("s5_a"), A.did("s5_a"))

            if stop <= 3:
                return
            sqrt_sd()
            normed_out(2)
            for c in range(4):
                ps = take(f"us{c}")
                act.activation(U[:, c], ps[:], ACT.Identity, bias=p_("b_us", c)).then_inc(taken(f"us{c}")[0], 1)
            ps = take("if")
            act.activation(IF[:], ps[:], ACT.Identity, bias=p_("b_if")).then_inc(taken("if")[0], 1)
            def silus(h):
                for c in range(2):
                    act.wait_ge(sem("cv_ready"), A.due("cv_ready"))
                    act.activation(CA[:, c], CA[:, c], ACT.Silu).then_inc(sem("cs2_ready"), 1)
                    act.wait_ge(sem("cs2_ready"), A.did("cs2_ready"))

            hi_upto(last_tile(INDEX[SPILLED[2]]))
            act.wait_ge(sem("bb_ready"), A.due("bb_ready"))
            act.wait_ge(*full("cT1"))
            for k, name in enumerate(SPILLED + [""]):
                if name:
                    ps = take(name)
                    if k >= 3:
                        act.wait_ge(sem(f"spilled{k % 3}"), 16 * (k // 3))
                    kind, n = name[:2], int(name[2:])
                    act.activation(stage[k % 3][:], ps[:], ACT.Identity if kind == "xm" else ACT.Sigmoid,
                                          bias=p_(f"b_{kind}", n)).then_inc(taken(name)[0], 1)
                if k:
                    act.wait_ge(*taken(SPILLED[k - 1]))
                    act.dma_start(spill[k - 1], stage[(k - 1) % 3][:]).then_inc(sem(f"spilled{(k - 1) % 3}"), 16)
                if k == 9:
                    act.wait_ge(sem("if_d"), A.due("if_d"))
                    act.activation(gr[0][32:36], gr[0][32:36], ACT.Exp, scale=-1.0).then_inc(sem("act_step"), 1)
                    act.wait_ge(sem("act_step"), A.did("act_step"))
                    act.activation(gr[0][32:36], gr[0][32:36], ACT.Ln, bias=1.0).then_inc(sem("if_a"), 1)
                    act.wait_ge(sem("if_a"), A.did("if_a"))
                if k == 13:
                    act.wait_ge(sem("if_d"), A.due("if_d"))
                    act.activation(gr[0][0:4], IF[32:36], ACT.Copy).then_inc(sem("if_a"), 1)
                    act.wait_ge(sem("if_a"), A.did("if_a"))
                if k == 19:
                    act.wait_ge(sem("if_d"), A.due("if_d"))
                    act.activation(gr[0][0:4], gr[0][0:4], ACT.Exp).then_inc(sem("ifr_ready"), 1)
                    act.wait_ge(sem("ifr_ready"), A.did("ifr_ready"))
                if k == 26:
                    act.wait_ge(*full("aec"))
                    ps = bank_of("aec")
                    act.activation(AEC[:].rearrange("p a b c -> p (a b c)"), ps[:, 0:32], ACT.Copy).then_inc(taken("aec")[0], 1)
                if k in (14, 22, 28):
                    act.wait_ge(sem("s5f_ready"), A.due("s5f_ready"))
                    act.activation(Fb[0][:], U[:, (k - 14) // 7], ACT.Gelu_apprx_tanh).then_inc(sem("s5g_ready"), 1)
                    act.wait_ge(sem("s5g_ready"), A.did("s5g_ready"))
            silus(0)
            act.wait_ge(sem("s5f_ready"), A.due("s5f_ready"))
            act.activation(Fb[0][:], U[:, 3], ACT.Gelu_apprx_tanh).then_inc(sem("s5g_ready"), 1)
            act.wait_ge(sem("s5g_ready"), A.did("s5g_ready"))
            if stop <= 4:
                return
            def head_in(h):
                for c in range(2):
                    act.wait_ge(*full(f"v{h}.{c}"))
                    ps = bank_of(f"v{h}.{c}")
                    if h and c == 0:
                        act.wait_ge(*full(f"mn{h - 1}.{NT - 1}"))
                    act.activation(V[:, :, c * P:(c + 1) * P], ps[:].rearrange("p (i c) -> p i c", i=NT),
                                          ACT.Copy).then_inc(taken(f"v{h}.{c}")[0], 1)

            def head_decay(h):
                act.wait_ge(sem("nb_ready"), A.due("nb_ready"))
                nb = bank_of(f"nb{h}")
                for j in range(NT):
                    n = S - j * P
                    if n > P:
                        ins = act.activation(E[h % 2][:, TRI[j] + P:TRI[j] + n], nb[:, (j + 1) * P:S], ACT.Exp,
                                             bias=AEC[:, 0, j, h:h + 1])
                    if j == NT - 2:
                        ins.then_inc(taken(f"nb{h}")[0], 1)
                    act.activation(E[h % 2][:, TRI[j]:TRI[j] + P], NBd[:, j, :], ACT.Exp,
                                          bias=AEC[:, 0, j, h:h + 1]).then_inc(sem("e_ready"), 1)
                    act.wait_ge(sem("e_ready"), A.did("e_ready"))

            def head_qk(h):
                for x, n in enumerate((f"mq{h}", f"mk{h}")):
                    ps = take(n)
                    act.activation(QK[:, x], ps[:], ACT.Copy, scale=[ML_DK ** -0.5, 1.0][x]).then_inc(taken(n)[0], 1)

            head_in(0)
            head_qk(0)
            head_decay(0)
            silus(1)
            head_qk(1)
            for h in range(ML_H):
                if h < ML_H - 1:
                    head_in(h + 1)
                if h < ML_H - 2:
                    silus(h + 2)
                if h < ML_H - 1:
                    head_decay(h + 1)
                act.wait_ge(sem("rvar_ready"), A.due("rvar_ready"))
                act.activation(sd[:], sd[:], ACT.Sqrt).then_inc(sem("sd_ready"), 1)
                act.wait_ge(sem("sd_ready"), A.did("sd_ready"))
                act.wait_ge(sem("hf_ready"), A.due("hf_ready"))
                if h:
                    act.wait_ge(*full(f"hT{h - 1}.1"))
                for i in range(NT):
                    ps = bank_of(f"mn{h}.{i}")
                    act.activation(H[:, i, :], ps[:, 0:ML_DV], ACT.Identity, scale=sd[:, i:i + 1],
                                          bias=nmr[:, i:i + 1]).then_inc(taken(f"mn{h}.{i}")[0], 1)
                for c in range(2):
                    act.wait_ge(sem("hf_out"), A.due("hf_out"))
                    act.activation(Bhi[:, 2 * h + c], Fb[c][:], ACT.Copy).then_inc(sem("hf_hi"), 1)
                    act.wait_ge(sem("hf_hi"), A.did("hf_hi"))
                if h < ML_H - 2:
                    head_qk(h + 2)
            if stop <= 5:
                return
            for n in range(DC):
                for x, nm, fn, bias in [(1, "gv", ACT.Copy, None), (2, "gg", ACT.Sigmoid, None),
                                        (0, "md", ACT.Copy, None)]:
                    ps = take(f"{nm}{n}")
                    if x == 1:
                        act.wait_ge(sem("g8_free"), A.due("g8_free"))
                    kw = {"bias": p_(bias, n)} if bias else {}
                    act.activation(G8[x][:], ps[:], fn, **kw).then_inc(taken(f"{nm}{n}")[0], 1)
            act.wait_ge(sem("g8_free"), A.due("g8_free"))
            for n in range(DC):
                back_out(f"mix{n}", G8[n % 2][:], scale=mod[:, 16 + n:17 + n],
                         wait=f"mix{n - 2}T" if n >= 2 else None)
            if stop <= 6:
                return
            for i in range(2):
                sqrt_sd()
            normed_out(3)
            for g, kg in enumerate(FF2_GROUPS):
                for j in range(kg):
                    ps = take(f"fv{g}.{j}")
                    if g or j:
                        act.wait_ge(sem("fb_done"), A.due("fb_done"))
                    act.activation(FV[:], ps[:], ACT.Copy).then_inc(taken(f"fv{g}.{j}")[0], 1)
                    ps = take(f"fg{g}.{j}")
                    act.activation(GP[:, 2:2 + S], ps[:], ACT.Copy).then_inc(taken(f"fg{g}.{j}")[0], 1)
                    act.wait_ge(sem("fc_ready"), A.due("fc_ready"))
                    act.activation(FG[:], FG[:], ACT.Gelu_apprx_tanh).then_inc(sem("fg_ready"), 1)
                    act.wait_ge(sem("fg_ready"), A.did("fg_ready"))
                for n in range(DC):
                    ps = take(f"fd{g}.{n}")
                    v = g * 8 + n
                    if v >= 2:
                        act.wait_ge(sem("fd_used"), v - 1)
                    act.activation(G8[v % 2][:], ps[:], ACT.Copy, scale=mod[:, 40 + n:41 + n]).then_inc(taken(f"fd{g}.{n}")[0], 1)
            sqrt_sd()

        @block.gpsimd
        def _(pool):
            last = {1: WIN[-1], 2: "wout7", 3: "dn3.7", 4: "gb7", 5: "mk3", 6: "mix7"}.get(stop)
            for t in range(min(NTILES, last_tile(INDEX[last]) + 2) if last else NTILES):
                pool.wait_ge(sem("hi_split"), t + 1)
                pool.tensor_tensor(wlo[t % 2][:], raw[t % RAW][:], rd(whi[t % 2][:]), ALU.subtract)\
                    .then_inc(sem("lo_split"), 1)

        @block.vector
        def _(dve):
            v = Count()
            tt, ts, stt = dve.tensor_tensor, dve.tensor_scalar, dve.scalar_tensor_tensor

            def quarter_stats(q, tiles=range(NT)):
                for i in tiles:
                    dve.bn_stats(st4[:, i, q, :], X[:, i, q * 256:(q + 1) * 256]).then_inc(sem("dve_step"), 1)
                    dve.wait_ge(sem("dve_step"), v.did("dve_step"))

            def row_stats(rms):
                for i in range(NT - 1):
                    dve.bn_aggr(mv[:, i, :], st4[:, i].rearrange("p a b -> p (a b)"))
                dve.bn_aggr(mv[:, NT - 1, :], st4[:, NT - 1].rearrange("p a b -> p (a b)")).then_inc(sem("dve_step"), 1)
                dve.wait_ge(sem("dve_step"), v.did("dve_step"))
                if rms:
                    tt(sd[:], mv[:, :, 0], mv[:, :, 0], ALU.mult).then_inc(sem("dve_step"), 1)
                    dve.wait_ge(sem("dve_step"), v.did("dve_step"))
                    tt(sd[:], sd[:], mv[:, :, 1], ALU.add).then_inc(sem("dve_step"), 1)
                    dve.wait_ge(sem("dve_step"), v.did("dve_step"))
                    ts(sd[:], sd[:], RMS_EPS, None, ALU.add).then_inc(sem("var_ready"), 1)
                    dve.wait_ge(sem("var_ready"), v.did("var_ready"))
                else:
                    ts(sd[:], mv[:, :, 1], LN_EPS, None, ALU.add).then_inc(sem("var_ready"), 1)
                    dve.wait_ge(sem("var_ready"), v.did("var_ready"))
                dve.wait_ge(sem("sd_ready"), v.due("sd_ready"))
                dve.reciprocal(sd[:], sd[:]).then_inc(sem("dve_step"), 1)
                dve.wait_ge(sem("dve_step"), v.did("dve_step"))

            def norm_rows(s):
                rms = s < 2
                row_stats(rms)
                if rms:
                    dve.sem_inc(sem("rstd_ready"), 1)
                else:
                    stt(nmr[:], mv[:, :, 0], -1.0, sd[:], ALU.mult, ALU.mult).then_inc(sem("rstd_ready"), 1)
                    dve.wait_ge(sem("rstd_ready"), v.did("rstd_ready"))
                for i in range(2):
                    if rms:
                        ins = ts(N[:, i, :], X[:, i, :], sd[:, i:i + 1], None, ALU.mult)
                    else:
                        ins = ts(N[:, i, :], X[:, i, :], mv[:, i, 0:1], sd[:, i:i + 1], ALU.subtract, ALU.mult)
                    ins.then_inc(sem("norm_rows"), 1)
                    dve.wait_ge(sem("norm_rows"), v.did("norm_rows"))
                dve.wait_ge(sem("norm_rows_a"), v.due("norm_rows_a", 2))

            def split_to(hi, lo, f, name):
                dve.tensor_copy(hi, f).then_inc(sem("dve_step"), 1)
                dve.wait_ge(sem("dve_step"), v.did("dve_step"))
                tt(lo, f, rd(hi), ALU.subtract).then_inc(sem(name), 1)
                dve.wait_ge(sem(name), v.did(name))

            def normed_in(s):
                for c in range(DC):
                    pool_, b, k = product[f"xT{s}.{c}"]
                    dve.wait_ge(sem(f"free_{pool_}{b}"), k)
                    dve.tensor_copy(Ahi[:, c], Fb[c % 2][:]).then_inc(sem("dve_step"), 1)
                    dve.wait_ge(sem("dve_step"), v.did("dve_step"))
                    tt(Alo[:, c], Fb[c % 2][:], rd(Ahi[:, c]), ALU.subtract).then_inc(sem("A_ready"), 1)
                    dve.wait_ge(sem("A_ready"), v.did("A_ready"))

            dve.wait_ge(sem("con_in"), v.due("con_in", 16))
            dve.wait_ge(sem("par_in"), v.due("par_in", 16))
            for i in range(NT):
                dve.wait_ge(sem(f"x_in{i}"), 16)
                for q in range(4):
                    quarter_stats(q, [i])
            norm_rows(0)
            dve.sem_inc(sem("n0_done"), 1)
            normed_in(0)

            def rope_chunk(n, c):
                f = F4[c % 4]
                dst = {"k": K, "q": Q}.get(n[0]) if n[0] != "r" else (RQ if n[1] == "q" else RK)
                idx = {"kc": 0, "ks": 1, "kw": 2}.get(n, int(n[-1]) if n[-1].isdigit() else 0)
                o = dst[:, idx]
                dve.wait_ge(*full(f"rot_{n}"))
                ps = bank_of(f"rot_{n}")
                if n == ROPED[0]:
                    dve.wait_ge(sem("rope_tab"), v.due("rope_tab", 16))
                tt(o, f[:], rope[:, 0], ALU.mult).then_inc(sem("dve_step"), 1)
                dve.wait_ge(sem("dve_step"), v.did("dve_step"))
                tt(Fb[0][:], ps[:], rope[:, 1], ALU.mult).then_inc(taken(f"rot_{n}")[0], 1)
                dve.wait_ge(*taken(f"rot_{n}"))
                tt(o, o, Fb[0][:], ALU.add).then_inc(sem("roped"), 1)
                dve.wait_ge(sem("roped"), v.did("roped"))

            for c, n in enumerate(WIN + ["", ""]):
                if 1 <= c <= len(WIN) and WIN[c - 1] in NORMED:
                    m = WIN[c - 1]
                    dve.wait_ge(*taken(f"ssq_{m}"))
                    dve.reciprocal(RS[:], RS[:]).then_inc(sem("dve_step"), 1)
                    dve.wait_ge(sem("dve_step"), v.did("dve_step"))
                    w = p_("qn") if m[0] == "q" else p_("kn", ["kc", "ks", "kw"].index(m))
                    f = F4[(c - 1) % 4]
                    stt(f[:], f[:], w, RS[:], ALU.mult, ALU.mult).then_inc(sem("rope_in"), 1)
                    dve.wait_ge(sem("rope_in"), v.did("rope_in"))
                    dve.sem_inc(sem("rs_used"), 1)
                elif 1 <= c <= len(WIN) and WIN[c - 1] in ROPED:
                    dve.wait_ge(*taken(WIN[c - 1]))
                    dve.sem_inc(sem("rope_in"), 1)
                    v.did("rope_in")
                if c >= 2 and WIN[c - 2] in ROPED:
                    rope_chunk(WIN[c - 2], c - 2)

            if stop <= 1:
                return
            dve.wait_ge(sem("two_rows"), v.due("two_rows", 8 * 16))
            for w, (src, pe_) in enumerate(((kc2, "pek"), (vc2, "pev"))):
                view = src[:].rearrange("p g (n l) -> p l g n", l=16)
                for half in range(2):
                    for l in range(8):
                        lp = half * 8 + l
                        ts(kcp[w][:, lp], view[:, 2 * l, :, half:half + NCMP], p_(pe_, lp), None, ALU.add).then_inc(sem("dve_step"), 1)
                        dve.wait_ge(sem("dve_step"), v.did("dve_step"))
                dve.sem_inc(sem("cmp_in"), 1)
            dve.wait_ge(*taken("turn_rv3"))
            dve.sem_inc(sem("xfree"), 1)
            dve.sem_inc(sem("xfree_sp"), 1)
            dve.memset(KCM[:], 0.0).then_inc(sem("kcm_zero"), 1)
            dve.wait_ge(sem("kcm_zero"), v.did("kcm_zero"))
            dve.memset(VB[:], 0.0).then_inc(sem("vb_zero"), 1)
            dve.wait_ge(sem("vb_zero"), v.did("vb_zero"))
            dve.memset(HVr[:], 0.0).then_inc(sem("dve_step"), 1)
            dve.wait_ge(sem("dve_step"), v.did("dve_step"))
            dve.wait_ge(*taken("hidT1"))
            for hc in range(2):
                for g in range(2):
                    dve.tensor_copy(HVr[:, hc, g, :, 0:NCMP],
                                           HK[1][:, hc, g, :].unsqueeze(1).to_broadcast([P, REP, NCMP])).then_inc(sem("dve_step"), 1)
                    dve.wait_ge(sem("dve_step"), v.did("dve_step"))
            dve.sem_inc(sem("hidv_ready"), 1)

            dve.wait_ge(sem("mask_in"), v.due("mask_in", 32))
            cm = masks[:, 1280:1536].rearrange("p (x i n) -> p x i n", x=2, i=NT)
            def cmp_scores(i):
                mb = cm[:, 0, i, :].unsqueeze(1).to_broadcast([P, HEADS, NCMP_PAD])
                c = cS[i % 2]
                for g in range(GROUPS):
                    dve.wait_ge(*full(f"cs{i}.{g}"))
                    ps = bank_of(f"cs{i}.{g}")
                    tt(c[:, 4 * g:4 * g + 4], ps[:, 0:P].rearrange("p (h n) -> p h n", h=REP),
                              mb[:, 4 * g:4 * g + 4], ALU.add).then_inc(taken(f"cs{i}.{g}")[0], 1)
                    dve.wait_ge(*taken(f"cs{i}.{g}"))
                dve.tensor_reduce(m8[0][:], c[:], AX, ALU.max).then_inc(sem("dve_step"), 1)
                dve.wait_ge(sem("dve_step"), v.did("dve_step"))
                tt(c[:], c[:], m8[0][:].unsqueeze(2).to_broadcast([P, HEADS, NCMP_PAD]), ALU.subtract).then_inc(sem("cs_ready"), 1)
                dve.wait_ge(sem("cs_ready"), v.did("cs_ready"))

            def cmp_probs(i):
                m1 = cm[:, 1, i, :].unsqueeze(1).to_broadcast([P, HEADS, NCMP_PAD])
                c = cP[i % 2]
                dve.wait_ge(sem("ce_ready"), v.due("ce_ready"))
                dve.tensor_reduce(m8[1][:], c[:], AX, ALU.add).then_inc(sem("dve_step"), 1)
                dve.wait_ge(sem("dve_step"), v.did("dve_step"))
                dve.reciprocal(m8[2][:], m8[1][:]).then_inc(sem("dve_step"), 1)
                dve.wait_ge(sem("dve_step"), v.did("dve_step"))
                tt(m8[3][:], m8[2][:], GT[:, i, 0:8], ALU.mult)
                tt(c[:], c[:], m1, ALU.mult).then_inc(sem("dve_step"), 1)
                dve.wait_ge(sem("dve_step"), v.did("dve_step"))
                tt(c[:], c[:], m8[3][:].unsqueeze(2).to_broadcast([P, HEADS, NCMP_PAD]), ALU.mult).then_inc(sem("cp_ready"), 1)
                dve.wait_ge(sem("cp_ready"), v.did("cp_ready"))
            for i in range(NT + 1):
                if i < NT:
                    cmp_scores(i)
                if i:
                    cmp_probs(i - 1)

            def score_max(u):
                i, hh, b = UNITS[u]
                n = keys(i, b)[1] * P
                dve.wait_ge(*full(f"s{u}"))
                ps = bank_of(f"s{u}")
                if u >= 3:
                    dve.wait_ge(sem("e_done"), u - 2)
                m = masks[:, 384 - i * P:384 - i * P + n] if b == 0 else masks[:, 896 + 384 - n:896 + 384]
                dve.tensor_tensor_reduce(sS[u % 3][:, 0:n], ps[:, 0:n], m, 1.0, NEG, ALU.add, ALU.max,
                                                MX[:, u:u + 1]).then_inc(taken(f"s{u}")[0], 1)
                dve.wait_ge(*taken(f"s{u}"))
                ts(NM[:, u:u + 1], MX[:, u:u + 1], -DH ** -0.5, None, ALU.mult).then_inc(sem("s_ready"), 1)
                dve.wait_ge(sem("s_ready"), v.did("s_ready"))

            def gated(u):
                i, hh, b = UNITS[u]
                n = keys(i, b)[1] * P
                dve.wait_ge(sem("e_done"), u + 1)
                dve.reciprocal(MX[:, u:u + 1], SUM[:, u:u + 1]).then_inc(sem("dve_step"), 1)
                dve.wait_ge(sem("dve_step"), v.did("dve_step"))
                g = 8 + 8 * b + hh
                ts(Pr[u % 3][:, 0:n], Pr[u % 3][:, 0:n], MX[:, u:u + 1], GT[:, i, g:g + 1], ALU.mult,
                          ALU.mult).then_inc(sem("p_ready"), 1)
                dve.wait_ge(sem("p_ready"), v.did("p_ready"))

            def mixed(i):
                dve.wait_ge(*full(f"o{i}"))
                ps = bank_of(f"o{i}")
                o4 = ps[:].rearrange("p (c t) -> p c t", c=4)
                cols = slice(i * P, (i + 1) * P)
                dve.tensor_copy(Bhi[:, 0:4, cols], o4).then_inc(sem("dve_step"), 1)
                dve.wait_ge(sem("dve_step"), v.did("dve_step"))
                tt(Blo[:, 0:4, cols], o4, rd(Bhi[:, 0:4, cols]), ALU.subtract).then_inc(taken(f"o{i}")[0], 1)
                dve.wait_ge(*taken(f"o{i}"))
            for u in range(len(UNITS) + 6):
                if u < len(UNITS):
                    score_max(u)
                if 1 <= u <= len(UNITS):
                    gated(u - 1)
                if u >= 6 and (u - 6) % 16 == 15:
                    mixed((u - 6) // 16)
            for c in range(4):
                dve.sem_inc(sem("B_ready"), 1)
                v.did("B_ready")

            def decayed(h):
                for j in range(NT):
                    dve.wait_ge(*full(f"rs{h}.{j}"))
                    ps = bank_of(f"rs{h}.{j}")
                    n = S - j * P
                    a = [0, 512, 896, 1152][j]
                    tt(RW[h % 2][:, a:a + n], ps[:, 0:n], decay[:, h, 0:n], ALU.mult).then_inc(taken(f"rs{h}.{j}")[0], 1)
                    dve.wait_ge(*taken(f"rs{h}.{j}"))
                    dve.sem_inc(sem("rw_ready"), 1)

            def group_norm(h):
                dve.wait_ge(*full(f"ry{h}"))
                ps = bank_of(f"ry{h}")
                for i in range(NT):
                    dve.bn_stats(st4[:, i, 0, :], ps[:, i * P:(i + 1) * P]).then_inc(sem("dve_step"), 1)
                    dve.wait_ge(sem("dve_step"), v.did("dve_step"))
                for i in range(NT):
                    dve.bn_aggr(mv[:, i, :], st4[:, i, 0, :]).then_inc(sem("dve_step"), 1)
                    dve.wait_ge(sem("dve_step"), v.did("dve_step"))
                ts(sd[:], mv[:, :, 1], RMS_EPS, None, ALU.add).then_inc(sem("rvar_ready"), 1)
                dve.wait_ge(sem("rvar_ready"), v.did("rvar_ready"))
                dve.wait_ge(sem("sd_ready"), v.due("sd_ready"))
                dve.reciprocal(sd[:], sd[:]).then_inc(sem("dve_step"), 1)
                dve.wait_ge(sem("dve_step"), v.did("dve_step"))
                if h:
                    dve.wait_ge(*full(f"mixT{3 + h}"))
                for i in range(NT):
                    ins = ts(YN[:, i, :], ps[:, i * P:(i + 1) * P], mv[:, i, 0:1], sd[:, i:i + 1],
                             ALU.subtract, ALU.mult)
                    if i == NT - 1:
                        ins.then_inc(taken(f"ry{h}")[0], 1)
                        dve.wait_ge(*taken(f"ry{h}"))
                dve.sem_inc(sem("yn_ready"), 1)

            def retention_out(h):
                dve.wait_ge(*full(f"mixT{4 + h}"))
                ps = bank_of(f"mixT{4 + h}")
                stt(Fb[0][:], ps[:], p_("retn", h), RG[:, h], ALU.mult, ALU.mult).then_inc(taken(f"mixT{4 + h}")[0], 1)
                dve.wait_ge(*taken(f"mixT{4 + h}"))
                split_to(Bhi[:, 4 + h], Blo[:, 4 + h], Fb[0][:], "B_ready")
            for h in range(RET_H + 2):
                if h < RET_H:
                    decayed(h)
                if h >= 2:
                    retention_out(h - 2)
                if 1 <= h <= RET_H:
                    group_norm(h - 1)
            dve.sem_inc(sem("mix_done"), 1)

            def back_in(name, n, alpha=None):
                dve.wait_ge(*full(f"{name}T"))
                ps = bank_of(f"{name}T")
                x = X[:, :, n * P:(n + 1) * P]
                t = ps[:].rearrange("p (i c) -> p i c", i=NT)
                if alpha is None:
                    ins = tt(x, x, t, ALU.add)
                else:
                    ins = stt(x, x, alpha, t, ALU.mult, ALU.add)
                ins.then_inc(taken(f"{name}T")[0], 1)
                dve.wait_ge(*taken(f"{name}T"))
                if n % 2:
                    quarter_stats(n // 2)

            dve.wait_ge(sem("x_again"), v.due("x_again", 64))
            for n in range(DC):
                back_in(f"wout{n}", n)
            if stop <= 2:
                dve.sem_inc(sem("x_final"), 1)
                return
            norm_rows(1)
            normed_in(1)
            ada = [0]

            def ada_tile():
                t = ada[0]
                if t == 48:
                    return
                ada[0] += 1
                dve.wait_ge(sem(f"ada_in{t % 3}"), 16 * (t // 3 + 1))
                dve.tensor_tensor_reduce(junk[:], adaw[t % 3][:], cB[:], 1.0, 0.0, ALU.mult, ALU.add,
                                                mod[:, t:t + 1]).then_inc(sem("ada_used"), 1)
                dve.wait_ge(sem("ada_used"), v.did("ada_used"))

            def c16(i):
                return s16[:, i]
            lre, lim = p_("lre", 0, 16), p_("lim", 0, 16)
            mag, si, co = c16(3), c16(4), c16(7)
            ar1, ai, den, zr, zi, t1, t2 = (c16(i) for i in range(9, 16))

            def s5_angles():
                dve.wait_ge(sem("s5_a"), v.due("s5_a"))
                tt(c16(1), lre, c16(0), ALU.mult).then_inc(sem("dve_step"), 1)
                dve.wait_ge(sem("dve_step"), v.did("dve_step"))
                tt(c16(2), lim, c16(0), ALU.mult).then_inc(sem("s5_d"), 1)
                dve.wait_ge(sem("s5_d"), v.did("s5_d"))
                ts(c16(8), c16(2), 1.0 / (2 * math.pi), ROUND, ALU.mult, ALU.add).then_inc(sem("dve_step"), 1)
                dve.wait_ge(sem("dve_step"), v.did("dve_step"))
                ts(c16(8), c16(8), ROUND, None, ALU.subtract).then_inc(sem("dve_step"), 1)
                dve.wait_ge(sem("dve_step"), v.did("dve_step"))
                c1 = 6.28125
                c2 = round((2 * math.pi - c1) * 2.0 ** 20) / 2.0 ** 20
                c3 = 2 * math.pi - c1 - c2
                for k in (c1, c2, c3):
                    stt(c16(2), c16(8), -k, c16(2), ALU.mult, ALU.add).then_inc(sem("dve_step"), 1)
                    dve.wait_ge(sem("dve_step"), v.did("dve_step"))
                ts(c16(5), c16(2), math.pi - 1e-6, -math.pi + 1e-6, ALU.min, ALU.max).then_inc(sem("dve_step"), 1)
                dve.wait_ge(sem("dve_step"), v.did("dve_step"))
                stt(c16(6), c16(5), -1.0, c16(5), ALU.mult, ALU.max).then_inc(sem("dve_step"), 1)
                dve.wait_ge(sem("dve_step"), v.did("dve_step"))
                ts(c16(6), c16(6), -1.0, math.pi / 2, ALU.mult, ALU.add).then_inc(sem("s5_d"), 1)
                dve.wait_ge(sem("s5_d"), v.did("s5_d"))

            def s5_factors():
                dve.wait_ge(sem("s5_a"), v.due("s5_a", 3))
                tt(ar1, mag, co, ALU.mult).then_inc(sem("dve_step"), 1)
                dve.wait_ge(sem("dve_step"), v.did("dve_step"))
                ts(ar1, ar1, 1.0, None, ALU.subtract).then_inc(sem("dve_step"), 1)
                dve.wait_ge(sem("dve_step"), v.did("dve_step"))
                tt(ai, mag, si, ALU.mult).then_inc(sem("dve_step"), 1)
                dve.wait_ge(sem("dve_step"), v.did("dve_step"))
                tt(den, lre, lre, ALU.mult).then_inc(sem("dve_step"), 1)
                dve.wait_ge(sem("dve_step"), v.did("dve_step"))
                tt(t1, lim, lim, ALU.mult).then_inc(sem("dve_step"), 1)
                dve.wait_ge(sem("dve_step"), v.did("dve_step"))
                tt(den, den, t1, ALU.add).then_inc(sem("dve_step"), 1)
                dve.wait_ge(sem("dve_step"), v.did("dve_step"))
                dve.reciprocal(den, den).then_inc(sem("dve_step"), 1)
                dve.wait_ge(sem("dve_step"), v.did("dve_step"))
                for z, (a, b_, op) in ((zr, (ar1, ai, ALU.add)), (zi, (ai, ar1, ALU.subtract))):
                    tt(t1, a, lre, ALU.mult).then_inc(sem("dve_step"), 1)
                    dve.wait_ge(sem("dve_step"), v.did("dve_step"))
                    tt(t2, b_, lim, ALU.mult).then_inc(sem("dve_step"), 1)
                    dve.wait_ge(sem("dve_step"), v.did("dve_step"))
                    tt(z, t1, t2, op).then_inc(sem("dve_step"), 1)
                    dve.wait_ge(sem("dve_step"), v.did("dve_step"))
                    tt(z, z, den, ALU.mult).then_inc(sem("dve_step"), 1)
                    dve.wait_ge(sem("dve_step"), v.did("dve_step"))
                dve.tensor_copy(pw[:, 0, 0], co).then_inc(sem("dve_step"), 1)
                dve.wait_ge(sem("dve_step"), v.did("dve_step"))
                dve.tensor_copy(pw[:, 0, 1], si).then_inc(sem("dve_step"), 1)
                dve.wait_ge(sem("dve_step"), v.did("dve_step"))
                for m in range(8):
                    tt(t1, pw[:, m, 0], pw[:, m, 0], ALU.mult).then_inc(sem("dve_step"), 1)
                    dve.wait_ge(sem("dve_step"), v.did("dve_step"))
                    tt(t2, pw[:, m, 1], pw[:, m, 1], ALU.mult).then_inc(sem("dve_step"), 1)
                    dve.wait_ge(sem("dve_step"), v.did("dve_step"))
                    tt(pw[:, m + 1, 0], t1, t2, ALU.subtract).then_inc(sem("dve_step"), 1)
                    dve.wait_ge(sem("dve_step"), v.did("dve_step"))
                    tt(t1, pw[:, m, 0], pw[:, m, 1], ALU.mult).then_inc(sem("dve_step"), 1)
                    dve.wait_ge(sem("dve_step"), v.did("dve_step"))
                    ts(pw[:, m + 1, 1], t1, 2.0, None, ALU.mult).then_inc(sem("dve_step"), 1)
                    dve.wait_ge(sem("dve_step"), v.did("dve_step"))
                sg = seg[:]
                dve.memset(sg[:, 0, :, 0], 1.0).then_inc(sem("dve_step"), 1)
                dve.wait_ge(sem("dve_step"), v.did("dve_step"))
                dve.memset(sg[:, 1, :, 0], 0.0).then_inc(sem("dve_step"), 1)
                dve.wait_ge(sem("dve_step"), v.did("dve_step"))
                for x in range(2):
                    dve.tensor_copy(sg[:, x, :, 1], pw[:, 7, x]).then_inc(sem("dve_step"), 1)
                    dve.wait_ge(sem("dve_step"), v.did("dve_step"))
                    dve.tensor_copy(sg[:, x, :, 2], pw[:, 8, x]).then_inc(sem("dve_step"), 1)
                    dve.wait_ge(sem("dve_step"), v.did("dve_step"))
                tt(t1, pw[:, 7, 0], pw[:, 8, 0], ALU.mult).then_inc(sem("dve_step"), 1)
                dve.wait_ge(sem("dve_step"), v.did("dve_step"))
                tt(t2, pw[:, 7, 1], pw[:, 8, 1], ALU.mult).then_inc(sem("dve_step"), 1)
                dve.wait_ge(sem("dve_step"), v.did("dve_step"))
                tt(sg[:, 0, :, 3], t1, t2, ALU.subtract).then_inc(sem("dve_step"), 1)
                dve.wait_ge(sem("dve_step"), v.did("dve_step"))
                tt(t1, pw[:, 7, 0], pw[:, 8, 1], ALU.mult).then_inc(sem("dve_step"), 1)
                dve.wait_ge(sem("dve_step"), v.did("dve_step"))
                tt(t2, pw[:, 7, 1], pw[:, 8, 0], ALU.mult).then_inc(sem("dve_step"), 1)
                dve.wait_ge(sem("dve_step"), v.did("dve_step"))
                tt(sg[:, 1, :, 3], t1, t2, ALU.add).then_inc(sem("dve_step"), 1)
                dve.wait_ge(sem("dve_step"), v.did("dve_step"))
                for x in range(2):
                    dve.memset(ring_step[x][:, :, 0], 1.0 - x).then_inc(sem("dve_step"), 1)
                    dve.wait_ge(sem("dve_step"), v.did("dve_step"))

            def s5_inputs():
                dve.wait_ge(sem("s5_in"), v.due("s5_in", 64))
                zrb, zib = (z.unsqueeze(2).to_broadcast([P, 16, 16]) for z in (zr, zi))
                b0, b1 = (junk[:, 256 * x:256 * x + 256].rearrange("p (a b) -> p a b", a=16) for x in range(2))
                tt(b0, bri[1][:], zib, ALU.mult).then_inc(sem("dve_step"), 1)
                dve.wait_ge(sem("dve_step"), v.did("dve_step"))
                tt(b1, bri[0][:], zib, ALU.mult).then_inc(sem("dve_step"), 1)
                dve.wait_ge(sem("dve_step"), v.did("dve_step"))
                tt(bri[0][:], bri[0][:], zrb, ALU.mult).then_inc(sem("dve_step"), 1)
                dve.wait_ge(sem("dve_step"), v.did("dve_step"))
                tt(bri[0][:], bri[0][:], b0, ALU.subtract).then_inc(sem("dve_step"), 1)
                dve.wait_ge(sem("dve_step"), v.did("dve_step"))
                tt(bri[1][:], bri[1][:], zrb, ALU.mult).then_inc(sem("dve_step"), 1)
                dve.wait_ge(sem("dve_step"), v.did("dve_step"))
                tt(bri[1][:], bri[1][:], b1, ALU.add).then_inc(sem("dve_step"), 1)
                dve.wait_ge(sem("dve_step"), v.did("dve_step"))

            def s5_double(e, k0, k1):
                w = 1 << e
                n = k1 - k0
                pc, ps_ = (pw[:, e, x, k0:k1].unsqueeze(2).to_broadcast([P, n, w]) for x in range(2))
                c_old, s_old = (ring_step[x][:, k0:k1, 0:w] for x in range(2))
                c_new, s_new = (ring_step[x][:, k0:k1, w:2 * w] for x in range(2))
                a, b = (dbl[x][:, k0:k1, 0:w] for x in range(2))
                tt(a, s_old, ps_, ALU.mult).then_inc(sem("dve_step"), 1)
                dve.wait_ge(sem("dve_step"), v.did("dve_step"))
                tt(b, c_old, ps_, ALU.mult).then_inc(sem("dve_step"), 1)
                dve.wait_ge(sem("dve_step"), v.did("dve_step"))
                tt(c_new, c_old, pc, ALU.mult).then_inc(sem("dve_step"), 1)
                dve.wait_ge(sem("dve_step"), v.did("dve_step"))
                tt(c_new, c_new, a, ALU.subtract).then_inc(sem("dve_step"), 1)
                dve.wait_ge(sem("dve_step"), v.did("dve_step"))
                tt(s_new, s_old, pc, ALU.mult).then_inc(sem("dve_step"), 1)
                dve.wait_ge(sem("dve_step"), v.did("dve_step"))
                tt(s_new, s_new, b, ALU.add).then_inc(sem("dve_step"), 1)
                dve.wait_ge(sem("dve_step"), v.did("dve_step"))

            def s5_piece(n):
                if n == 1:
                    s5_angles()
                elif n == 5:
                    s5_factors()
                elif n == 6:
                    s5_inputs()
                elif 8 <= n < 14:
                    s5_double(n - 8, 0, 16)
                elif 14 <= n < 16:
                    s5_double(6, 8 * n - 112, 8 * n - 104)

            dve.wait_ge(sem("cB_ready"), v.due("cB_ready"))
            for g, kg in enumerate(FF1_GROUPS):
                for j in range(kg):
                    dve.wait_ge(*taken(f"up{g}.{j}"))
                    r = G4[2 + (g * 8 + j) % 2]
                    tt(r[:], r[:], r[:], ALU.mult).then_inc(sem("dve_step"), 1)
                    dve.wait_ge(sem("dve_step"), v.did("dve_step"))
                    dve.tensor_copy(Bhi[:, j], r[:]).then_inc(sem("dve_step"), 1)
                    dve.wait_ge(sem("dve_step"), v.did("dve_step"))
                    tt(Blo[:, j], r[:], rd(Bhi[:, j]), ALU.subtract).then_inc(sem("B_ready"), 1)
                    dve.wait_ge(sem("B_ready"), v.did("B_ready"))
                    dve.sem_inc(sem("up_used"), 1)
                    ada_tile()
                for n in range(DC):
                    dve.wait_ge(*taken(f"dn{g}.{n}"))
                    f = G4[(g * 8 + n) % 2]
                    if g == 0:
                        ins = dve.tensor_copy(Y[:, n], f[:])
                    else:
                        ins = tt(Y[:, n], Y[:, n], f[:], ALU.add)
                    ins.then_inc(sem("dn_used"), 1)
                    dve.wait_ge(sem("dn_used"), v.did("dn_used"))
                    ada_tile()
                    s5_piece(g * 8 + n)
                    if g == 3:
                        if n:
                            back_in(f"dn{n - 1}", n - 1)
            back_in(f"dn{DC - 1}", DC - 1)
            dve.sem_inc(sem("ff1_done"), 1)
            tt(mod[:], mod[:], p_("bada", 0, 48), ALU.add).then_inc(sem("dve_step"), 1)
            dve.wait_ge(sem("dve_step"), v.did("dve_step"))
            for a in (8, 16, 32, 40):
                ts(mod[:, a:a + 8], mod[:, a:a + 8], 1.0, None, ALU.add).then_inc(sem("dve_step"), 1)
                dve.wait_ge(sem("dve_step"), v.did("dve_step"))
            dve.sem_inc(sem("mod_ready"), 1)
            if stop <= 3:
                dve.sem_inc(sem("x_final"), 1)
                return
            norm_rows(2)
            normed_in(2)

            for x in range(2):
                dve.memset(BT[x][:], 0.0).then_inc(sem("dve_step"), 1)
                dve.wait_ge(sem("dve_step"), v.did("dve_step"))
                dve.memset(CT[x][:], 0.0).then_inc(sem("dve_step"), 1)
                dve.wait_ge(sem("dve_step"), v.did("dve_step"))
                for m in range(4):
                    for p2 in range(2):
                        rows, a = slice(64 * p2, 64 * p2 + 64), 32 * m + 16 * p2
                        dve.tensor_copy(BT[x][rows, m::4, a:a + 16], bri[x][rows, m::4, :]).then_inc(sem("dve_step"), 1)
                        dve.wait_ge(sem("dve_step"), v.did("dve_step"))
            dve.sem_inc(sem("bb_ready"), 1)
            for x in range(2):
                dve.wait_ge(*full(f"cT{x}"))
                ps = bank_of(f"cT{x}")
                pv = ps[:].rearrange("p (c n) -> p c n", c=4)
                for m in range(4):
                    for p2 in range(2):
                        rows, a = slice(64 * p2, 64 * p2 + 64), 32 * m + 16 * p2
                        ins = ts(CT[x][rows, m::4, a:a + 16], pv[rows, :, a:a + 16], [1.0, -1.0][x], None, ALU.mult)
                        if (m, p2) == (3, 1):
                            ins.then_inc(taken(f"cT{x}")[0], 1)
                            dve.wait_ge(*taken(f"cT{x}"))
                        else:
                            ins.then_inc(sem("dve_step"), 1)
                            dve.wait_ge(sem("dve_step"), v.did("dve_step"))
            for x in range(2):
                for q in range(4):
                    dve.wait_ge(*full(f"bt{x}.{q}"))
                    ps = bank_of(f"bt{x}.{q}")
                    dve.tensor_copy(BT[x][:, 4 * q:4 * q + 4, :].rearrange("p a b -> p (a b)"), ps[:]).then_inc(taken(f"bt{x}.{q}")[0], 1)
                    dve.wait_ge(*taken(f"bt{x}.{q}"))
            dve.sem_inc(sem("bt_ready"), 1)
            dve.sem_inc(sem("bt_ready"), 1)
            C, SN, ta, tb, zr_, zi_ = y8[1], y8[2], y8[3], y8[4], y8[5], y8[6]

            def conv(h):
                dve.wait_ge(sem(f"xm_in{h % 2}"), 32 * (h // 2 + 1))
                k = 2 * h
                ts(CA[:, 0], XM[h % 2][:, 0, 0:S], p_("cw", 4 * k), p_("cb", k), ALU.mult, ALU.add)
                ts(CA[:, 1], XM[h % 2][:, 1, 0:S], p_("cw", 4 * k + 4), p_("cb", k + 1), ALU.mult, ALU.add).then_inc(sem("dve_step"), 1)
                dve.wait_ge(sem("dve_step"), v.did("dve_step"))
                for t in range(1, 4):
                    for c in range(2):
                        stt(CA[:, c], XM[h % 2][:, c, t:t + S], p_("cw", 4 * (k + c) + t), CA[:, c],
                                   ALU.mult, ALU.add).then_inc(sem("dve_step"), 1)
                        dve.wait_ge(sem("dve_step"), v.did("dve_step"))
                        if t == 3:
                            dve.sem_inc(sem("cv_ready"), 1)
                dve.sem_inc(sem("conv_done"), 1)

            def gate_rows(part):
                f_, i_ = IF[32:36, :], IF[0:4, :]
                if part == 1:
                    dve.wait_ge(*taken("if"))
                    stt(gr[0][32:36, :], f_, -1.0, f_, ALU.mult, ALU.max).then_inc(sem("if_d"), 1)
                    dve.wait_ge(sem("if_d"), v.did("if_d"))
                    ts(gr[1][32:36, :], f_, 0.0, None, ALU.min).then_inc(sem("dve_step"), 1)
                    dve.wait_ge(sem("dve_step"), v.did("dve_step"))
                    dve.memset(dd[32:36, 2:3], 1.0).then_inc(sem("dve_step"), 1)
                    dve.wait_ge(sem("dve_step"), v.did("dve_step"))
                elif part == 2:
                    dve.wait_ge(sem("if_a"), v.due("if_a"))
                    tt(gr[1][32:36, :], gr[1][32:36, :], gr[0][32:36, :], ALU.subtract).then_inc(sem("dve_step"), 1)
                    dve.wait_ge(sem("dve_step"), v.did("dve_step"))
                    dve.tensor_tensor_scan(f_, dd[32:36, 2:3].to_broadcast([4, S]), gr[1][32:36, :],
                                                  0.0, ALU.mult, ALU.add).then_inc(sem("if_d"), 1)
                    dve.wait_ge(sem("if_d"), v.did("if_d"))
                else:
                    dve.wait_ge(sem("if_a"), v.due("if_a"))
                    tt(gr[1][0:4, :], i_, gr[0][0:4, :], ALU.subtract).then_inc(sem("dve_step"), 1)
                    dve.wait_ge(sem("dve_step"), v.did("dve_step"))
                    dve.tensor_tensor_scan(i_, gr[1][0:4, :], gr[1][0:4, :], 0.0, ALU.max, ALU.max).then_inc(sem("dve_step"), 1)
                    dve.wait_ge(sem("dve_step"), v.did("dve_step"))
                    stt(gr[0][0:4, :], gr[0][0:4, :], -1.0, i_, ALU.mult, ALU.subtract).then_inc(sem("if_d"), 1)
                    dve.wait_ge(sem("if_d"), v.did("if_d"))
                    ts(i_, i_, -1.0, None, ALU.mult).then_inc(sem("negM_ready"), 1)
                    dve.wait_ge(sem("negM_ready"), v.did("negM_ready"))

            def s5_out(cc):
                dve.wait_ge(*full(f"s5y{cc}"))
                ps = bank_of(f"s5y{cc}")
                stt(U[:, cc], U[:, cc], p_("s5d", cc), ps[:], ALU.mult, ALU.add).then_inc(taken(f"s5y{cc}")[0], 1)
                dve.wait_ge(*taken(f"s5y{cc}"))
                dve.sem_inc(sem("s5f_ready"), 1)

            for k in range(S5_CHUNKS):
                cc, m = divmod(k, 4)
                C4, S4, a4, b4 = (t[:].rearrange("p (s t) -> p s t", s=4) for t in (C, SN, ta, tb))
                gc, gs = (seg[:, x, k, :].unsqueeze(2).to_broadcast([P, 4, P]) for x in range(2))
                c1, s1 = (ring_step[x][:, k, :].unsqueeze(1).to_broadcast([P, 4, P]) for x in range(2))
                tt(a4, gs, s1, ALU.mult)
                tt(C4, gc, c1, ALU.mult)
                tt(b4, gs, c1, ALU.mult)
                tt(S4, gc, s1, ALU.mult).then_inc(sem("dve_step"), 1)
                dve.wait_ge(sem("dve_step"), v.did("dve_step"))
                tt(C4, C4, a4, ALU.subtract)
                tt(S4, S4, b4, ALU.add).then_inc(sem("dve_step"), 1)
                dve.wait_ge(sem("dve_step"), v.did("dve_step"))
                dve.wait_ge(*full(f"bu0.{k}"))
                dve.wait_ge(*full(f"bu1.{k}"))
                br, bi = bank_of(f"bu0.{k}"), bank_of(f"bu1.{k}")
                tt(zr_[:], br[:], C[:], ALU.mult)
                tt(ta[:], bi[:], SN[:], ALU.mult)
                tt(zi_[:], bi[:], C[:], ALU.mult).then_inc(taken(f"bu1.{k}")[0], 1)
                dve.wait_ge(*taken(f"bu1.{k}"))
                tt(tb[:], br[:], SN[:], ALU.mult).then_inc(taken(f"bu0.{k}")[0], 1)
                dve.wait_ge(*taken(f"bu0.{k}"))
                tt(zr_[:], zr_[:], ta[:], ALU.add)
                tt(zi_[:], zi_[:], tb[:], ALU.subtract).then_inc(sem("dve_step"), 1)
                dve.wait_ge(sem("dve_step"), v.did("dve_step"))
                decay_ = mag[:, k:k + 1].to_broadcast([P, S])
                dve.tensor_tensor_scan(ta[:], decay_, zr_[:], 0.0, ALU.mult, ALU.add)
                dve.tensor_tensor_scan(tb[:], decay_, zi_[:], 0.0, ALU.mult, ALU.add).then_inc(sem("dve_step"), 1)
                dve.wait_ge(sem("dve_step"), v.did("dve_step"))
                if k:
                    if k % 4 == 0:
                        dve.wait_ge(*full(f"s5y{cc - 1}"))
                    else:
                        dve.wait_ge(sem("xs_used"), v.due("xs_used"))
                tt(xx[0][:], ta[:], C[:], ALU.mult)
                tt(zr_[:], tb[:], SN[:], ALU.mult)
                tt(xx[1][:], ta[:], SN[:], ALU.mult)
                tt(zi_[:], tb[:], C[:], ALU.mult).then_inc(sem("dve_step"), 1)
                dve.wait_ge(sem("dve_step"), v.did("dve_step"))
                tt(xx[0][:], xx[0][:], zr_[:], ALU.subtract)
                tt(xx[1][:], xx[1][:], zi_[:], ALU.add).then_inc(sem("xs_ready"), 1)
                dve.wait_ge(sem("xs_ready"), v.did("xs_ready"))
                if k in (1, 4, 7):
                    gate_rows((k + 2) // 3)
                if k == 14:
                    dve.wait_ge(*full(SPILLED[-1]))
                    dve.memset(XM[0][:, :, 0:3], 0.0).then_inc(sem("dve_step"), 1)
                    dve.wait_ge(sem("dve_step"), v.did("dve_step"))
                    dve.memset(XM[1][:, :, 0:3], 0.0).then_inc(sem("xm_zero"), 1)
                    dve.wait_ge(sem("xm_zero"), v.did("xm_zero"))
                if k % 4 == 0 and k:
                    s5_out(cc - 1)
                if k % 4 == 2 and k > 4:
                    dve.wait_ge(sem("s5g_ready"), v.due("s5g_ready"))
                    split_to(YShi[:, cc - 1], YSlo[:, cc - 1], Fb[0][:], "ys_ready")
            conv(0)
            s5_out(3)
            dve.wait_ge(sem("s5g_ready"), v.due("s5g_ready"))
            split_to(YShi[:, 3], YSlo[:, 3], Fb[0][:], "ys_ready")
            if stop <= 4:
                return

            dve.memset(V[:, :, ML_DV:ML_DV + 1], 1.0).then_inc(sem("dve_step"), 1)
            dve.wait_ge(sem("dve_step"), v.did("dve_step"))

            def conv_out(h):
                for c in range(2):
                    dve.wait_ge(sem("cs2_ready"), v.due("cs2_ready"))
                    if h and c == 0:
                        dve.wait_ge(*full(f"mk{h - 1}"))
                    dve.tensor_copy(XCh[:, c], CA[:, c]).then_inc(sem("dve_step"), 1)
                    dve.wait_ge(sem("dve_step"), v.did("dve_step"))
                    tt(XCl[:, c], CA[:, c], rd(XCh[:, c]), ALU.subtract).then_inc(sem("xc_ready"), 1)
                    dve.wait_ge(sem("xc_ready"), v.did("xc_ready"))

            def diagonal(h):
                dve.wait_ge(*full(f"nb{h}"))
                ps = bank_of(f"nb{h}")
                tt(NBd[:], ps[:].rearrange("p (i c) -> p i c", i=NT),
                          c_("tri").unsqueeze(1).to_broadcast([P, NT, P]), ALU.add).then_inc(sem("nb_ready"), 1)
                dve.wait_ge(sem("nb_ready"), v.did("nb_ready"))

            def weighted(h):
                for j in range(NT):
                    n = S - j * P
                    a = TRI[j]
                    dve.wait_ge(*full(f"ms{h}.{j}"))
                    ps = bank_of(f"ms{h}.{j}")
                    dve.wait_ge(sem("e_ready"), v.due("e_ready"))
                    tt(W[:, a:a + n], ps[:, 0:n], E[h % 2][:, a:a + n], ALU.mult).then_inc(taken(f"ms{h}.{j}")[0], 1)
                    dve.wait_ge(*taken(f"ms{h}.{j}"))
                    dve.sem_inc(sem("mw_ready"), 1)

            def values_out(h):
                for i in range(NT):
                    dve.wait_ge(*full(f"mn{h}.{i}"))
                    ps = bank_of(f"mn{h}.{i}")
                    ts(dd[:, i:i + 1], ps[:, ML_DV:ML_DV + 1], -1.0, AEC[:, 1, i, h:h + 1], ALU.mult,
                              ALU.max).then_inc(sem("dve_step"), 1)
                    dve.wait_ge(sem("dve_step"), v.did("dve_step"))
                    tt(dd[:, 4 + i:5 + i], dd[:, i:i + 1], ps[:, ML_DV:ML_DV + 1], ALU.max).then_inc(sem("dve_step"), 1)
                    dve.wait_ge(sem("dve_step"), v.did("dve_step"))
                    dve.bn_stats(st4[:, i, 0, :], ps[:, 0:ML_DV])
                dve.reciprocal(dd[:, 4:8], dd[:, 4:8]).then_inc(sem("dve_step"), 1)
                dve.wait_ge(sem("dve_step"), v.did("dve_step"))
                for i in range(NT - 1):
                    dve.bn_aggr(mv[:, i, :], st4[:, i, 0, :])
                dve.bn_aggr(mv[:, NT - 1, :], st4[:, NT - 1, 0, :]).then_inc(sem("dve_step"), 1)
                dve.wait_ge(sem("dve_step"), v.did("dve_step"))
                tt(sd[:], mv[:, :, 1], dd[:, 4:8], ALU.mult).then_inc(sem("dve_step"), 1)
                dve.wait_ge(sem("dve_step"), v.did("dve_step"))
                tt(sd[:], sd[:], dd[:, 4:8], ALU.mult).then_inc(sem("dve_step"), 1)
                dve.wait_ge(sem("dve_step"), v.did("dve_step"))
                ts(sd[:], sd[:], LN_EPS, None, ALU.add).then_inc(sem("rvar_ready"), 1)
                dve.wait_ge(sem("rvar_ready"), v.did("rvar_ready"))
                dve.wait_ge(sem("sd_ready"), v.due("sd_ready"))
                dve.reciprocal(sd[:], sd[:]).then_inc(sem("dve_step"), 1)
                dve.wait_ge(sem("dve_step"), v.did("dve_step"))
                tt(sd[:], sd[:], dd[:, 4:8], ALU.mult).then_inc(sem("dve_step"), 1)
                dve.wait_ge(sem("dve_step"), v.did("dve_step"))
                stt(nmr[:], mv[:, :, 0], -1.0, sd[:], ALU.mult, ALU.mult).then_inc(sem("hf_ready"), 1)
                dve.wait_ge(sem("hf_ready"), v.did("hf_ready"))

            def head_out(h):
                dve.wait_ge(sem(f"so_in{h % 2}"), v.due(f"so_in{h % 2}", 32))
                for c in range(2):
                    k = 2 * h + c
                    dve.wait_ge(*full(f"hT{h}.{c}"))
                    ps = bank_of(f"hT{h}.{c}")
                    stt(Fb[c][:], ps[:], p_("mg", k), SO[:, h % 2, c], ALU.mult, ALU.mult).then_inc(taken(f"hT{h}.{c}")[0], 1)
                    dve.wait_ge(*taken(f"hT{h}.{c}"))
                    dve.sem_inc(sem("hf_out"), 1)
                dve.sem_inc(sem("so_used"), 1)

            def head_low(h):
                for c in range(2):
                    k = 2 * h + c
                    dve.wait_ge(sem("hf_hi"), v.due("hf_hi"))
                    tt(Blo[:, k], Fb[c][:], rd(Bhi[:, k]), ALU.subtract).then_inc(sem("B_ready"), 1)
                    dve.wait_ge(sem("B_ready"), v.did("B_ready"))

            conv_out(0)
            diagonal(0)
            conv(1)
            conv_out(1)
            for h in range(ML_H):
                weighted(h)
                if h:
                    head_low(h - 1)
                if h < ML_H - 2:
                    conv(h + 2)
                if h < ML_H - 1:
                    diagonal(h + 1)
                values_out(h)
                if h < ML_H - 2:
                    conv_out(h + 2)
                head_out(h)
            head_low(ML_H - 1)
            if stop <= 5:
                return
            dve.sem_inc(sem("heads_done"), 1)
            dve.sem_inc(sem("g8_free"), 1)
            for n in range(DC):
                dve.wait_ge(*taken(f"md{n}"))
                dve.wait_ge(sem(f"gates_in{n % 3}"), 32 * (n // 3 + 1))
                tt(Y[:, n], G8[0][:], gates[:, n % 3, 0], ALU.mult).then_inc(sem("dve_step"), 1)
                dve.wait_ge(sem("dve_step"), v.did("dve_step"))
                tt(G8[1][:], G8[1][:], G8[2][:], ALU.mult).then_inc(sem("dve_step"), 1)
                dve.wait_ge(sem("dve_step"), v.did("dve_step"))
                tt(G8[1][:], G8[1][:], gates[:, n % 3, 1], ALU.mult).then_inc(sem("dve_step"), 1)
                dve.wait_ge(sem("dve_step"), v.did("dve_step"))
                tt(Y[:, n], Y[:, n], G8[1][:], ALU.add).then_inc(sem("dve_step"), 1)
                dve.wait_ge(sem("dve_step"), v.did("dve_step"))
                dve.sem_inc(sem("g8_free"), 1)
                split_to(Ahi[:, n], Alo[:, n], Y[:, n], "A_ready")
            for n in range(DC):
                back_in(f"mix{n}", n, ALPHA)
            if stop <= 6:
                dve.sem_inc(sem("x_final"), 1)
                return

            def layer_norm(x):
                row_stats(False)
                dve.wait_ge(sem("gb_in"), v.due("gb_in", 32))
                for i in range(NT):
                    stt(X[:, i, :], X[:, i, :], mv[:, i, 0:1], GB[:, 0], ALU.subtract, ALU.mult).then_inc(sem("dve_step"), 1)
                    dve.wait_ge(sem("dve_step"), v.did("dve_step"))
                    stt(X[:, i, :], X[:, i, :], sd[:, i:i + 1], GB[:, 1], ALU.mult, ALU.add).then_inc(sem("x_final"), 1)
                    dve.wait_ge(sem("x_final"), v.did("x_final"))
                if not x:
                    dve.sem_inc(sem("gb_used"), 1)
            layer_norm(0)
            for q in range(4):
                quarter_stats(q)
            norm_rows(3)
            normed_in(3)
            dve.memset(GP[:, 0:2], 0.0).then_inc(sem("dve_step"), 1)
            dve.wait_ge(sem("dve_step"), v.did("dve_step"))
            for g, kg in enumerate(FF2_GROUPS):
                for j in range(kg):
                    k = g * 8 + j
                    dve.wait_ge(*taken(f"fg{g}.{j}"))
                    ts(FG[:], GP[:, 0:S], p_("fcw", 3 * k), p_("fcb", k), ALU.mult, ALU.add).then_inc(sem("dve_step"), 1)
                    dve.wait_ge(sem("dve_step"), v.did("dve_step"))
                    stt(FG[:], GP[:, 1:1 + S], p_("fcw", 3 * k + 1), FG[:], ALU.mult, ALU.add).then_inc(sem("dve_step"), 1)
                    dve.wait_ge(sem("dve_step"), v.did("dve_step"))
                    stt(FG[:], GP[:, 2:2 + S], p_("fcw", 3 * k + 2), FG[:], ALU.mult, ALU.add).then_inc(sem("fc_ready"), 1)
                    dve.wait_ge(sem("fc_ready"), v.did("fc_ready"))
                    dve.wait_ge(sem("fg_ready"), v.due("fg_ready"))
                    tt(FG[:], FG[:], FV[:], ALU.mult).then_inc(sem("dve_step"), 1)
                    dve.wait_ge(sem("dve_step"), v.did("dve_step"))
                    split_to(Bhi[:, j], Blo[:, j], FG[:], "B_ready")
                    dve.sem_inc(sem("fb_done"), 1)
                for n in range(DC):
                    dve.wait_ge(*taken(f"fd{g}.{n}"))
                    f = G8[(g * 8 + n) % 2]
                    if g == 0:
                        ins = dve.tensor_copy(Y[:, n], f[:])
                    else:
                        ins = tt(Y[:, n], Y[:, n], f[:], ALU.add)
                    ins.then_inc(sem("fd_used"), 1)
                    dve.wait_ge(sem("fd_used"), v.did("fd_used"))
                    if g == 2:
                        if n:
                            back_in(f"fd{n - 1}", n - 1, ALPHA)
            back_in(f"fd{DC - 1}", DC - 1, ALPHA)
            layer_norm(1)

        @block.sync
        def _(sp):
            L = Count()

            def tiles(a, b):
                for t in range(a, b):
                    if t >= RAW:
                        sp.wait_ge(sem("lo_split"), t - RAW + 1)
                    sp.dma_start(raw[t % RAW][:], d["ws"][t]).then_inc(sem(f"raw_in{t % RAW}"), 16)

            def at_chunk(name):
                return FIRST_BLOCK[INDEX[name]] // TILE_BLOCKS
            xv = d["x"].rearrange("(i p) n -> i p n", p=P)
            for i in range(NT):
                sp.dma_start(X[:, i, :], xv[i]).then_inc(sem(f"x_in{i}"), 16)
            sp.dma_start(con[:], d["con"]).then_inc(sem("con_in"), 16)
            sp.dma_start(par[:], d["par"]).then_inc(sem("par_in"), 16)
            tiles(0, 2)
            for w, nm in enumerate(("w1k", "w1v")):
                sp.dma_start(w1[w][:], d[nm].rearrange("p (a b) -> p a b", a=16)).then_inc(sem("w1_in"), 16)
            sp.wait_ge(sem("n0_done"), L.due("n0_done"))
            sp.dma_start(rope[:], d["rope"].rearrange("p (a b) -> p a b", a=2)).then_inc(sem("rope_tab"), 16)
            n_win = last_tile(INDEX[WIN[-1]]) + 2
            tiles(2, n_win)

            def store(each):
                ov = out.rearrange("(i p) n -> i p n", p=P)
                for i in range(NT):
                    if each or i == 0:
                        sp.wait_ge(sem("x_final"), L.due("x_final", 1 + NT if each and i == 0 else 1))
                    sp.dma_start(ov[i], X[:, i, :]).then_inc(sem("out_done"), 16)
                sp.wait_ge(sem("out_done"), 64)

            sp.wait_ge(*full(WIN[-1]))
            sp.dma_start(masks[:], d["masks"]).then_inc(sem("mask_in"), 16)
            sp.dma_start(decay[:], d["decay"].rearrange("p (a b) -> p a b", a=4)).then_inc(sem("mask_in"), 16)
            sp.wait_ge(sem("xfree_sp"), L.due("xfree_sp"))
            sp.dma_start(w2k[:], d["w2k"].rearrange("p (a b) -> p a b", a=2)).then_inc(sem("w1_in"), 16)
            sp.dma_start(w2v[:], d["w2v"].rearrange("p (a b) -> p a b", a=2)).then_inc(sem("w1_in"), 16)
            sp.wait_ge(sem("mix_done"), L.due("mix_done"))
            for i in range(NT):
                sp.dma_start(X[:, i, :], xv[i]).then_inc(sem("x_again"), 16)
            n_out = last_tile(INDEX["wout7"]) + 2
            tiles(n_win, n_out)
            if stop <= 2:
                store(False)
                return
            sp.dma_start(cB[:], d["c"].partition_broadcast(P)).then_inc(sem("cB_in"), 16)
            for x in range(2):
                sp.dma_start(bri[x][:], d[["bre", "bim"][x]].rearrange("p (a b) -> p a b", a=16))\
                  .then_inc(sem("s5_in"), 16)
                sp.dma_start(cri[x][:], d[["cre", "cim"][x]].rearrange("p (a b) -> p a b", a=4))\
                  .then_inc(sem("s5_in"), 16)
            for t in range(48):
                if t >= 3:
                    sp.wait_ge(sem("ada_used"), t - 2)
                sp.dma_start(adaw[t % 3][:], d["ada"][t // 2][:, t % 2 * D:(t % 2 + 1) * D])\
                  .then_inc(sem(f"ada_in{t % 3}"), 16)
                if t % 2:
                    tiles(n_out + t // 2, n_out + t // 2 + 1)
            n_ff1 = last_tile(INDEX["dn3.7"]) + 2
            tiles(n_out + 24, n_ff1)
            if stop <= 3:
                store(False)
                return
            n_s5 = last_tile(INDEX[SPILLED[-1]]) + 2
            tiles(n_ff1, n_s5)

            def whole_spill():
                for x in range(3):
                    sp.wait_ge(sem(f"spilled{x}"), 16 * len(range(x, len(SPILLED), 3)))

            sp.wait_ge(*full(SPILLED[-1]))
            sp.wait_ge(sem("xm_zero"), L.due("xm_zero"))
            whole_spill()
            def load_xm(h):
                for c in range(2):
                    sp.dma_start(XM[h % 2][:, c, 3:3 + S], spill[SPILLED.index(f"xm{2 * h + c}")])\
                      .then_inc(sem(f"xm_in{h % 2}"), 16)

            def load_so(h):
                for c in range(2):
                    sp.dma_start(SO[:, h % 2, c], spill[SPILLED.index(f"om{2 * h + c}")])\
                      .then_inc(sem(f"so_in{h % 2}"), 16)
            for h in range(2):
                load_xm(h)
                load_so(h)
            tiles(n_s5, n_s5 + 1)
            for h in range(2, ML_H):
                sp.wait_ge(sem("conv_done"), L.due("conv_done"))
                sp.wait_ge(*taken(f"v{h - 2}.1"))
                load_xm(h)
            for h in range(2, ML_H):
                sp.wait_ge(sem("so_used"), L.due("so_used"))
                load_so(h)
                tiles(n_s5 + h - 1, n_s5 + h)
            n_heads = n_s5 + 3
            if stop <= 5:
                return
            sp.wait_ge(sem("heads_done"), L.due("heads_done"))
            for x, nm in enumerate(("ln1g", "ln1b")):
                sp.dma_start(GB[:, x], d[nm].partition_broadcast(P)).then_inc(sem("gb_in"), 16)
            n_mix = last_tile(INDEX["mix7"]) + 2
            for n in range(DC):
                if n >= 3:
                    sp.wait_ge(sem("g8_free"), n - 1)
                for x, nm in enumerate(("ga", "gb")):
                    sp.dma_start(gates[:, n % 3, x], spill[SPILLED.index(f"{nm}{n}")])\
                      .then_inc(sem(f"gates_in{n % 3}"), 16)
                tiles(n_heads + n, n_heads + n + 1)
            tiles(n_heads + DC, n_mix)
            if stop <= 6:
                store(False)
                return
            sp.wait_ge(sem("gb_used"), L.due("gb_used"))
            for x, nm in enumerate(("ln2g", "ln2b")):
                sp.dma_start(GB[:, x], d[nm].partition_broadcast(P)).then_inc(sem("gb_in"), 16)
            tiles(n_mix, NTILES)
            store(True)


def stream_weights(w):
    sizes = [512] + [128] * 6 + [24, 256, 256, 512, 512]
    off = np.concatenate([[0], np.cumsum(sizes)])
    part = {n: w["w_in"][:, off[i]:off[i + 1]] for i, n in enumerate(
        ["q", "kc", "vc", "ks", "vs", "kw", "vw", "gate", "rq", "rk", "rv", "rg"])}
    w2 = w["w_in_2"]
    part2 = {"xm": w2[:, 0:1024], "om": w2[:, 1024:2048], "us": w2[:, 2056:2568], "ga": w2[:, 2568:3592],
             "gb": w2[:, 3592:4616]}

    def cols(a, n):
        return a[:, n * P:(n + 1) * P]

    def of(name):
        head, _, rest_ = name.partition(".")
        if name in ("kc", "vc", "ks", "kw", "vs", "vw"):
            return part[name]
        if name[0] == "q":
            r = int(name[1])
            q = part["q"].reshape(D, GROUPS, REP, DH)[:, :, r]
            return q.reshape(D, P)
        if name == "gate":
            return np.concatenate([part["gate"], np.zeros((D, P - 24), np.float32)], 1)
        if name[:2] in ("rq", "rk", "rv", "rg"):
            return cols(part[name[:2]], int(name[2]))
        if name[:4] == "wout":
            return cols(w["w_out"], int(name[4]))
        if name[:2] == "up":
            return cols(w["w_up"], 8 * int(head[2:]) + int(rest_))
        if name[:2] == "dn":
            g = int(head[2:])
            return cols(w["w_down"][g * 1024:(g + 1) * 1024], int(rest_))
        if name == "if":
            z = np.zeros((D, P), np.float32)
            z[:, 0:4], z[:, 32:36] = w2[:, 2048:2052], w2[:, 2052:2056]
            return z
        if name[:2] in part2:
            return cols(part2[name[:2]], int(name[2:]))
        if name[:2] == "mq":
            return w["w_mlstm_q_2"][int(name[2])]
        if name[:2] == "mk":
            return w["w_mlstm_k_2"][int(name[2])]
        if name[:2] == "md":
            return cols(w["w_mlstm_down_2"], int(name[2]))
        if name[:2] == "gv":
            return cols(w["w_s5_glu_2"], int(name[2]))
        if name[:2] == "gg":
            return cols(w["w_s5_glu_2"], 8 + int(name[2]))
        if name[:3] == "mix":
            return cols(w["w_mix_out_2"], int(name[3]))
        if name[:2] == "fv":
            return cols(w["w_ffn_up_2"], 8 * int(head[2:]) + int(rest_))
        if name[:2] == "fg":
            return cols(w["w_ffn_up_2"], 22 + 8 * int(head[2:]) + int(rest_))
        g = int(head[2:])
        return cols(w["w_ffn_down_2"][g * 1024:(g + 1) * 1024], int(rest_))

    blocks = []
    for name, kn in CHUNKS:
        a = of(name)
        assert a.shape == (kn * P, P), (name, a.shape)
        blocks.append(a.reshape(kn, P, P))
    b = np.concatenate(blocks, 0).reshape(NTILES, TILE_BLOCKS, P, P)
    return np.ascontiguousarray(b.transpose(0, 2, 1, 3).reshape(NTILES, P, TILE_COLS))


def lay_out(inputs):
    w = {k: np.asarray(a) for k, a in inputs.items()}
    flat = ("x",)
    w = {k: (a[0] if a.ndim > 1 else a) for k, a in w.items()}
    bin2 = w["b_in_2"]

    def col(a):
        return a.reshape(-1, P).T

    def states(a):
        return a.reshape(S5_CHUNKS, P).T
    bif = np.zeros(P, np.float32)
    bif[0:4], bif[32:36] = bin2[2048:2052], bin2[2052:2056]
    cols = {
        "ln1": col(w["ln1_w"]), "qn": np.concatenate([w["q_norm_w"]] * 2)[:, None],
        "kn": np.concatenate([w["k_norm_w"]] * 2, 1).T, "retn": w["ret_norm_w"].T, "ln2": col(w["ln2_w"]),
        "pek": w["cmp_pe_k"].reshape(16, P).T, "pev": w["cmp_pe_v"].reshape(16, P).T,
        "b_us": col(bin2[2056:2568]), "b_if": bif[:, None], "b_xm": col(bin2[0:1024]),
        "b_om": col(bin2[1024:2048]), "b_ga": col(bin2[2568:3592]), "b_gb": col(bin2[3592:4616]),
        "cw": w["w_mlstm_conv_2"].reshape(4, 8, P).transpose(2, 1, 0).reshape(P, 32),
        "cb": col(w["b_mlstm_conv_2"]), "mg": col(w["mlstm_norm_gain_2"]),
        "lre": states(w["s5_lam_re_2"]), "lim": states(w["s5_lam_im_2"]),
        "ldt": states(np.repeat(w["s5_log_dt_2"], 64)), "s5d": col(w["s5_d_2"]),
        "fcw": w["w_ffn_conv_2"].reshape(3, 22, P).transpose(2, 1, 0).reshape(P, 66),
        "fcb": col(w["b_ffn_conv_2"]), "bada": col(w["b_ada_2"]),
    }
    par = np.concatenate([cols[n] for n in PAR], 1)
    assert par.shape == (P, NPAR)

    def tall(a, k):
        return a.reshape(k, P, -1).transpose(1, 0, 2).reshape(P, -1)

    def c_dup(a):
        a = tall(a.reshape(512, 64), 4).reshape(P, 4, 64)
        return np.concatenate([a, a], 2).reshape(P, 512)
    out = {
        "x": w["x"], "ws": stream_weights(w), "par": par,
        "ada": np.ascontiguousarray(w["w_ada_2"].T).reshape(24, 2, P, D).transpose(0, 2, 1, 3).reshape(24, P, 2 * D),
        "c": w["c_2"], "w1k": tall(w["cmp_wk1"], 16), "w1v": tall(w["cmp_wv1"], 16),
        "w2k": np.concatenate([w["cmp_wk2"].reshape(2, P, DH)] * 2, 2).transpose(1, 0, 2).reshape(P, 2 * P),
        "w2v": tall(w["cmp_wv2"], 2),
        "bre": w["s5_b_re_2"].reshape(16, P, 16).transpose(1, 0, 2).reshape(P, 256),
        "bim": w["s5_b_im_2"].reshape(16, P, 16).transpose(1, 0, 2).reshape(P, 256),
        "cre": c_dup(w["s5_c_re_2"]), "cim": c_dup(w["s5_c_im_2"]),
        "ln1g": w["ln1_gain_2"], "ln1b": w["ln1_bias_2"], "ln2g": w["ln2_gain_2"], "ln2b": w["ln2_bias_2"],
    }
    out.update({k: a.astype(np.float32) for k, a in constants().items()})
    return {k: np.ascontiguousarray(a) for k, a in out.items()}


def kernel(**inputs):
    import concourse.bacc as bacc
    from concourse.bass_utils import run_bass_kernel_spmd

    arrays = lay_out(inputs)
    nc = bacc.Bacc("TRN2", target_bir_lowering=False, num_devices=1)
    d = {k: nc.dram_tensor(f"in_{k}", a.shape, F32, kind="ExternalInput").ap() for k, a in arrays.items()}
    out = nc.dram_tensor("out_x", (S, D), F32, kind="ExternalOutput").ap()
    build(nc, d, out)
    r = run_bass_kernel_spmd(nc, [{f"in_{k}": a for k, a in arrays.items()}], core_ids=[0])
    return r.results[0]["out_x"].reshape(1, S, D)
```
